# Optimizing a Trainium2 kernel written in Bass

```python
import math
import numpy as np
import jax
import jax.numpy as jnp
from jax import lax

D_MODEL = 1024
BATCH = 1
SEQ = 128
DEPTH = 2
DEC_BATCH = 1
DEC_SEQ = 512
PAST_LEN = 128

GRID_W = 64
N_BRANCH = 4
BR_W = 256
MLA_H = 4
MLA_NOPE = 64
MLA_ROPE = 32
MLA_V = 64
MLA_Q_LORA = 256
MLA_KV_LORA = 128
GDN_H = 4
GDN_DK = 64
GDN_DV = 64
GDN_CHUNK = 64
SHORT_K = 3
HY_W = 256
HY_BANDS = 16
HY_EMB = 1 + 2 * HY_BANDS
HY_FH = 64
HY_SLOW_DECAY = math.log(1e-2) / 1.5
HY_FAST_DECAY = math.log(1e-2) / 0.3
DA_H = 4
DA_DK = 32
DA_DV = 64
D_FF = 4 * D_MODEL
ROPE_BASE = 10000.0
Q_BLOCK = 128
EPS = 1e-6
IN_SPLITS = (MLA_Q_LORA, MLA_KV_LORA, MLA_ROPE,
             GDN_H * GDN_DK, GDN_H * GDN_DK, GDN_H * GDN_DV, GDN_H * GDN_DV, 2 * GDN_H, 2 * GDN_H,
             3 * HY_W,
             DA_H * 2 * DA_DK, DA_H * 2 * DA_DK, DA_H * DA_DV,
             N_BRANCH * D_MODEL)
IN_W = (MLA_Q_LORA + MLA_KV_LORA + MLA_ROPE + 2 * GDN_H * GDN_DK + 2 * GDN_H * GDN_DV + 4 * GDN_H
        + 3 * HY_W + 4 * DA_H * DA_DK + DA_H * DA_DV + N_BRANCH * D_MODEL)

kernel_name = 'hybrid_diffusion_prefix_trunk'

def _rmsnorm(x, w):
    xf = x.astype(jnp.float32)
    y = xf * lax.rsqrt(jnp.mean(xf * xf, axis=-1, keepdims=True) + EPS)
    return (y * w.astype(jnp.float32)).astype(x.dtype)

def _l2norm(x):
    xf = x.astype(jnp.float32)
    return xf * lax.rsqrt(jnp.sum(xf * xf, axis=-1, keepdims=True) + EPS)

def _dwconv_centred(x, w):
    seq = x.shape[1]
    pad = w.shape[0] // 2
    xp = jnp.pad(x, ((0, 0), (pad, pad), (0, 0)))
    out = xp[:, :seq] * w[0]
    for i in range(1, w.shape[0]):
        out = out + xp[:, i:i + seq] * w[i]
    return out

def _axial_rope_angles(seq, rot_dim):
    rows = seq // GRID_W
    m = rot_dim // 4
    inv = ROPE_BASE ** (-jnp.arange(m, dtype=jnp.float32) / m)
    row_pos = jnp.repeat(jnp.arange(rows, dtype=jnp.float32), GRID_W)
    col_pos = jnp.tile(jnp.arange(GRID_W, dtype=jnp.float32), rows)
    return row_pos[:, None] * inv, col_pos[:, None] * inv

def _rope_half(x, ang):
    shape = (ang.shape[0],) + (1,) * (x.ndim - 3) + (ang.shape[1],)
    cos = jnp.cos(ang).reshape(shape)
    sin = jnp.sin(ang).reshape(shape)
    x1, x2 = jnp.split(x.astype(jnp.float32), 2, axis=-1)
    return jnp.concatenate([x1 * cos - x2 * sin, x2 * cos + x1 * sin], axis=-1)

def _apply_axial_rope(x, ang_row, ang_col):
    xr, xc = jnp.split(x, 2, axis=-1)
    return jnp.concatenate([_rope_half(xr, ang_row), _rope_half(xc, ang_col)], axis=-1).astype(x.dtype)

def _map_query_blocks(fn, q):
    bsz, lq = q.shape[:2]
    nb = lq // Q_BLOCK
    qb = jnp.moveaxis(q.reshape((bsz, nb, Q_BLOCK) + q.shape[2:]), 1, 0)
    out = lax.map(fn, qb)
    return jnp.moveaxis(out, 0, 1).reshape((bsz, lq) + out.shape[3:])

def _mla_expand(ckv, kpe, w_ukv):
    bsz, seq = ckv.shape[:2]
    kv = (ckv @ w_ukv).reshape(bsz, seq, MLA_H, MLA_NOPE + MLA_V)
    k = jnp.concatenate([kv[..., :MLA_NOPE], jnp.broadcast_to(kpe[:, :, None, :], (bsz, seq, MLA_H, MLA_ROPE))], axis=-1)
    return k, kv[..., MLA_NOPE:]

def _mla_attend(q, k, v):
    scale = (MLA_NOPE + MLA_ROPE) ** -0.5

    def block(qb):
        s = jnp.einsum('bqhd,bkhd->bhqk', qb, k).astype(jnp.float32) * scale
        p = jax.nn.softmax(s, axis=-1).astype(v.dtype)
        return jnp.einsum('bhqk,bkhd->bqhd', p, v)

    return _map_query_blocks(block, q)

def _diff_attend(q, k, v, lam):
    scale = DA_DK ** -0.5
    k1, k2 = k[..., 0, :], k[..., 1, :]

    def block(qb):
        s1 = jnp.einsum('bqhd,bkhd->bhqk', qb[..., 0, :], k1).astype(jnp.float32) * scale
        s2 = jnp.einsum('bqhd,bkhd->bhqk', qb[..., 1, :], k2).astype(jnp.float32) * scale
        p = jax.nn.softmax(s1, axis=-1) - lam * jax.nn.softmax(s2, axis=-1)
        return jnp.einsum('bhqk,bkhd->bqhd', p.astype(v.dtype), v)

    return _map_query_blocks(block, q)

def _gdn_chunked(q, k, v, g, beta, s0):
    f32 = jnp.float32
    bsz, seq, nh, dk = q.shape
    dv = v.shape[-1]
    n = seq // GDN_CHUNK

    def chunks(t):
        return t.astype(f32).reshape(bsz, n, GDN_CHUNK, nh, -1).transpose(1, 0, 3, 2, 4)

    qc = chunks(q) * (dk ** -0.5)
    kc = chunks(k)
    vc = chunks(v)
    gc = jnp.cumsum(chunks(g[..., None])[..., 0], axis=-1)
    bc = chunks(beta[..., None])
    incl = jnp.tril(jnp.ones((GDN_CHUNK, GDN_CHUNK), dtype=bool))
    strict = jnp.tril(jnp.ones((GDN_CHUNK, GDN_CHUNK), dtype=bool), k=-1)
    gdiff = gc[..., :, None] - gc[..., None, :]
    decay = jnp.where(incl, jnp.exp(jnp.where(incl, gdiff, 0.0)), 0.0)
    kb = kc * bc
    lower = jnp.where(strict, jnp.einsum('nbhid,nbhjd->nbhij', kb, kc) * decay, 0.0)
    a_mat = lower + jnp.eye(GDN_CHUNK, dtype=f32)
    rhs = jnp.concatenate([vc * bc, kb * jnp.exp(gc)[..., None]], axis=-1)
    sol = lax.linalg.triangular_solve(a_mat, rhs, left_side=True, lower=True, unit_diagonal=True)
    u, w = sol[..., :dv], sol[..., dv:]
    intra = jnp.where(incl, jnp.einsum('nbhid,nbhjd->nbhij', qc, kc) * decay, 0.0)

    def step(state, xs):
        q_i, k_i, u_i, w_i, g_i, a_i = xs
        v_new = u_i - jnp.einsum('bhck,bhkv->bhcv', w_i, state)
        o_i = (jnp.einsum('bhck,bhkv->bhcv', q_i * jnp.exp(g_i)[..., None], state)
               + jnp.einsum('bhij,bhjv->bhiv', a_i, v_new))
        g_last = g_i[..., -1:]
        state = (state * jnp.exp(g_last)[..., None]
                 + jnp.einsum('bhck,bhcv->bhkv', k_i * jnp.exp(g_last - g_i)[..., None], v_new))
        return state, o_i

    s_final, o = lax.scan(step, s0.astype(f32), (qc, kc, u, w, gc, intra))
    return o.transpose(1, 0, 3, 2, 4).reshape(bsz, seq, nh, dv), s_final

def _reverse_seq(t):
    return jnp.flip(t, axis=1)

def _gdn_bidirectional(q, k, v, g, beta, s0):
    o_f, s_f = _gdn_chunked(q, k, v, g[:, :, 0], beta[:, :, 0], s0[:, 0])
    o_b, s_b = _gdn_chunked(_reverse_seq(q), _reverse_seq(k), _reverse_seq(v),
                            _reverse_seq(g[:, :, 1]), _reverse_seq(beta[:, :, 1]), s0[:, 1])
    return o_f + _reverse_seq(o_b), jnp.stack([s_f, s_b], axis=1)

def _gdn_branch(zq, zk, zv, zz, za, zb, conv_w, a_log, dt_bias, norm_w, s0):
    f32 = jnp.float32
    bsz, seq = zq.shape[:2]
    qkv = jax.nn.silu(_dwconv_centred(jnp.concatenate([zq, zk, zv], axis=-1), conv_w))
    q, k, v = jnp.split(qkv, [GDN_H * GDN_DK, 2 * GDN_H * GDN_DK], axis=-1)
    q = _l2norm(q.reshape(bsz, seq, GDN_H, GDN_DK))
    k = _l2norm(k.reshape(bsz, seq, GDN_H, GDN_DK))
    v = v.reshape(bsz, seq, GDN_H, GDN_DV)
    g = -jnp.exp(a_log.astype(f32)) * jax.nn.softplus(za.reshape(bsz, seq, 2, GDN_H).astype(f32) + dt_bias.astype(f32))
    beta = jax.nn.sigmoid(zb.reshape(bsz, seq, 2, GDN_H).astype(f32))
    o, s = _gdn_bidirectional(q, k, v, g, beta, s0)
    o = _rmsnorm(o, norm_w) * jax.nn.silu(zz.reshape(bsz, seq, GDN_H, GDN_DV).astype(f32))
    return o.reshape(bsz, seq, GDN_H * GDN_DV).astype(zq.dtype), s.astype(zq.dtype)

def _hyena_filters(seq, w1, b1, w2, b2, w3, freq):
    f32 = jnp.float32
    pos = jnp.arange(seq, dtype=f32)
    t = pos / max(seq - 1, 1)
    ang = (2.0 * math.pi * pos / seq)[:, None] * jnp.linspace(1e-4, HY_BANDS - 1, HY_BANDS, dtype=f32)
    z = jnp.concatenate([t[:, None], jnp.cos(ang), -jnp.sin(ang)], axis=-1)
    fr = freq.astype(f32)
    h = jnp.sin(fr * (z @ w1.astype(f32) + b1.astype(f32)))
    h = jnp.sin(fr * (h @ w2.astype(f32) + b2.astype(f32)))
    h = h @ w3.astype(f32)
    deltas = jnp.abs(jnp.linspace(HY_SLOW_DECAY, HY_FAST_DECAY, HY_W, dtype=f32))
    return h * jnp.exp(-t[:, None] * jnp.tile(deltas, 2))

def _hyena_branch(u, conv_w, conv_b, filt, d_bias):
    f32 = jnp.float32
    seq = u.shape[1]
    uc = _dwconv_centred(u, conv_w) + conv_b
    x0, x1, v = jnp.split(uc.astype(f32), 3, axis=-1)
    v = v * x1
    h_fwd, h_bwd = filt[:, :HY_W], filt[:, HY_W:]
    h_circ = jnp.concatenate([h_fwd, jnp.zeros((1, HY_W), f32), jnp.flip(h_bwd[1:], axis=0)], axis=0)
    n_fft = 2 * seq
    y = jnp.fft.irfft(jnp.fft.rfft(v, n=n_fft, axis=1) * jnp.fft.rfft(h_circ, n=n_fft, axis=0), n=n_fft, axis=1)[:, :seq]
    return ((y + v * d_bias.astype(f32)) * x0).astype(u.dtype)

def _gated_merge(branches, z_gate, w_branch, w_out):
    bsz, seq = z_gate.shape[:2]
    stacked = jnp.stack(branches, axis=2)
    proj = jnp.einsum('blnc,ncd->blnd', stacked, w_branch)
    gates = jax.nn.sigmoid(z_gate.reshape(bsz, seq, N_BRANCH, D_MODEL))
    return jnp.einsum('bld,de->ble', jnp.sum(gates * proj, axis=2), w_out)

def _mixer_sublayer(h, p, l, ctx):
    bsz, seq = h.shape[:2]
    split_at = [int(s) for s in np.cumsum(IN_SPLITS)[:-1]]
    (m_cq, m_ckv, m_kpe, g_q, g_k, g_v, g_z, g_a, g_b, hy_u, d_q, d_k, d_v, z_gate) = jnp.split(
        h @ p['w_in'][l], split_at, axis=-1)
    w_ukv = p['mla_w_ukv'][l]
    q = (_rmsnorm(m_cq, p['mla_q_norm_w'][l]) @ p['mla_w_uq'][l]).reshape(bsz, seq, MLA_H, MLA_NOPE + MLA_ROPE)
    ckv = _rmsnorm(m_ckv, p['mla_kv_norm_w'][l])
    kpe = m_kpe
    dq = d_q.reshape(bsz, seq, DA_H, 2, DA_DK)
    dk = d_k.reshape(bsz, seq, DA_H, 2, DA_DK)
    dv = d_v.reshape(bsz, seq, DA_H, DA_DV)
    if ctx is None:
        s0 = jnp.zeros((bsz, 2, GDN_H, GDN_DK, GDN_DV), h.dtype)
        q_a = q
        k_a, v_a = _mla_expand(ckv, kpe, w_ukv)
        q_d, k_d, v_d = dq, dk, dv
    else:
        ckv_c, kpe_c, dk_c, dv_c, s0 = ctx
        ang_r, ang_c = _axial_rope_angles(seq, MLA_ROPE)
        q_a = jnp.concatenate([q[..., :MLA_NOPE], _apply_axial_rope(q[..., MLA_NOPE:], ang_r, ang_c)], axis=-1)
        k_lat, v_lat = _mla_expand(ckv, _apply_axial_rope(kpe, ang_r, ang_c), w_ukv)
        k_ctx, v_ctx = _mla_expand(ckv_c, kpe_c, w_ukv)
        k_a = jnp.concatenate([k_lat, k_ctx], axis=1)
        v_a = jnp.concatenate([v_lat, v_ctx], axis=1)
        dang_r, dang_c = _axial_rope_angles(seq, DA_DK)
        q_d = _apply_axial_rope(dq, dang_r, dang_c)
        k_d = jnp.concatenate([_apply_axial_rope(dk, dang_r, dang_c), dk_c], axis=1)
        v_d = jnp.concatenate([dv, dv_c], axis=1)
    o_a = _mla_attend(q_a, k_a, v_a).reshape(bsz, seq, MLA_H * MLA_V)
    o_b, s_gdn = _gdn_branch(g_q, g_k, g_v, g_z, g_a, g_b, p['gdn_conv_w'][l], p['gdn_a_log'][l],
                             p['gdn_dt_bias'][l], p['gdn_norm_w'][l], s0)
    filt = _hyena_filters(seq, p['hy_f_w1'][l], p['hy_f_b1'][l], p['hy_f_w2'][l], p['hy_f_b2'][l],
                          p['hy_f_w3'][l], p['hy_f_freq'][l])
    o_c = _hyena_branch(hy_u, p['hy_conv_w'][l], p['hy_conv_b'][l], filt, p['hy_d'][l])
    lam_init = 0.8 - 0.6 * math.exp(-0.3 * l)
    f32 = jnp.float32
    lam = (jnp.exp(jnp.sum(p['da_lq1'][l].astype(f32) * p['da_lk1'][l].astype(f32)))
           - jnp.exp(jnp.sum(p['da_lq2'][l].astype(f32) * p['da_lk2'][l].astype(f32))) + lam_init)
    o_d = _diff_attend(q_d, k_d, v_d, lam)
    o_d = (_rmsnorm(o_d, p['da_norm_w'][l]) * (1.0 - lam_init)).reshape(bsz, seq, DA_H * DA_DV)
    merged = _gated_merge([o_a, o_b, o_c, o_d], z_gate, p['w_branch'][l], p['w_out'][l])
    new_ctx = (ckv, kpe, dk, dv, s_gdn) if ctx is None else None
    return merged, new_ctx

def _trunk_layer(x, p, l, cond, ctx):
    mod = (cond @ p['w_ada'][l] + p['b_ada'][l]).reshape(cond.shape[0], 1, 6, D_MODEL)
    sh_a, sc_a, gt_a, sh_m, sc_m, gt_m = [mod[:, :, i] for i in range(6)]
    h = _rmsnorm(x, p['norm_mix_w'][l]) * (1.0 + sc_a) + sh_a
    mix, new_ctx = _mixer_sublayer(h, p, l, ctx)
    x = x + gt_a * mix
    h = _rmsnorm(x, p['norm_mlp_w'][l]) * (1.0 + sc_m) + sh_m
    x = x + gt_m * (jnp.square(jax.nn.relu(h @ p['mlp_w1'][l])) @ p['mlp_w2'][l])
    return x, new_ctx

def setup_inputs(seed: int = 0) -> dict:
    key = jax.random.key(seed)
    ks = iter(jax.random.split(key, 48))
    f32 = jnp.float32

    def nrm(shape, scale):
        return jax.random.normal(next(ks), shape, f32) * scale

    def gain(shape):
        return 1.0 + nrm(shape, 0.02)

    a_vals = jax.random.uniform(next(ks), (DEPTH, 2, GDN_H), f32, 1.0, 16.0)
    dt = jnp.exp(jax.random.uniform(next(ks), (DEPTH, 2, GDN_H), f32, math.log(1e-3), math.log(1e-1)))
    gdn_dt_bias = dt + jnp.log(-jnp.expm1(-dt))
    return {
        'x_prompt': nrm((BATCH, SEQ, D_MODEL), 1.0),
        'x_sample': nrm((DEC_BATCH, DEC_SEQ, D_MODEL), 1.0),
        'cache_mla_ckv': nrm((DEC_BATCH, DEPTH, PAST_LEN, MLA_KV_LORA), 1.0),
        'cache_mla_kpe': nrm((DEC_BATCH, DEPTH, PAST_LEN, MLA_ROPE), 1.0),
        'cache_diff_k': nrm((DEC_BATCH, DEPTH, PAST_LEN, DA_H, 2, DA_DK), 1.0),
        'cache_diff_v': nrm((DEC_BATCH, DEPTH, PAST_LEN, DA_H, DA_DV), 1.0),
        'state_gdn': nrm((DEC_BATCH, DEPTH, 2, GDN_H, GDN_DK, GDN_DV), 0.1),
        'c': nrm((DEC_BATCH, D_MODEL), 1.0),
        'c_ctx': nrm((D_MODEL,), 1.0),
        'w_ada': nrm((DEPTH, D_MODEL, 6 * D_MODEL), D_MODEL ** -0.5),
        'b_ada': nrm((DEPTH, 6 * D_MODEL), 0.01),
        'norm_mix_w': gain((DEPTH, D_MODEL)),
        'norm_mlp_w': gain((DEPTH, D_MODEL)),
        'w_in': nrm((DEPTH, D_MODEL, IN_W), D_MODEL ** -0.5),
        'mla_q_norm_w': gain((DEPTH, MLA_Q_LORA)),
        'mla_w_uq': nrm((DEPTH, MLA_Q_LORA, MLA_H * (MLA_NOPE + MLA_ROPE)), MLA_Q_LORA ** -0.5),
        'mla_kv_norm_w': gain((DEPTH, MLA_KV_LORA)),
        'mla_w_ukv': nrm((DEPTH, MLA_KV_LORA, MLA_H * (MLA_NOPE + MLA_V)), MLA_KV_LORA ** -0.5),
        'gdn_conv_w': nrm((DEPTH, SHORT_K, 2 * GDN_H * GDN_DK + GDN_H * GDN_DV), SHORT_K ** -0.5),
        'gdn_a_log': jnp.log(a_vals),
        'gdn_dt_bias': gdn_dt_bias,
        'gdn_norm_w': gain((DEPTH, GDN_DV)),
        'hy_conv_w': nrm((DEPTH, SHORT_K, 3 * HY_W), SHORT_K ** -0.5),
        'hy_conv_b': nrm((DEPTH, 3 * HY_W), 0.01),
        'hy_f_w1': nrm((DEPTH, HY_EMB, HY_FH), HY_EMB ** -0.5),
        'hy_f_b1': nrm((DEPTH, HY_FH), 0.01),
        'hy_f_w2': nrm((DEPTH, HY_FH, HY_FH), HY_FH ** -0.5),
        'hy_f_b2': nrm((DEPTH, HY_FH), 0.01),
        'hy_f_w3': nrm((DEPTH, HY_FH, 2 * HY_W), 0.1 * HY_FH ** -0.5),
        'hy_f_freq': gain((DEPTH, HY_FH)),
        'hy_d': nrm((DEPTH, HY_W), 0.5),
        'da_lq1': nrm((DEPTH, DA_DK), 0.1),
        'da_lk1': nrm((DEPTH, DA_DK), 0.1),
        'da_lq2': nrm((DEPTH, DA_DK), 0.1),
        'da_lk2': nrm((DEPTH, DA_DK), 0.1),
        'da_norm_w': gain((DEPTH, DA_DV)),
        'w_branch': nrm((DEPTH, N_BRANCH, BR_W, D_MODEL), BR_W ** -0.5),
        'w_out': nrm((DEPTH, D_MODEL, D_MODEL), D_MODEL ** -0.5),
        'mlp_w1': nrm((DEPTH, D_MODEL, D_FF), D_MODEL ** -0.5),
        'mlp_w2': nrm((DEPTH, D_FF, D_MODEL), D_FF ** -0.5),
        'final_norm_w': gain((D_MODEL,)),
    }

def reference(x_prompt, x_sample, cache_mla_ckv, cache_mla_kpe, cache_diff_k, cache_diff_v, state_gdn,
              c, c_ctx, w_ada, b_ada, norm_mix_w, norm_mlp_w, w_in, mla_q_norm_w, mla_w_uq, mla_kv_norm_w,
              mla_w_ukv, gdn_conv_w, gdn_a_log, gdn_dt_bias, gdn_norm_w, hy_conv_w, hy_conv_b, hy_f_w1, hy_f_b1,
              hy_f_w2, hy_f_b2, hy_f_w3, hy_f_freq, hy_d, da_lq1, da_lk1, da_lq2, da_lk2, da_norm_w, w_branch,
              w_out, mlp_w1, mlp_w2, final_norm_w):
    p = {
        'w_ada': w_ada, 'b_ada': b_ada, 'norm_mix_w': norm_mix_w, 'norm_mlp_w': norm_mlp_w, 'w_in': w_in,
        'mla_q_norm_w': mla_q_norm_w, 'mla_w_uq': mla_w_uq, 'mla_kv_norm_w': mla_kv_norm_w, 'mla_w_ukv': mla_w_ukv,
        'gdn_conv_w': gdn_conv_w, 'gdn_a_log': gdn_a_log, 'gdn_dt_bias': gdn_dt_bias, 'gdn_norm_w': gdn_norm_w,
        'hy_conv_w': hy_conv_w, 'hy_conv_b': hy_conv_b, 'hy_f_w1': hy_f_w1, 'hy_f_b1': hy_f_b1,
        'hy_f_w2': hy_f_w2, 'hy_f_b2': hy_f_b2, 'hy_f_w3': hy_f_w3, 'hy_f_freq': hy_f_freq, 'hy_d': hy_d,
        'da_lq1': da_lq1, 'da_lk1': da_lk1, 'da_lq2': da_lq2, 'da_lk2': da_lk2, 'da_norm_w': da_norm_w,
        'w_branch': w_branch, 'w_out': w_out, 'mlp_w1': mlp_w1, 'mlp_w2': mlp_w2,
    }
    cond_ctx = jax.nn.silu(c_ctx)[None, :]
    x = x_prompt
    ctx_tensors = []
    for l in range(DEPTH):
        x, new_ctx = _trunk_layer(x, p, l, cond_ctx, None)
        ctx_tensors.append(new_ctx)
    y_prompt = _rmsnorm(x, final_norm_w)
    new_mla_ckv = jnp.stack([t[0] for t in ctx_tensors], axis=1)
    new_mla_kpe = jnp.stack([t[1] for t in ctx_tensors], axis=1)
    new_diff_k = jnp.stack([t[2] for t in ctx_tensors], axis=1)
    new_diff_v = jnp.stack([t[3] for t in ctx_tensors], axis=1)
    new_gdn_state = jnp.stack([t[4] for t in ctx_tensors], axis=1)
    cond = jax.nn.silu(c)
    x = x_sample
    for l in range(DEPTH):
        ctx_l = (cache_mla_ckv[:, l], cache_mla_kpe[:, l], cache_diff_k[:, l], cache_diff_v[:, l], state_gdn[:, l])
        x, _ = _trunk_layer(x, p, l, cond, ctx_l)
    y_sample = _rmsnorm(x, final_norm_w)
    return (y_prompt, y_sample, new_mla_ckv, new_mla_kpe, new_diff_k, new_diff_v, new_gdn_state)


_drawn_inputs = setup_inputs


def setup_inputs(seed=0):
    import zlib

    import numpy as np

    out = dict(_drawn_inputs(seed))
    spreads = {}
    factors = {'cache_mla_ckv': 4.337,
     'cache_mla_kpe': 8.0,
     'norm_mlp_w': 2.78,
     'mla_q_norm_w': 8.0,
     'mla_kv_norm_w': 2.861,
     'gdn_norm_w': 8.0,
     'hy_conv_b': 6.654,
     'hy_f_b1': 7.701,
     'hy_f_b2': 5.401,
     'hy_f_freq': 7.613,
     'da_lq1': 7.47,
     'da_lk1': 7.11,
     'da_lq2': 8.0,
     'da_lk2': 7.526,
     'da_norm_w': 8.0}
    for name, (base, spread) in spreads.items():
        noise = np.random.default_rng([zlib.crc32(name.encode()), seed]).standard_normal(out[name].shape)
        drawn = base * np.exp(spread * noise) if base else spread * noise
        out[name] = jnp.asarray(drawn.astype(out[name].dtype))
    for name, factor in factors.items():
        out[name] = (out[name] * factor).astype(out[name].dtype)
    return out
```

```python
import math
from contextlib import ExitStack

import numpy as np
import concourse.bass as bass
from concourse import mybir

F32 = mybir.dt.float32
F32R = mybir.dt.float32r
ALU = mybir.AluOpType
ACT = mybir.ActivationFunctionType
AX = mybir.AxisListType

P = 128
D = 1024
KC = D // P
DEPTH = 2
LAT, CTX = 512, 128
T = LAT + CTX
NT = T // P
SEGS = ((0, LAT), (LAT, T))
HALF = T // 2
KEYS = LAT + 128 + CTX
H = 4
GRID_W = 64
EPS = 1e-6
BANDS = 16
RING = 4

N_EARLY, N_LATE = 16, 32
N_WIN, N_GATE, N_OUT = 24, 32, 8
GROUPS = 4
N_GROUP = 2 * KC + N_EARLY // GROUPS
WIN_1 = 14
B_LATE = WIN_1
B_GATE = N_WIN + N_LATE
B_OUT = B_GATE + N_GATE
B_MLP = B_OUT + N_OUT
N_BLOCKS = B_MLP + GROUPS * N_GROUP
N_SPLIT = N_GATE + N_OUT + GROUPS * 2 * KC
PER_SLOT = N_BLOCKS // RING


def win_at(n):
    return n if n < WIN_1 else n + N_LATE


CV = LAT + CTX + 2
PAD = CV + 2


def tok_cols(t):
    return t * P if t < NT - 1 else LAT + 2


def layout(fields):
    at, out = 0, {}
    for name, width in fields:
        out[name] = (at, width)
        at += width
    return out, at


PAR, PAR_W = layout([
    ("wab", KC * 16), ("uq", 2 * 384), ("ukv", 512), ("w1", 64), ("w2", 64), ("w3", 512),
    ("ckv_c", 128), ("kpe_c", 128), ("dk_c", 256), ("dv_c", 256), ("s0", 256),
    ("lam", 128), ("danw", 64), ("alog", 8), ("dtb", 8), ("bada", 48), ("nmix", 8), ("nmlp", 8),
    ("qn", 2), ("kvn", 1), ("gcw", 18), ("gnw", 1), ("hcw", 18), ("hcb", 6), ("hb1", 1), ("hb2", 1),
    ("hfr", 1), ("hyd", 2), ("lamc", 2)])

CON, CON_W = layout([
    ("ident", 128), ("ones", 128), ("blk", 128), ("tri", 256), ("maskt", 256), ("maskn", 256),
    ("lvl", 7 * 256), ("rot", 128), ("cos", LAT), ("sin", LAT), ("wf", 5), ("alt", 1), ("altrow", LAT),
    ("eps", 1), ("eps4", 1), ("fin", 8)])

DFT, DFT_W = layout([("cs", 4 * 2 * LAT), ("csp", 2 * CTX), ("win", NT * 512), ("z", T)])

TWO_PI_HI = 6.28125
TWO_PI_LO = 2 * math.pi - TWO_PI_HI
ROUND = 12582912.0

DVE_LINKS = 255
ACT_LINKS = 7


class Signal:

    def __init__(self, sem, per_layer, base=0, unit=1):
        self.sem, self.per_layer, self.base, self.unit = sem, per_layer, base, unit

    def nth(self, l, n):
        return self.sem, (l * self.per_layer + (self.base + n)) * self.unit


class Chain:

    def __init__(self, eng, sem, per_layer):
        self.eng, self.sem, self.per_layer, self.n, self.l = eng, sem, per_layer, 0, 0

    def link(self, ins):
        ins.then_inc(self.sem, 1)
        self.n += 1
        self.eng.wait_ge(self.sem, self.l * self.per_layer + self.n)


def trunk(nc, ins, outs, links):
    ctx = ExitStack()
    with ctx:
        def sb(name, shape):
            return ctx.enter_context(nc.sbuf_tensor(name, shape, F32))

        def signal(name, per_layer, base=0, unit=1):
            return Signal(ctx.enter_context(nc.semaphore(name)), per_layer, base, unit)

        x = sb("x_res", [P, KC, T])
        ring = sb("w_ring", [P, RING, 10, P])
        par = sb("par", [P, PAR_W])
        con = sb("con", [P, CON_W])
        bout = sb("bout", [P, 4, 2, T])
        stage = sb("stage", [P, 2, PAD])
        mod = sb("mod", [P, 48, 2])
        mod_a = sb("mod_a", [P, 2, KC, 2])
        gt_half = sb("gt_half", [P, KC, 2])
        cond = sb("cond_s", [P, KC, 2])
        cond_t = sb("cond_t", [P, KC, 2])
        rs = sb("rs", [P, T])
        lam_s = sb("lam_s", [P, 72])
        ARENA = 22400
        with ExitStack() as mixer:
            h = mixer.enter_context(nc.sbuf_tensor("h_norm", [P, KC, T], F32))
            arena = mixer.enter_context(nc.sbuf_tensor("arena", [P, ARENA], F32))

        def sbr(name, shape):
            return ctx.enter_context(nc.sbuf_tensor(name, shape, F32R))

        FLOW = ARENA - 3 * KC * T - 4 * KC * P
        h_low = sbr("h_low", [P, KC, T])
        z_high = sbr("z_high", [P, KC, T])
        z_low = sbr("z_low", [P, KC, T])
        flow = sb("flow", [P, FLOW])
        w_high = sbr("w_high", [P, 2, KC, P])
        w_low = sbr("w_low", [P, 2, KC, P])
        h_high = sbr("h_high", [P, KC, T])

        psD = ctx.enter_context(nc.psum_tensor("ps_dense", [P, 2, 1024], F32))
        psA = ctx.enter_context(nc.psum_tensor("ps_aux", [P, 4, 512], F32))

        def p_(name, rows=slice(0, P)):
            a, w = PAR[name]
            return par[rows, a:a + w]

        def c_(name, rows=slice(0, P)):
            a, w = CON[name]
            return con[rows, a:a + w]

        class Carve:
            def __init__(self, at=0):
                self.at = at

            def __call__(self, *dims, rows=P):
                n = math.prod(dims)
                a = arena[0:rows, self.at:self.at + n]
                self.at += n
                assert self.at <= ARENA, self.at
                if len(dims) == 1:
                    return a
                names = " ".join("abcd"[:len(dims)])
                return a.rearrange(f"p ({names}) -> p {names}", **dict(zip("abcd", dims)))

        cv = Carve()
        dft = cv(DFT_W)
        hx0, hx1, hv = cv(2, CV), cv(2, CV), cv(2, CV)
        hvt = cv(NT, 256)
        filt = cv(NT, 2, 256)
        hspec = cv(NT, 3, 256)
        yspec = filt
        hprod = cv(2, 512)
        hnyq = cv(2, 256)
        hmul = cv(512)
        sarg, sn, ssin = (hspec.rearrange("p a b c -> p (a b c)")[:, i * T:(i + 1) * T] for i in range(3))
        dcs = dft[:, 0:4096].rearrange("p (k c f) -> p k c f", k=4, c=2)
        dcsp = dft[:, 4096:4352].rearrange("p (c f) -> p c f", c=2)
        win = dft[:, 4352:4352 + 2560].rearrange("p (t c) -> p t c", t=NT)
        zf = dft[0:33, 4352 + 2560:4352 + 2560 + T]

        cv = Carve()
        qkv = cv(6, CV)
        gz = cv(2, T)
        th = cv(2, CV)
        ktok, vtok = cv(NT, 256), cv(NT, 256)
        small = {n: cv(5, 2, 4) for n in ("g", "beta", "gcol", "es", "eg", "etot", "nbeg", "u", "e", "w", "d", "z0",
                                          "ln", "tot")}
        ab = cv(5, 2, 8)
        expa = cv(8)
        oT = cv(2, T)
        state = cv(2, 2, 2, 64)
        at_norm = cv.at
        rn = cv(4, CV)
        osq = cv(2, T)
        cv = Carve(at_norm)
        decay_t, decay_n, lmat, lmat_t = cv(2, 4, P), cv(2, 4, P), cv(2, 4, P), cv(2, 4, P)
        xi, xit, wm = cv(2, 4, P), cv(2, 4, P), cv(2, 4, P)
        earg = wm
        eq, qg = cv(2, 2, P), cv(2, 2, P)
        bv, ks, rhs, vn = cv(2, 4, 64), cv(2, 4, 64), cv(2, 4, 64), cv(2, 4, 64)

        cv = Carve()
        m_cq, m_ckv = cv(2, T), cv(KEYS)
        m_q, m_k = cv(H, T), cv(H, KEYS)
        m_v = cv(6, 256)
        kpe = cv(KEYS)
        m_sq = cv(3, T)
        m_rs = cv(2, T)
        prob, prob_t = cv(2, T), cv(2, T)
        o_tok = cv(NT, H, 64)
        rot_s = cv(H, LAT)
        att_small = cv(4, 20)
        cv = Carve()
        d_q, d_k = cv(2, T), cv(2, KEYS)
        d_vf = cv(2, T)
        d_v = cv(6, 256)
        d_prob, d_prob2, d_prob_t = cv(2, T), cv(2, T), cv(2, T)
        do_tok = cv(NT, H, 64)
        do_sq = cv(NT, H, 64)
        d_rot = cv(4, LAT)
        d_small = cv(8, 20)
        tg = flow[:, 0:2 * T].rearrange("p (b t) -> p b t", b=2)
        hid_sq = tg
        md, mt = flow[:, 2 * T:3 * T], flow[:, 3 * T:4 * T]

        const_in = signal("const_in", 0, 1, 16)
        x_in = signal("x_in", 0, 1, 16)
        cond_in = signal("cond_in", 0, 1, 16)
        cond_tanh = signal("cond_tanh", 0, 1)
        ring_in = [signal(f"ring_in{j}", PER_SLOT, N_EARLY // RING, 16) for j in range(RING)]
        block_done = signal("block_done", N_BLOCKS, RING + N_EARLY)
        params_in = signal("params_in", 1, 0, 16)
        dft_in = signal("dft_in", 1, 0, 16)
        mod_ready = signal("mod_ready", 2)
        residual = signal("residual_added", 40, 1)
        x_squared = signal("x_squared", 16)
        sumsq_done = signal("sumsq_done", 2)
        rstd_ready = signal("rstd_ready", 2)
        x_scaled = signal("x_scaled", 16)
        h_ready = signal("h_ready", 16)
        dense_out = signal("dense_out", N_WIN)
        conv_out = signal("conv_out", 12)
        filt_ps = signal("filt_ps", 2 + NT)
        filt_arg = signal("filt_arg", 2)
        filt_sin = signal("filt_sin", 2)
        filt_out = signal("filt_out", NT)
        hv_ready = signal("hv_ready", 1)
        hvt_ps = signal("hvt_ps", 1)
        hvt_ready = signal("hvt_ready", 1)
        hspec_ps = signal("hspec_ps", NT)
        hspec_ready = signal("hspec_ready", NT)
        vspec_ps = signal("vspec_ps", NT)
        yspec_ready = signal("yspec_ready", NT)
        nyq_ps = signal("nyq_ps", 1)
        nyq_ready = signal("nyq_ready", 1)
        hy_ps = signal("hy_ps", 2)
        hy_done = signal("hyena_done", 1)
        g_tanh = signal("gdn_tanh", 8)
        g_silu = signal("gdn_silu", 8)
        ab_ps = signal("ab_ps", 1)
        ab_in = signal("ab_in", 1)
        ab_e = signal("ab_e", 1)
        ab_w = signal("ab_w", 1)
        ab_ln = signal("ab_ln", 1)
        g_ready = signal("g_ready", 1)
        cum_ps = signal("cum_ps", 1)
        cum_in = signal("cum_in", 1)
        cum_exp = signal("cum_exp", 1)
        steps_in = signal("step_scalars_ready", 1)
        qk_sq = signal("qk_squared", 4)
        qk_ps = signal("qk_ps", 4)
        qk_ln = signal("qk_ln", 4)
        qk_rs = signal("qk_rs", 1)
        qk_norm = signal("qk_normed", 1)
        kv_ps = signal("kv_ps", NT)
        kv_tok = signal("kv_tok", NT)
        gram_ps = signal("gram_ps", 5)
        decay_arg = signal("decay_arg", 5)
        eq_ready = signal("eq_ready", 5)
        masked = signal("masked", 10)
        decay_ready = signal("decay_ready", 10)
        l_ready = signal("l_ready", 5)
        lt_ps = signal("lt_ps", 5)
        lt_ready = signal("lt_ready", 5)
        at_ps = signal("at_ps", 5)
        x_inv = signal("inverse_level", 35)
        w_ps = signal("w_ps", 30)
        w_ready = signal("w_ready", 30)
        xw_ps = signal("xw_ps", 30)
        scan_in = signal("scan_inputs", 5)
        ks_ps = signal("ks_ps", 5)
        rhs_ready = signal("rhs_ready", 5)
        vn_ps = signal("vn_ps", 5)
        vn_ready = signal("vn_ready", 5)
        o_ps = signal("o_ps", 5)
        scan_done = signal("scan_done", 5)
        osq_ready = signal("osq_ready", 1)
        osum_ps = signal("osum_ps", 1)
        o_rs = signal("o_rs", 1)
        gdn_done = signal("gdn_done", 1)
        mla_sq = signal("mla_sq", 1)
        mla_sum = signal("mla_sum", 2)
        mla_rs = signal("mla_rs", 2)
        mla_n = signal("mla_normed", 2)
        mla_q_ps = signal("mla_q_ps", H)
        mla_q_in = signal("mla_q_in", H)
        mla_k_ps = signal("mla_k_ps", H)
        mla_k_in = signal("mla_k_in", H)
        mla_v_ps = signal("mla_v_ps", 3)
        mla_v_in = signal("mla_v_in", 3)
        rot_ps = signal("rot_ps", 5)
        rot_in = signal("rot_in", 5)
        mla_k_rope = signal("mla_k_rope", 1)
        d_rot_ps = signal("d_rot_ps", 4)
        d_rot_in = signal("d_rot_in", 4)
        dv_ps = signal("dv_ps", 3)
        dv_in = signal("dv_in", 3)
        U = NT * H
        s_ps = signal("scores_ps", 2 * U)
        negmax = signal("negmax", 3 * U)
        exps = signal("exps", 3 * U)
        comb = signal("combined", U)
        pt_ps = signal("pt_ps", 2 * U)
        pt_in = signal("pt_in", 2 * U)
        pv_ps = signal("pv_ps", 2 * U)
        pv_in = signal("pv_in", 2 * U)
        do_sum = signal("do_sum", 1)
        do_rs = signal("do_rs", 1)
        do_normed = signal("do_normed", 1)
        ot_ps = signal("ot_ps", 2)
        br_done = signal("attention_branch_done", 2)
        lam_sum = signal("lam_sum", 1)
        lam_exp = signal("lam_exp", 1)
        gate_act = signal("gate_act", N_GATE)
        proj_used = signal("proj_used", N_GATE + 2)
        merged_add = signal("merged_add", 24)
        merged_high = signal("merged_high", KC)
        merged_ready = signal("merged_ready", KC)
        w_high_in = signal("w_high_ready", N_SPLIT)
        w_low_in = signal("w_low_ready", N_SPLIT)
        h_high_in = signal("h_high_ready", 2 * KC)
        h_split = signal("h_split", 2)
        cond_sum = signal("cond_sum", 0)
        hid_relu = signal("hid_relu", 32)
        hid_square = signal("hid_square", 32)
        hid_high = signal("hid_high", 32)
        hid_ready = signal("hid_ready", 32)
        stored = signal("stored", 5, 0, 16)
        y_ready = signal("y_ready", 0)
        y_out = signal("y_out", 0)
        dve_chain = signal("dve_chain", 0)
        act_chain = signal("act_chain", 0)
        held_waits = signal("held_waits", 0)
        pool_chain = signal("pool_chain", 0)

        def halves(ap):
            return ap.rearrange("p (s n) -> p s n", s=2)

        def psum_halves(b):
            return psD[:, b, :].rearrange("p (s n) -> p s n", s=2)[:, :, 0:HALF]

        def held(eng, *event):
            eng.wait_ge(*event)
            eng.nop().then_inc(held_waits.sem, 1)

        block = ctx.enter_context(nc.Block())

        @block.sync
        def _(sp):
            sp.dma_start(con[:], ins["const"]).then_inc(const_in.sem, 16)
            sp.dma_start(x[:], ins["x"]).then_inc(x_in.sem, 16)
            sp.dma_start(cond[:], ins["cond"]).then_inc(cond_in.sem, 16)

            def load(l, place, dram, at, subs, more=0):
                sp.wait_ge(block_done.sem, l * N_BLOCKS + more + (N_EARLY + place + 1))
                src = dram[l, at].rearrange("o p (s m) -> p (o s) m", m=P)
                j = place % RING
                sp.dma_start(ring[:, j, 0:subs, :], src).then_inc(ring_in[j].sem, 16)

            def stream(l, place, first, n, dram, subs):
                with sp.Fori(0, n // RING) as i:
                    for j in range(RING):
                        load(l, place + j, dram, bass.ds(i * RING + (first + j), 1), subs, i * RING)

            with sp.Fori(0, N_EARLY // RING) as i:
                for j in range(RING):
                    sp.wait_ge(block_done.sem, i * RING + (j + 1))
                    src = ins["w_early"][DEPTH - 1, bass.ds(i * RING + j, 1)].rearrange("o p (s m) -> p (o s) m", m=P)
                    sp.dma_start(ring[:, j, 0:KC, :], src).then_inc(ring_in[j].sem, 16)
            with sp.Fori(0, DEPTH) as l:
                stream(l, 0, 0, 12, ins["w_in"], KC)
                for n in (12, 13):
                    load(l, n, ins["w_in"], slice(n, n + 1), KC)
                stream(l, B_LATE, 0, N_LATE, ins["w_late"], KC)
                for n in (14, 15):
                    load(l, win_at(n), ins["w_in"], slice(n, n + 1), KC)
                stream(l, win_at(16), 16, 8, ins["w_in"], KC)
                stream(l, B_GATE, 0, N_GATE, ins["w_gate"], 10)
                stream(l, B_OUT, 0, N_OUT, ins["w_out"], KC)
                with sp.Fori(0, GROUPS) as g:
                    for j in range(RING):
                        load(l, B_MLP + j, ins["w_early"], bass.ds(g * RING + j, 1), KC, g * N_GROUP)
                    for j in range(2 * KC):
                        load(l, B_MLP + RING + j, ins["w_mlp"], bass.ds(g * (2 * KC) + j, 1), KC, g * N_GROUP)
            sp.wait_ge(y_ready.sem, KC)
            sp.dma_start(outs["y"], h[:]).then_inc(y_out.sem, 16)
            sp.wait_ge(y_out.sem, 16)

        @block.gpsimd
        def _(pool):
            g = nc.gpsimd
            with pool.Fori(0, DEPTH) as l:
                held(pool, *residual.nth(l, 0))
                pool.dma_start(par[:], ins["par"][bass.ds(l, 1)].rearrange("o p w -> p (o w)"))\
                    .then_inc(params_in.sem, 16)
                pool.dma_start(dft, ins["dft"]).then_inc(dft_in.sem, 16)
                for s in range(5):
                    tiles = (s, 3 - s) if s < 4 else (4, 4)
                    pool.wait_ge(*decay_arg.nth(l, s + 1))
                    for m, (dst, mask) in enumerate(((decay_t, "maskt"), (decay_n, "maskn"))):
                        mk = c_(mask).rearrange("p (d j) -> p d j", d=2).unsqueeze(2).to_broadcast([P, 2, 4, P])
                        g.tensor_tensor(dst, earg, mk, ALU.add).then_inc(masked.sem, 1)
                    pool.wait_ge(*steps_in.nth(l, 1))
                    pool.wait_ge(*kv_tok.nth(l, NT))
                    pool.wait_ge(*eq_ready.nth(l, s + 1))
                    for d in range(2):
                        t = tiles[d]
                        vt = vtok[:, t].rearrange("p (h v) -> p h v", h=H)
                        kt = ktok[:, t].rearrange("p (h v) -> p h v", h=H)
                        g.tensor_tensor(bv[:, d], vt, small["beta"][:, s, d].unsqueeze(2).to_broadcast([P, H, 64]),
                                        ALU.mult)
                        g.tensor_tensor(ks[:, d], kt, small["es"][:, s, d].unsqueeze(2).to_broadcast([P, H, 64]),
                                        ALU.mult)
                        c0 = tok_cols(t)
                        last = g.tensor_tensor(qg[:, d], eq[:, d], qkv[:, 0:2, c0:c0 + P], ALU.mult)
                    last.then_inc(scan_in.sem, 1)
                for name, src, complete in (
                        ("state", state[:, 1].rearrange("p d q v -> p (d q v)"), scan_done.nth(l, 5)),
                        ("ckv", m_ckv[:, T:KEYS], mla_n.nth(l, 2)),
                        ("kpe", kpe[64:96, T:KEYS], mla_n.nth(l, 2)),
                        ("dk", d_k[:, :, T:KEYS], dense_out.nth(l, 22)),
                        ("dv", d_v[:, 5], dv_in.nth(l, 3))):
                    held(pool, *complete)
                    dst = outs[name][bass.ds(l, 1)]
                    dst = dst.rearrange("o p c w -> p (o c) w") if name == "dk" else dst.rearrange("o p w -> p (o w)")
                    pool.dma_start(dst, src).then_inc(stored.sem, 16)
                held(pool, *block_done.nth(l, win_at(N_WIN - 1) + 1))
                for c in range(KC):
                    g.tensor_copy(h_high[:, c], h[:, c]).then_inc(h_high_in.sem, 1)
                for c in range(KC):
                    held(pool, *h_high_in.nth(l, c + 1))
                    last = g.tensor_tensor(h_low[:, c], h[:, c], h_high[:, c].bitcast(F32), ALU.subtract)
                last.then_inc(h_split.sem, 1)
                held(pool, *stored.nth(l, 5))

                def low_part(l, n, slot, more=0):
                    pool.wait_ge(w_high_in.sem, l * N_SPLIT + more + (n + 1))
                    g.tensor_tensor(w_low[:, n % 2], ring[:, slot, 0:KC, :], w_high[:, n % 2].bitcast(F32),
                                    ALU.subtract).then_inc(w_low_in.sem, 1)

                with pool.Fori(0, KC) as d:
                    for n in range(4):
                        low_part(l, n, n, d * 4)
                for m in range(N_OUT):
                    low_part(l, N_GATE + m, m % RING)
                with pool.Fori(0, GROUPS) as g_:
                    for j in range(2 * KC):
                        low_part(l, N_GATE + N_OUT + j, j % RING, g_ * (2 * KC))

        @block.tensor
        def _(pe):
            mm = nc.tensor.matmul

            def dense(out, j, rhs):
                for k in range(KC):
                    for a, b in SEGS:
                        last = mm(out[:, a:b], ring[:, j, k, :], rhs[:, k, a:b], start=k == 0, stop=k == KC - 1)
                return last

            def dense_split(b, par_, x_high, x_low):
                for k in range(KC):
                    for w_, x_ in ((w_high, x_high), (w_high, x_low), (w_low, x_high)):
                        for s in range(2):
                            last = mm(psD[:, b, s * 512:s * 512 + HALF], w_[:, par_, k, :],
                                      x_[:, k, s * HALF:(s + 1) * HALF], start=k == 0 and x_ is x_high and w_ is w_high,
                                      stop=k == KC - 1 and w_ is w_low)
                last.then_inc(block_done.sem, 1)

            def landed(l, place, turns=0):
                j = place % RING
                pe.wait_ge(ring_in[j].sem, (l * PER_SLOT + turns + ((N_EARLY + place) // RING + 1)) * 16)

            def modulation(out, j):
                for k in range(KC):
                    last = mm(out, ring[:, j, k, :], cond[:, k, :], start=k == 0, stop=k == KC - 1)
                last.then_inc(block_done.sem, 1)

            def late_modulation(l, n):
                landed(l, B_LATE + n)
                modulation(psD[:, 0, 2 * n:2 * n + 2], (B_LATE + n) % RING)

            def norm_sum(l, which):
                for c in range(KC):
                    pe.wait_ge(*x_squared.nth(l, which * KC + c + 1))
                    for a, b in SEGS:
                        last = mm(psD[:, 0, a:b], c_("ones"), h[:, c, a:b], start=c == 0, stop=c == KC - 1)
                last.then_inc(sumsq_done.sem, 1)

            def win_block(l, n):
                j = n % RING
                landed(l, win_at(n))
                if n >= 2:
                    pe.wait_ge(*dense_out.nth(l, n - 1))
                dense(psD[:, n % 2], j, h).then_inc(block_done.sem, 1)

            for _ in range(RING):
                pe.nop().then_inc(block_done.sem, 1)
            pe.wait_ge(const_in.sem, 16)

            def hyena(l):
                pe.wait_ge(*params_in.nth(l, 1))
                pe.wait_ge(*dft_in.nth(l, 1))
                held(pe, *mod_ready.nth(l, 1))
                flat = psA[0:64, 2:4, :].rearrange("p b n -> p (b n)")
                for a, b in SEGS:
                    last = mm(flat[:, a:b], p_("w1", slice(0, 33)), zf[:, a:b], start=True, stop=True)
                last.then_inc(filt_ps.sem, 1)
                held(pe, *filt_sin.nth(l, 1))
                for a, b in SEGS:
                    last = mm(flat[:, a:b], p_("w2", slice(0, 64)), ssin[0:64, a:b], start=True, stop=True)
                last.then_inc(filt_ps.sem, 1)
                pe.wait_ge(*filt_sin.nth(l, 2))
                for t in range(NT):
                    if t >= 2:
                        pe.wait_ge(*filt_out.nth(l, t - 1))
                    mm(psA[:, t % 2, :], ssin[0:64, t * P:(t + 1) * P], p_("w3", slice(0, 64)), start=True, stop=True)\
                        .then_inc(filt_ps.sem, 1)
                pe.wait_ge(*filt_out.nth(l, NT))
                for f in range(NT):
                    if f >= 2:
                        pe.wait_ge(*hspec_ready.nth(l, f - 1))
                    for c in range(2):
                        out = psA[:, f % 2, c * 256:(c + 1) * 256]
                        if f < 4:
                            for k in range(4):
                                last = mm(out, dcs[:, k, c, f * P:(f + 1) * P], filt[:, k, c, :],
                                          start=k == 0, stop=k == 3)
                        else:
                            last = mm(out, dcsp[:, c, :], filt[:, 4, c, :], start=True, stop=True)
                    last.then_inc(hspec_ps.sem, 1)
                pe.wait_ge(*hv_ready.nth(l, 1))
                pe.wait_ge(*hspec_ready.nth(l, NT))
                for t in range(NT):
                    for c in range(2):
                        c0 = tok_cols(t)
                        last = nc.tensor.transpose(psA[:, t // 2, (t % 2) * 256 + c * P:(t % 2) * 256 + (c + 1) * P],
                                                   hv[:, c, c0:c0 + P], c_("ident"))
                last.then_inc(hvt_ps.sem, 1)
                pe.wait_ge(*hvt_ready.nth(l, 1))
                for s, tiles in enumerate((range(4), (4,))):
                    for i, src in enumerate((filt, hvt)):
                        for n, t in enumerate(tiles):
                            r = src[:, t, 0, :] if i == 0 else src[:, t, :]
                            last = mm(psA[0:1, 2 + s, i * 256:(i + 1) * 256], c_("alt"), r,
                                      start=n == 0, stop=n == len(tiles) - 1)
                last.then_inc(nyq_ps.sem, 1)
                pe.wait_ge(*nyq_ready.nth(l, 1))
                for f in range(NT):
                    if f >= 2:
                        pe.wait_ge(*yspec_ready.nth(l, f - 1))
                    for c in range(2):
                        out = psA[:, f % 2, c * 256:(c + 1) * 256]
                        if f < 4:
                            for k in range(4):
                                last = mm(out, dcs[:, k, c, f * P:(f + 1) * P], hvt[:, k, :],
                                          start=k == 0, stop=k == 3)
                        else:
                            last = mm(out, dcsp[:, c, :], hvt[:, 4, :], start=True, stop=True)
                    last.then_inc(vspec_ps.sem, 1)
                pe.wait_ge(*yspec_ready.nth(l, NT))
                for c in range(2):
                    cols = slice(c * P, (c + 1) * P)
                    for k in range(4):
                        for r in range(2):
                            mm(psD[:, c, 0:LAT], yspec[:, k, r, cols], dcs[:, k, r, :],
                               start=k == 0 and r == 0, stop=False)
                    mm(psD[:, c, 0:LAT], hnyq[0:1, 0, cols], c_("altrow", slice(0, 1)), start=False, stop=True)
                    for r in range(2):
                        mm(psD[:, c, LAT:T], yspec[:, 4, r, cols], dcsp[:, r, :], start=r == 0, stop=False)
                    mm(psD[:, c, LAT:T], hnyq[0:1, 1, cols], c_("altrow", slice(0, 1))[:, 0:CTX],
                       start=False, stop=True).then_inc(hy_ps.sem, 1)

            def gdn(l):
                for t in range(NT):
                    for k in range(KC):
                        last = mm(psA[:, 0, t * 16:(t + 1) * 16], h[:, k, t * P:(t + 1) * P],
                                  p_("wab")[:, k * 16:(k + 1) * 16], start=k == 0, stop=k == KC - 1)
                last.then_inc(ab_ps.sem, 1)
                pe.wait_ge(*g_ready.nth(l, 1))
                tri = c_("tri").rearrange("p (d j) -> p d j", d=2)
                for d in range(2):
                    mm(psA[:, 1, d * 20:(d + 1) * 20], tri[:, d], small["g"][:, :, d, :], start=True, stop=True)
                mm(psA[:, 1, 40:80], c_("ones"), small["g"].rearrange("p s d h -> p (s d h)"), start=True, stop=True)\
                    .then_inc(cum_ps.sem, 1)
                pe.wait_ge(*cum_in.nth(l, 1))
                for c in range(4):
                    pe.wait_ge(*qk_sq.nth(l, c + 1))
                    if c >= 2:
                        pe.wait_ge(*qk_ln.nth(l, c - 1))
                    out = psA[:, 2 * (c % 2):2 * (c % 2) + 2, :].rearrange("p b n -> p (b n)")
                    for a, b in ((0, 512), (512, CV)):
                        last = mm(out[:, a:b], c_("blk"), th[:, c % 2, a:b], start=True, stop=True)
                    last.then_inc(qk_ps.sem, 1)
                pe.wait_ge(*qk_norm.nth(l, 1))
                for t in range(NT):
                    if t >= 2:
                        pe.wait_ge(*kv_tok.nth(l, t - 1))
                    c0 = tok_cols(t)
                    for c in range(4):
                        last = nc.tensor.transpose(psA[:, t % 2, c * P:(c + 1) * P], qkv[:, 2 + c, c0:c0 + P],
                                                   c_("ident"))
                    last.then_inc(kv_ps.sem, 1)
                pe.wait_ge(*kv_tok.nth(l, NT))
                pe.wait_ge(*steps_in.nth(l, 1))
                units = [(d, hh) for d in range(2) for hh in range(H)]
                pe.wait_ge(*dense_out.nth(l, WIN_1))
                late = 0
                for s in range(5):
                    tiles = (s, 3 - s) if s < 4 else (4, 4)
                    seq = 0 if s < 4 else 1
                    if s:
                        pe.wait_ge(*scan_done.nth(l, s))
                    for d, hh in units:
                        mm(psA[:, d, hh * P:(hh + 1) * P], small["g"][:, s, d, hh:hh + 1].to_broadcast([P, P]),
                           tri[:, d], start=True, stop=True)

                    def rows(hh):
                        return slice(64 * (hh % 2), 64 * (hh % 2) + 64)

                    def part(hh, d, c):
                        c0 = tok_cols(tiles[d])
                        return qkv[rows(hh), c + hh // 2, c0:c0 + P]

                    for d, hh in units:
                        q4 = d * 2 + hh // 2
                        last = mm(psA[:, 2 + hh % 2, q4 * P:(q4 + 1) * P], part(hh, d, 2), part(hh, d, 2),
                                  start=True, stop=True)
                    last.then_inc(gram_ps.sem, 1)
                    pe.wait_ge(*eq_ready.nth(l, s + 1))
                    pe.wait_ge(*l_ready.nth(l, s + 1))
                    for d, hh in units:
                        last = nc.tensor.transpose(psA[:, d, hh * P:(hh + 1) * P], lmat[:, d, hh], c_("ident"))
                    last.then_inc(lt_ps.sem, 1)
                    for d, hh in units:
                        q4 = d * 2 + hh // 2
                        last = mm(psA[:, 2 + hh % 2, q4 * P:(q4 + 1) * P], part(hh, d, 2), part(hh, d, 0),
                                  start=True, stop=True)
                    last.then_inc(at_ps.sem, 1)
                    for k in range(1, 7):
                        pe.wait_ge(*x_inv.nth(l, s * 7 + k))
                        for d, hh in units:
                            last = mm(psA[:, d, hh * P:(hh + 1) * P], lmat_t[:, d, hh], xi[:, d, hh],
                                      start=True, stop=True)
                        last.then_inc(w_ps.sem, 1)
                        for _ in range(1 if s < 3 or k > 1 else 2):
                            late_modulation(l, late)
                            late += 1
                        pe.wait_ge(*w_ready.nth(l, s * 6 + k))
                        for d, hh in units:
                            last = mm(psA[:, 2 + d, hh * P:(hh + 1) * P], wm[:, d, hh], xit[:, d, hh],
                                      start=True, stop=True)
                        if k < 6:
                            for d, hh in units:
                                last = mm(psA[:, d, hh * P:(hh + 1) * P], xit[:, d, hh], wm[:, d, hh],
                                          start=True, stop=True)
                        last.then_inc(xw_ps.sem, 1)
                    pe.wait_ge(*x_inv.nth(l, s * 7 + 7))
                    for d, hh in units:
                        q4 = d * 2 + hh // 2
                        last = mm(psA[:, hh % 2, q4 * 64:(q4 + 1) * 64], part(hh, d, 2),
                                  state[rows(hh), seq, d, hh // 2, :], start=True, stop=True)
                    last.then_inc(ks_ps.sem, 1)
                    pe.wait_ge(*rhs_ready.nth(l, s + 1))
                    for d, hh in units:
                        last = mm(psA[:, 2, (d * 4 + hh) * 64:(d * 4 + hh + 1) * 64], xit[:, d, hh], rhs[:, d, hh],
                                  start=True, stop=True)
                    last.then_inc(vn_ps.sem, 1)
                    pe.wait_ge(*vn_ready.nth(l, s + 1))
                    pe.wait_ge(*scan_in.nth(l, s + 1))
                    for d, hh in units:
                        q4 = d * 2 + hh // 2
                        out = psA[rows(hh), 3, q4 * P:(q4 + 1) * P]
                        mm(out, vn[:, d, hh], decay_t[:, d, hh], start=True, stop=False)
                        mm(out, state[rows(hh), seq, d, hh // 2, :], qg[rows(hh), d, hh // 2], start=False, stop=True)
                    for d, hh in units:
                        q4 = d * 2 + hh // 2
                        last = mm(psA[rows(hh), 0, q4 * 64:(q4 + 1) * 64], ks[:, d, hh], vn[:, d, hh],
                                  start=True, stop=True)
                    last.then_inc(o_ps.sem, 1)
                assert late == N_LATE
                pe.wait_ge(*osq_ready.nth(l, 1))
                for c in range(2):
                    out = psA[:, 2 * c:2 * c + 2, :].rearrange("p b n -> p (b n)")
                    for a, b in SEGS:
                        last = mm(out[:, a:b], c_("blk"), osq[:, c, a:b], start=True, stop=True)
                last.then_inc(osum_ps.sem, 1)

            def attend(l, n0, scores, ready, v, pt_src, n_maps):
                e0 = n0

                def score(u):
                    hh, t = divmod(u, NT)
                    if n_maps == 1:
                        if u >= 2:
                            pe.wait_ge(*exps.nth(l, u - 1))
                    elif u >= 1:
                        pe.wait_ge(*exps.nth(l, U + 2 * u))
                    for m in range(n_maps):
                        b2 = 2 * (u % 2) if n_maps == 1 else 2 * m
                        out = psA[:, b2:b2 + 2, :].rearrange("p b n -> p (b n)")
                        q, k = scores(hh, m)
                        qt = q[:, t * P:(t + 1) * P]
                        if t < NT - 1:
                            for a, b in SEGS:
                                last = mm(out[:, a:b], qt, k[:, a:b], start=True, stop=True)
                        else:
                            last = mm(out[:, 0:CTX], qt, k[:, T:KEYS], start=True, stop=True)
                    last.then_inc(s_ps.sem, 1)

                score(0)
                for u in range(U):
                    hh, t = divmod(u, NT)
                    if u + 1 < U:
                        score(u + 1)
                    nk = 5 if t < NT - 1 else 1
                    pe.wait_ge(*ready(u))
                    if u >= 2:
                        pe.wait_ge(*pv_in.nth(l, n0 + u - 1))
                    for k in range(nk):
                        last = nc.tensor.transpose(psD[:, u % 2, k * P:(k + 1) * P],
                                                   pt_src[:, u % 2, k * P:(k + 1) * P], c_("ident"))
                    last.then_inc(pt_ps.sem, 1)
                    pe.wait_ge(*pt_in.nth(l, n0 + u + 1))
                    pt = prob_t if n_maps == 1 else d_prob_t
                    for k in range(nk):
                        last = mm(psD[:, u % 2, T:T + 64], pt[:, u % 2, k * P:(k + 1) * P],
                                  v[:, k if nk > 1 else 5, hh * 64:(hh + 1) * 64], start=k == 0, stop=k == nk - 1)
                    last.then_inc(pv_ps.sem, 1)

            def turn_outputs(o):
                for c in range(2):
                    out = psA[:, 2 * c:2 * c + 2, :].rearrange("p b n -> p (b n)")
                    for t in range(NT):
                        src = o[:, t].rearrange("p h v -> p (h v)")[:, c * P:(c + 1) * P]
                        last = nc.tensor.transpose(out[:, t * P:(t + 1) * P], src, c_("ident"))
                last.then_inc(ot_ps.sem, 1)

            def mla(l):
                pe.wait_ge(*gdn_done.nth(l, 1))
                pe.wait_ge(*mla_sq.nth(l, 1))
                for n, chunks in enumerate(((0, 1), (2,))):
                    out = psA[:, 2 * n:2 * n + 2, :].rearrange("p b n -> p (b n)")
                    for c in chunks:
                        for a, b in SEGS:
                            last = mm(out[:, a:b], c_("ones"), m_sq[:, c, a:b], start=c == chunks[0],
                                      stop=c == chunks[-1])
                    last.then_inc(mla_sum.sem, 1)
                pe.wait_ge(*mla_n.nth(l, 1))
                uq = p_("uq").rearrange("p (k c) -> p k c", k=2)
                for hh in range(H):
                    if hh >= 2:
                        pe.wait_ge(*mla_q_in.nth(l, hh - 1))
                    for k in range(2):
                        for a, b in SEGS:
                            last = mm(psD[0:96, hh % 2, a:b], uq[:, k, hh * 96:(hh + 1) * 96], m_cq[:, k, a:b],
                                      start=k == 0, stop=k == 1)
                    last.then_inc(mla_q_ps.sem, 1)
                pe.wait_ge(*mla_n.nth(l, 2))
                pe.wait_ge(*mla_q_in.nth(l, H))
                ukv = p_("ukv").rearrange("p (h c) -> p h c", h=H)
                for hh in range(H):
                    if hh >= 2:
                        pe.wait_ge(*mla_k_in.nth(l, hh - 1))
                    for a, b in ((0, 512), (512, KEYS)):
                        last = mm(psD[0:64, hh % 2, a:b], ukv[:, hh, 0:64], m_ckv[:, a:b], start=True, stop=True)
                    last.then_inc(mla_k_ps.sem, 1)
                for n in range(3):
                    for t in (2 * n, 2 * n + 1):
                        last = mm(psA[:, n, (t % 2) * 256:(t % 2 + 1) * 256], m_ckv[:, t * P:(t + 1) * P],
                                  ukv[:, :, 64:128], start=True, stop=True)
                    last.then_inc(mla_v_ps.sem, 1)
                for n in range(5):
                    if n == 0:
                        held(pe, *mla_k_in.nth(l, H))
                    else:
                        held(pe, *rot_in.nth(l, n))
                    src = m_q[64:96, n, 0:LAT] if n < H else kpe[64:96, 0:LAT]
                    mm(psD[64:96, n % 2, 0:LAT], c_("rot", slice(64, 96))[:, 64:96], src, start=True, stop=True)\
                        .then_inc(rot_ps.sem, 1)
                pe.wait_ge(*mla_k_rope.nth(l, 1))
                pe.wait_ge(*mla_v_in.nth(l, 3))
                attend(l, 0, lambda hh, m: (m_q[0:96, hh], m_k[0:96, hh]), lambda u: exps.nth(l, u + 1), m_v, prob, 1)
                pe.wait_ge(*pv_in.nth(l, U))
                turn_outputs(o_tok)

            def diff(l):
                pe.wait_ge(*br_done.nth(l, 1))
                for n in range(4):
                    if n == 0:
                        pe.wait_ge(*dense_out.nth(l, N_WIN))
                    else:
                        pe.wait_ge(*d_rot_in.nth(l, n))
                    src = (d_q if n < 2 else d_k)[:, n % 2, 0:LAT]
                    mm(psD[:, n % 2, 0:LAT], c_("rot"), src, start=True, stop=True).then_inc(d_rot_ps.sem, 1)
                for n in range(3):
                    for t in (2 * n, 2 * n + 1):
                        if t < NT:
                            for c in range(2):
                                last = nc.tensor.transpose(
                                    psA[:, n, (t % 2) * 256 + c * P:(t % 2) * 256 + (c + 1) * P],
                                    d_vf[:, c, t * P:(t + 1) * P], c_("ident"))
                    last.then_inc(dv_ps.sem, 1)
                pe.wait_ge(*d_rot_in.nth(l, 4))
                pe.wait_ge(*dv_in.nth(l, 3))

                def scores(hh, m):
                    g4 = hh * 2 + m
                    r = slice(32 * (g4 % 4), 32 * (g4 % 4) + 32)
                    return d_q[r, g4 // 4], d_k[r, g4 // 4]

                attend(l, U, scores, lambda u: comb.nth(l, u + 1), d_v, d_prob, 2)
                pe.wait_ge(*do_normed.nth(l, 1))
                turn_outputs(do_tok)

            def merge(l):
                held(pe, *br_done.nth(l, 2))
                held(pe, *h_split.nth(l, 1))
                with pe.Fori(0, KC) as d:
                    for n in range(4):
                        landed(l, B_GATE + n, d)
                        b = n % 2
                        pe.wait_ge(proj_used.sem, l * (N_GATE + 2) + d * 4 + (n + 1))
                        out = psA[:, 2 * b:2 * b + 2, :].rearrange("p b n -> p (b n)")
                        for k in range(2):
                            for a, c in SEGS:
                                mm(out[:, a:c], ring[:, n, KC + k, :], bout[:, n, k, a:c], start=k == 0, stop=k == 1)
                        pe.wait_ge(w_low_in.sem, l * N_SPLIT + d * 4 + (n + 1))
                        dense_split(b, b, h_high, h_low)

            def out_proj(l):
                for m in range(KC):
                    pe.wait_ge(*w_low_in.nth(l, N_GATE + m + 1))
                    if m == 0:
                        pe.wait_ge(*merged_ready.nth(l, KC))
                    elif m >= 2:
                        pe.wait_ge(*residual.nth(l, m - 1))
                    dense_split(m % 2, m % 2, z_high, z_low)

            def mlp(l):
                with pe.Fori(0, GROUPS) as g:
                    for j in range(RING):
                        landed(l, B_MLP + j, g * (N_GROUP // RING))
                        modulation(psA[:, 0, bass.ds(g * (2 * RING) + 2 * j, 2)], j)
                    for j in range(KC):
                        pe.wait_ge(w_low_in.sem, l * N_SPLIT + g * (2 * KC) + (N_GATE + N_OUT + j + 1))
                        if j == 0:
                            pe.wait_ge(*h_split.nth(l, 2))
                        if j < 2:
                            pe.wait_ge(residual.sem, l * 40 + g * 8 + (1 + 7 + j))
                        else:
                            pe.wait_ge(hid_relu.sem, l * 32 + g * 8 + (j - 1))
                        dense_split(j % 2, j % 2, h_high, h_low)
                    for m in range(KC):
                        pe.wait_ge(w_low_in.sem, l * N_SPLIT + g * (2 * KC) + (N_GATE + N_OUT + KC + m + 1))
                        if m == 0:
                            pe.wait_ge(hid_ready.sem, l * 32 + g * 8 + 8)
                        if m < 2:
                            pe.wait_ge(hid_relu.sem, l * 32 + g * 8 + (7 + m))
                        else:
                            pe.wait_ge(residual.sem, l * 40 + g * 8 + (1 + 8 + m - 1))
                        dense_split(m % 2, m % 2, z_high, z_low)

            pe.wait_ge(residual.sem, 1)
            with pe.Fori(0, N_EARLY // RING) as i:
                for j in range(RING):
                    pe.wait_ge(ring_in[j].sem, (i + 1) * 16)
                    modulation(psA[:, 0, bass.ds(i * (2 * RING) + 2 * j, 2)], j)
            with pe.Fori(0, DEPTH) as l:
                norm_sum(l, 0)
                pe.wait_ge(*h_ready.nth(l, KC))
                for n in range(6):
                    win_block(l, n)
                hyena(l)
                pe.wait_ge(*hy_done.nth(l, 1))
                for n in range(6, 14):
                    win_block(l, n)
                gdn(l)
                pe.wait_ge(*gdn_done.nth(l, 1))
                for n in range(14, 18):
                    win_block(l, n)
                mla(l)
                pe.wait_ge(*br_done.nth(l, 1))
                for n in range(18, 24):
                    win_block(l, n)
                diff(l)
                merge(l)
                out_proj(l)
                pe.wait_ge(*residual.nth(l, 7))
                norm_sum(l, 1)
                mlp(l)
            norm_sum(DEPTH, 0)

        @block.scalar
        def _(act):
            a = nc.scalar.activation
            chain = Chain(act, act_chain.sem, links[1])

            def evac(l, n, dst):
                act.wait_ge(*block_done.nth(l, win_at(n) + 1))
                a(dst, psD[:, n % 2, 0:T], ACT.Copy).then_inc(dense_out.sem, 1)

            def evac_conv(l, n):
                act.wait_ge(*block_done.nth(l, win_at(n) + 1))
                if n >= 2:
                    act.wait_ge(*conv_out.nth(l, n - 1))
                a(stage[:, n % 2, 1:1 + LAT], psD[:, n % 2, 0:LAT], ACT.Copy)
                a(stage[:, n % 2, 3 + LAT:3 + T], psD[:, n % 2, LAT:T], ACT.Copy).then_inc(dense_out.sem, 1)

            def high_part(l, place, turns=0, back=2):
                j = place % RING
                act.wait_ge(ring_in[j].sem, (l * PER_SLOT + turns + ((N_EARLY + place) // RING + 1)) * 16)
                act.wait_ge(block_done.sem, l * N_BLOCKS + turns * RING + (RING + N_EARLY + place - back + 1))
                a(w_high[:, place % 2], ring[:, j, 0:KC, :], ACT.Copy).then_inc(w_high_in.sem, 1)

            def norm(l, which):
                for c in range(KC):
                    if which and c + 2 < N_OUT:
                        high_part(l, B_OUT + c + 2)
                    act.wait_ge(*residual.nth(l, which * (c + 1)))
                    a(h[:, c], x[:, c], ACT.Square).then_inc(x_squared.sem, 1)
                act.wait_ge(*sumsq_done.nth(l, which + 1))
                chain.link(a(rs[:], psD[:, 0, 0:T], ACT.Ln, scale=1.0 / D, bias=c_("eps")))
                a(rs[:], rs[:], ACT.Exp, scale=-0.5).then_inc(rstd_ready.sem, 1)

            def modulate(l, which):
                act.wait_ge(*mod_ready.nth(l, 1 + which))
                for c in range(KC):
                    act.wait_ge(*x_scaled.nth(l, which * KC + c + 1))
                    for s, (p, q) in enumerate(SEGS):
                        last = a(h[:, c, p:q], h[:, c, p:q], ACT.Identity, scale=mod_a[:, which, c, s:s + 1],
                                 bias=mod[:, which * 24 + c, s:s + 1])
                    last.then_inc(h_ready.sem, 1)

            def hyena(l):
                for n in range(2):
                    act.wait_ge(*filt_arg.nth(l, n + 1))
                    a(ssin[0:64], sarg[0:64], ACT.Sin).then_inc(filt_sin.sem, 1)
                for f in range(NT):
                    act.wait_ge(*hspec_ps.nth(l, f + 1))
                    wf = c_("wf")[:, f:f + 1]
                    a(hspec[:, f, 0:2], psA[:, f % 2, :].rearrange("p (c n) -> p c n", c=2), ACT.Identity, scale=wf)
                    a(hspec[:, f, 2], psA[:, f % 2, 0:256], ACT.Identity, scale=wf).then_inc(hspec_ready.sem, 1)
                act.wait_ge(*hvt_ps.nth(l, 1))
                a(hvt[:, 0:4], psA[:, 0:2, :].rearrange("p b (t n) -> p (b t) n", t=2), ACT.Copy)
                a(hvt[:, 4], psA[:, 2, 0:256], ACT.Copy).then_inc(hvt_ready.sem, 1)

            def gdn(l):
                act.wait_ge(*hy_done.nth(l, 1))
                for n in range(6, 12):
                    evac_conv(l, n)
                    if n > 6:
                        silu_tanh(l, n - 7)
                silu_tanh(l, 5)
                for c in range(2):
                    act.wait_ge(*block_done.nth(l, win_at(12 + c) + 1))
                    ins_ = a(gz[:, c], psD[:, c, 0:T], ACT.Copy)
                    ins_.then_inc(dense_out.sem, 1)
                    act.wait_ge(*dense_out.nth(l, 13 + c))
                    act.wait_ge(*g_silu.nth(l, 5 + c))
                    a(th[:, c, 0:T], gz[:, c], ACT.Tanh, scale=0.5).then_inc(g_tanh.sem, 1)
                act.wait_ge(*ab_in.nth(l, 1))
                f8 = lambda n: small[n].rearrange("p s d h -> p (s d h)")
                a(expa, p_("alog"), ACT.Exp)
                a(small["z0"], ab[:, :, :, 4:8], ACT.Tanh, scale=0.5)
                chain.link(a(f8("e"), f8("u"), ACT.Abs))
                a(f8("e"), f8("e"), ACT.Exp, scale=-1.0).then_inc(ab_e.sem, 1)
                act.wait_ge(*ab_w.nth(l, 1))
                a(f8("ln"), f8("w"), ACT.Ln).then_inc(ab_ln.sem, 1)
                act.wait_ge(*cum_in.nth(l, 1))
                a(f8("eg"), f8("gcol"), ACT.Exp)
                a(f8("etot"), f8("tot"), ACT.Exp)
                a(f8("es"), f8("es"), ACT.Exp).then_inc(cum_exp.sem, 1)
                for c in range(4):
                    act.wait_ge(*(g_silu.nth(l, 8) if c < 2 else qk_ps.nth(l, c - 1)))
                    a(th[:, c % 2], qkv[:, c], ACT.Square).then_inc(qk_sq.sem, 1)
                    if c >= 1:
                        length_ln(l, c - 1)
                length_ln(l, 3)
                act.wait_ge(*qk_ln.nth(l, 4))
                a(rn, rn, ACT.Exp, scale=-0.5).then_inc(qk_rs.sem, 1)
                for t in range(NT):
                    act.wait_ge(*kv_ps.nth(l, t + 1))
                    a(ktok[:, t], psA[:, t % 2, 0:256], ACT.Copy)
                    a(vtok[:, t], psA[:, t % 2, 256:512], ACT.Copy, scale=0.5).then_inc(kv_tok.sem, 1)
                for s in range(5):
                    act.wait_ge(*decay_arg.nth(l, s + 1))
                    for r in range(2):
                        lanes = slice(64 * r, 64 * r + 64)
                        src = psA[lanes, 0:2, :].rearrange("p d (q r j) -> p d q r j", q=2, r=2)[:, :, :, r]
                        last = a(eq[lanes], src, ACT.Exp)
                    last.then_inc(eq_ready.sem, 1)
                    act.wait_ge(*masked.nth(l, 2 * s + 1))
                    a(decay_t, decay_t, ACT.Exp).then_inc(decay_ready.sem, 1)
                    act.wait_ge(*masked.nth(l, 2 * s + 2))
                    a(decay_n, decay_n, ACT.Exp, scale=-1.0).then_inc(decay_ready.sem, 1)
                    act.wait_ge(*lt_ps.nth(l, s + 1))
                    a(lmat_t.rearrange("p d h j -> p d (h j)"), psA[:, 0:2, :], ACT.Copy).then_inc(lt_ready.sem, 1)
                    act.wait_ge(*vn_ps.nth(l, s + 1))
                    a(vn.rearrange("p d h v -> p (d h v)"), psA[:, 2, :], ACT.Copy).then_inc(vn_ready.sem, 1)
                act.wait_ge(*scan_done.nth(l, 5))
                a(osq, oT, ACT.Square).then_inc(osq_ready.sem, 1)
                act.wait_ge(*osum_ps.nth(l, 1))
                src = psA[:, :, :].rearrange("p (c b) n -> p c (b n)", c=2)[:, :, 0:T]
                chain.link(a(osq, src, ACT.Ln, scale=1.0 / 64, bias=c_("eps")))
                a(osq, osq, ACT.Exp, scale=-0.5).then_inc(o_rs.sem, 1)

            def silu_tanh(l, c):
                act.wait_ge(*conv_out.nth(l, 6 + c + 1))
                if c >= 2:
                    act.wait_ge(*g_silu.nth(l, c - 1))
                a(th[:, c % 2], qkv[:, c], ACT.Tanh, scale=0.5).then_inc(g_tanh.sem, 1)

            def length_ln(l, c):
                act.wait_ge(*qk_ps.nth(l, c + 1))
                src = psA[:, 2 * (c % 2):2 * (c % 2) + 2, :].rearrange("p b n -> p (b n)")[:, 0:CV]
                a(rn[:, c], src, ACT.Ln, bias=c_("eps4")).then_inc(qk_ln.sem, 1)

            def attend(l, n0, n_maps, sc, small_, probs, pt):
                x0 = 0 if n_maps == 1 else U

                def exp(u):
                    nk = T if u % NT < NT - 1 else CTX
                    for m in range(n_maps):
                        n = x0 + n_maps * u + m + 1
                        act.wait_ge(*negmax.nth(l, n))
                        b2 = 2 * (u % 2) if n_maps == 1 else 2 * m
                        src = psA[:, b2:b2 + 2, :].rearrange("p b n -> p (b n)")[:, 0:nk]
                        a(probs[m][:, u % 2, 0:nk], src, ACT.Exp, scale=sc, bias=small_[:, 2 * m, u:u + 1],
                          accum_out=small_[:, 2 * m + 1, u:u + 1]).then_inc(exps.sem, 1)

                exp(0)
                for u in range(U):
                    if u + 1 < U:
                        exp(u + 1)
                    nk = T if u % NT < NT - 1 else CTX
                    act.wait_ge(*pt_ps.nth(l, n0 + u + 1))
                    if u >= 2:
                        act.wait_ge(*pv_ps.nth(l, n0 + u - 1))
                    a(pt[:, u % 2, 0:nk], psD[:, u % 2, 0:nk], ACT.Copy).then_inc(pt_in.sem, 1)

            def branch_out(l, n, branch):
                act.wait_ge(*ot_ps.nth(l, n))
                for c in range(2):
                    last = a(bout[:, branch, c], psA[:, 2 * c:2 * c + 2, :].rearrange("p b n -> p (b n)")[:, 0:T],
                             ACT.Copy)
                last.then_inc(br_done.sem, 1)

            def mla(l):
                act.wait_ge(*gdn_done.nth(l, 1))
                act.wait_ge(*stored.nth(l, 1))
                evac(l, 14, m_cq[:, 0])
                evac(l, 15, m_cq[:, 1])
                for n, dst in ((16, m_ckv), (17, kpe)):
                    act.wait_ge(*block_done.nth(l, win_at(n) + 1))
                    a(dst[:, 0:LAT], psD[:, n % 2, 0:LAT], ACT.Copy)
                    a(dst[:, T:KEYS], psD[:, n % 2, LAT:T], ACT.Copy).then_inc(dense_out.sem, 1)
                act.wait_ge(*dense_out.nth(l, 18))
                a(m_sq[:, 0:2], m_cq, ACT.Square)
                a(m_sq[:, 2, 0:LAT], m_ckv[:, 0:LAT], ACT.Square)
                a(m_sq[:, 2, LAT:T], m_ckv[:, T:KEYS], ACT.Square).then_inc(mla_sq.sem, 1)
                for n, wd in enumerate((256, 128)):
                    act.wait_ge(*mla_sum.nth(l, n + 1))
                    src = psA[:, 2 * n:2 * n + 2, :].rearrange("p b n -> p (b n)")[:, 0:T]
                    chain.link(a(m_rs[:, n], src, ACT.Ln, scale=1.0 / wd, bias=c_("eps")))
                for n in range(2):
                    a(m_rs[:, n], m_rs[:, n], ACT.Exp, scale=-0.5).then_inc(mla_rs.sem, 1)
                for hh in range(H):
                    act.wait_ge(*mla_q_ps.nth(l, hh + 1))
                    a(m_q[0:96, hh], psD[0:96, hh % 2, 0:T], ACT.Copy).then_inc(mla_q_in.sem, 1)
                for hh in range(H):
                    act.wait_ge(*mla_k_ps.nth(l, hh + 1))
                    a(m_k[0:64, hh], psD[0:64, hh % 2, 0:KEYS], ACT.Copy).then_inc(mla_k_in.sem, 1)
                for n in range(3):
                    act.wait_ge(*mla_v_ps.nth(l, n + 1))
                    a(m_v[:, 2 * n:2 * n + 2], psA[:, n, :].rearrange("p (t c) -> p t c", t=2), ACT.Copy)\
                        .then_inc(mla_v_in.sem, 1)
                attend(l, 0, 1, 96 ** -0.5, att_small, (prob,), prob_t)
                branch_out(l, 1, 0)

            def diff(l):
                act.wait_ge(*stored.nth(l, 3))
                act.wait_ge(*br_done.nth(l, 1))
                for n in (18, 19):
                    evac(l, n, d_q[:, n - 18])
                for n in (20, 21):
                    act.wait_ge(*block_done.nth(l, win_at(n) + 1))
                    a(d_k[:, n - 20, 0:LAT], psD[:, n % 2, 0:LAT], ACT.Copy)
                    a(d_k[:, n - 20, T:KEYS], psD[:, n % 2, LAT:T], ACT.Copy).then_inc(dense_out.sem, 1)
                for n in (22, 23):
                    evac(l, n, d_vf[:, n - 22])
                a(d_k[:, :, LAT:T], p_("dk_c").rearrange("p (c t) -> p c t", c=2), ACT.Copy)
                a(d_v[:, 4], p_("dv_c"), ACT.Copy)
                for n in range(3):
                    act.wait_ge(*dv_ps.nth(l, n + 1))
                    if n < 2:
                        last = a(d_v[:, 2 * n:2 * n + 2], psA[:, n, :].rearrange("p (t c) -> p t c", t=2), ACT.Copy)
                    else:
                        last = a(d_v[:, 5], psA[:, n, 0:256], ACT.Copy)
                    last.then_inc(dv_in.sem, 1)
                act.wait_ge(*lam_sum.nth(l, 1))
                a(lam_s[:, 68:70], lam_s[:, 64:66], ACT.Exp).then_inc(lam_exp.sem, 1)
                attend(l, U, 2, 32 ** -0.5, d_small, (d_prob, d_prob2), d_prob_t)
                act.wait_ge(*do_sum.nth(l, 1))
                chain.link(a(d_small[:, 4], d_small[:, 4], ACT.Ln, scale=1.0 / 64, bias=c_("eps")))
                a(d_small[:, 4], d_small[:, 4], ACT.Exp, scale=-0.5).then_inc(do_rs.sem, 1)
                branch_out(l, 2, 3)

            def merge(l):
                act.wait_ge(*stored.nth(l, 5))
                high_part(l, B_GATE)
                with act.Fori(0, KC) as d:
                    for n in range(4):
                        high_part(l, B_GATE + n + 1, d)
                        act.wait_ge(block_done.sem, l * N_BLOCKS + d * 4 + (RING + N_EARLY + B_GATE + n + 1))
                        act.wait_ge(proj_used.sem, l * (N_GATE + 2) + d * 4 + (n + 1))
                        a(halves(tg[:, n % 2]), psum_halves(n % 2), ACT.Tanh, scale=0.5).then_inc(gate_act.sem, 1)

            def mlp(l):
                turns = N_GROUP // RING
                first = B_MLP + RING
                with act.Fori(0, GROUPS) as g:
                    high_part(l, first, g * turns, 2 + RING)
                    for j in range(KC):
                        high_part(l, first + j + 1, g * turns, 2 + RING if j == 0 else 2)
                        act.wait_ge(block_done.sem, l * N_BLOCKS + g * N_GROUP + (RING + N_EARLY + first + j + 1))
                        if j >= 2:
                            act.wait_ge(hid_ready.sem, l * 32 + g * 8 + (j - 1))
                        a(halves(hid_sq[:, j % 2]), psum_halves(j % 2), ACT.Relu).then_inc(hid_relu.sem, 1)
                        act.wait_ge(hid_relu.sem, l * 32 + g * 8 + (j + 1))
                        a(hid_sq[:, j % 2], hid_sq[:, j % 2], ACT.Square).then_inc(hid_square.sem, 1)
                    for m in range(1, KC):
                        high_part(l, first + KC + m, g * turns)

            act.wait_ge(const_in.sem, 16)
            act.wait_ge(cond_in.sem, 16)
            a(cond_t[:], cond[:], ACT.Tanh, scale=0.5).then_inc(cond_tanh.sem, 1)
            with act.Fori(0, DEPTH) as l:
                chain.l, chain.n = l, 0
                act.wait_ge(*params_in.nth(l, 1))
                norm(l, 0)
                modulate(l, 0)
                for n in range(6):
                    evac_conv(l, n)
                hyena(l)
                gdn(l)
                mla(l)
                diff(l)
                merge(l)
                high_part(l, B_OUT + 1)
                norm(l, 1)
                modulate(l, 1)
                mlp(l)
                n_links = chain.n
            assert n_links == links[1], ("ACT_LINKS", n_links)
            chain.l, chain.n = DEPTH, 0
            norm(DEPTH, 0)
            for c in range(KC):
                act.wait_ge(*x_scaled.nth(DEPTH, c + 1))
                a(h[:, c], h[:, c], ACT.Identity, scale=c_("fin")[:, c:c + 1]).then_inc(y_ready.sem, 1)

        @block.vector
        def _(dve):
            v = nc.vector
            chain = Chain(dve, dve_chain.sem, links[0])
            link = chain.link

            def norm_scale(which, name):
                return v.scalar_tensor_tensor(out=mod_a[:, which], in0=mod[:, which * 24 + 8:which * 24 + 16],
                                              scalar=1.0, in1=p_(name).unsqueeze(2).to_broadcast([P, KC, 2]),
                                              op0=ALU.add, op1=ALU.mult)

            def norm(l, which):
                dve.wait_ge(*rstd_ready.nth(l, which + 1))
                for c in range(KC):
                    v.tensor_tensor(h[:, c], x[:, c], rs[:], ALU.mult).then_inc(x_scaled.sem, 1)

            def split_h(l):
                for c in range(KC):
                    dve.wait_ge(*h_ready.nth(l, KC + c + 1))
                    v.tensor_copy(h_high[:, c], h[:, c]).then_inc(h_high_in.sem, 1)
                    dve.wait_ge(*h_high_in.nth(l, KC + c + 1))
                    last = v.tensor_tensor(h_low[:, c], h[:, c], h_high[:, c].bitcast(F32), ALU.subtract)
                last.then_inc(h_split.sem, 1)

            def conv(l, n, dst, w, bias):
                dve.wait_ge(*dense_out.nth(l, n + 1))
                st = stage[:, n % 2]
                i = n % 6
                if bias is None:
                    link(v.tensor_scalar(dst, st[:, 1:1 + CV], w[:, 3 * i + 1:3 * i + 2], None, ALU.mult))
                else:
                    link(v.tensor_scalar(dst, st[:, 1:1 + CV], w[:, 3 * i + 1:3 * i + 2], bias[:, i:i + 1],
                                         ALU.mult, ALU.add))
                link(v.scalar_tensor_tensor(out=dst, in0=st[:, 0:CV], scalar=w[:, 3 * i:3 * i + 1], in1=dst,
                                            op0=ALU.mult, op1=ALU.add))
                v.scalar_tensor_tensor(out=dst, in0=st[:, 2:2 + CV], scalar=w[:, 3 * i + 2:3 * i + 3], in1=dst,
                                       op0=ALU.mult, op1=ALU.add).then_inc(conv_out.sem, 1)

            def sin_arg(l, n, src, bias, r):
                dve.wait_ge(*filt_ps.nth(l, n))
                link(v.tensor_scalar(sarg[r], src, bias, p_("hfr", r), ALU.add, ALU.mult))
                link(v.tensor_scalar(sn[r], sarg[r], 1 / (2 * math.pi), ROUND, ALU.mult, ALU.add))
                link(v.tensor_scalar(sn[r], sn[r], ROUND, None, ALU.subtract))
                link(v.scalar_tensor_tensor(out=sarg[r], in0=sn[r], scalar=-TWO_PI_HI, in1=sarg[r], op0=ALU.mult,
                                            op1=ALU.add))
                link(v.scalar_tensor_tensor(out=sarg[r], in0=sn[r], scalar=-TWO_PI_LO, in1=sarg[r], op0=ALU.mult,
                                            op1=ALU.add))
                pi = float(np.nextafter(np.float32(math.pi), np.float32(0)))
                v.tensor_scalar(sarg[r], sarg[r], pi, -pi, ALU.min, ALU.max).then_inc(filt_arg.sem, 1)

            def hyena(l):
                w, bias = p_("hcw"), p_("hcb")
                for n, dst in enumerate((hx0[:, 0], hx0[:, 1], hx1[:, 0], hx1[:, 1], hv[:, 0], hv[:, 1])):
                    conv(l, n, dst, w, bias)
                dve.wait_ge(*conv_out.nth(l, 6))
                v.tensor_tensor(hv, hv, hx1, ALU.mult).then_inc(hv_ready.sem, 1)
                r = slice(0, 64)
                flat = psA[0:64, 2:4, :].rearrange("p b n -> p (b n)")[:, 0:T]
                dve.wait_ge(*dft_in.nth(l, 1))
                sin_arg(l, 1, flat, p_("hb1", r), r)
                sin_arg(l, 2, flat, p_("hb2", r), r)
                for t in range(NT):
                    dve.wait_ge(*filt_ps.nth(l, 3 + t))
                    link(v.tensor_tensor(hprod[:, t % 2], psA[:, t % 2, :], win[:, t], ALU.mult))
                    f, b = hprod[:, t % 2, 0:256], hprod[:, t % 2, 256:512]
                    v.tensor_tensor(filt[:, t, 0], f, b, ALU.add)
                    v.tensor_tensor(filt[:, t, 1], b, f, ALU.subtract).then_inc(filt_out.sem, 1)
                dve.wait_ge(*nyq_ps.nth(l, 1))
                for s in range(2):
                    v_ = hmul[0:1, s * 256:(s + 1) * 256]
                    link(v.tensor_scalar(v_, psA[0:1, 2 + s, 0:256], 1.0 / (2 * (LAT, CTX)[s]), None, ALU.mult))
                    last = v.tensor_tensor(hnyq[0:1, s], psA[0:1, 2 + s, 256:512], v_, ALU.mult)
                last.then_inc(nyq_ready.sem, 1)
                for f in range(NT):
                    dve.wait_ge(*vspec_ps.nth(l, f + 1))
                    src = psA[:, f % 2, :].rearrange("p (c n) -> p c n", c=2)
                    pr = hprod.rearrange("p a (c n) -> p a c n", c=2)
                    v.tensor_tensor(pr[:, 0], src, hspec[:, f, 0:2], ALU.mult)
                    link(v.tensor_tensor(pr[:, 1], src, hspec[:, f, 1:3], ALU.mult))
                    v.tensor_tensor(yspec[:, f, 0], pr[:, 0, 0], pr[:, 0, 1], ALU.add)
                    ins_ = v.tensor_tensor(yspec[:, f, 1], pr[:, 1, 1], pr[:, 1, 0], ALU.subtract)
                    ins_.then_inc(yspec_ready.sem, 1)
                    dve.wait_ge(*yspec_ready.nth(l, f + 1))
                for c in range(2):
                    dve.wait_ge(*hy_ps.nth(l, c + 1))
                    for (p, q), o in zip(SEGS, (0, 2)):
                        link(v.scalar_tensor_tensor(out=bout[:, 2, c, p:q], in0=hv[:, c, p + o:q + o],
                                                    scalar=p_("hyd")[:, c:c + 1], in1=psD[:, c, p:q],
                                                    op0=ALU.mult, op1=ALU.add))
                        last = v.tensor_tensor(bout[:, 2, c, p:q], bout[:, 2, c, p:q], hx0[:, c, p + o:q + o], ALU.mult)
                last.then_inc(hy_done.sem, 1)

            def silu(l, c):
                dve.wait_ge(*g_tanh.nth(l, c + 1))
                v.scalar_tensor_tensor(out=qkv[:, c], in0=th[:, c % 2], scalar=1.0, in1=qkv[:, c], op0=ALU.add,
                                       op1=ALU.mult).then_inc(g_silu.sem, 1)

            def gdn(l):
                dve.wait_ge(*hy_done.nth(l, 1))
                for n in range(6, 12):
                    conv(l, n, qkv[:, n - 6], p_("gcw"), None)
                    if n > 6:
                        silu(l, n - 7)
                silu(l, 5)
                for c in range(2):
                    dve.wait_ge(*g_tanh.nth(l, 7 + c))
                    v.scalar_tensor_tensor(out=gz[:, c], in0=th[:, c, 0:T], scalar=1.0, in1=gz[:, c], op0=ALU.add,
                                           op1=ALU.mult).then_inc(g_silu.sem, 1)
                dve.wait_ge(*ab_ps.nth(l, 1))
                src = psA[:, 0, 0:NT * 16].rearrange("p (t d c) -> p t d c", t=NT, d=2)
                v.tensor_copy(ab[:, :, 0], src[:, :, 0])
                for s in range(5):
                    last = v.tensor_copy(ab[:, s, 1], src[:, 3 - s if s < 4 else 4, 1])
                link(last)
                f8 = lambda n: small[n].rearrange("p s d h -> p (s d h)")
                dtb = p_("dtb").rearrange("p (d h) -> p d h", d=2).unsqueeze(1).to_broadcast([P, 5, 2, 4])
                v.tensor_tensor(small["u"], ab[:, :, :, 0:4], dtb, ALU.add).then_inc(ab_in.sem, 1)
                dve.wait_ge(*ab_e.nth(l, 1))
                link(v.tensor_scalar(f8("w"), f8("e"), 1.0, None, ALU.add))
                v.tensor_scalar(f8("beta"), f8("z0"), 0.5, 0.5, ALU.mult, ALU.add).then_inc(ab_w.sem, 1)
                link(v.tensor_scalar(f8("d"), f8("w"), 1.0, None, ALU.subtract))
                dve.wait_ge(*ab_ln.nth(l, 1))
                link(v.tensor_scalar(f8("nbeg"), f8("d"), 0.0, None, ALU.is_equal))
                v.tensor_tensor(f8("ln"), f8("ln"), f8("nbeg"), ALU.add)
                link(v.tensor_tensor(f8("d"), f8("d"), f8("nbeg"), ALU.add))
                link(v.reciprocal(f8("d"), f8("d")))
                link(v.tensor_tensor(f8("ln"), f8("ln"), f8("d"), ALU.mult))
                link(v.tensor_tensor(f8("ln"), f8("ln"), f8("e"), ALU.mult))
                link(v.scalar_tensor_tensor(out=f8("g"), in0=f8("u"), scalar=0.0, in1=f8("ln"), op0=ALU.max,
                                            op1=ALU.add))
                link(v.tensor_scalar(f8("g"), f8("g"), -1.0, None, ALU.mult))
                ea = expa.rearrange("p (d h) -> p d h", d=2).unsqueeze(1).to_broadcast([P, 5, 2, 4])
                v.tensor_tensor(small["g"], small["g"], ea, ALU.mult).then_inc(g_ready.sem, 1)
                dve.wait_ge(*cum_ps.nth(l, 1))
                for d in range(2):
                    last = v.tensor_copy(small["gcol"][:, :, d, :],
                                         psA[:, 1, d * 20:(d + 1) * 20].rearrange("p (s h) -> p s h", s=5))
                link(last)
                v.tensor_copy(f8("tot"), psA[:, 1, 40:80])
                v.tensor_tensor(f8("es"), psA[:, 1, 40:80], f8("gcol"), ALU.subtract).then_inc(cum_in.sem, 1)
                v.memset(oT, 0.0)
                v.memset(state[:, 1], 0.0)
                v.tensor_copy(state[:, 0].rearrange("p d q v -> p (d q v)"), p_("s0"))
                dve.wait_ge(*cum_exp.nth(l, 1))
                v.tensor_tensor(f8("nbeg"), f8("beta"), f8("eg"), ALU.mult).then_inc(steps_in.sem, 1)
                dve.wait_ge(*qk_rs.nth(l, 1))
                v.scalar_tensor_tensor(out=qkv[:, 0:2], in0=qkv[:, 0:2], scalar=0.125, in1=rn[:, 0:2], op0=ALU.mult,
                                       op1=ALU.mult)
                v.tensor_tensor(qkv[:, 2:4], qkv[:, 2:4], rn[:, 2:4], ALU.mult).then_inc(qk_norm.sem, 1)
                masks = c_("lvl").rearrange("p (k d j) -> p k d j", k=7, d=2)
                ident4 = c_("ident").unsqueeze(1).unsqueeze(1).to_broadcast([P, 2, 4, P])

                def mask(k):
                    return masks[:, k].unsqueeze(2).to_broadcast([P, 2, 4, P])

                for s in range(5):
                    tiles = (s, 3 - s) if s < 4 else (4, 4)
                    seq = 0 if s < 4 else 1
                    dve.wait_ge(*gram_ps.nth(l, s + 1))
                    for d in range(2):
                        last = v.tensor_tensor(earg[:, d], psA[:, d, :].rearrange("p (h j) -> p h j", h=H),
                                               small["gcol"][:, s, d].unsqueeze(2).to_broadcast([P, H, P]),
                                               ALU.subtract)
                    last.then_inc(decay_arg.sem, 1)
                    dve.wait_ge(*decay_ready.nth(l, 2 * s + 2))
                    for d in range(2):
                        for hh in range(H):
                            q4 = d * 2 + hh // 2
                            last = v.scalar_tensor_tensor(out=lmat[:, d, hh],
                                                          in0=psA[:, 2 + hh % 2, q4 * P:(q4 + 1) * P],
                                                          scalar=small["beta"][:, s, d, hh:hh + 1],
                                                          in1=decay_n[:, d, hh], op0=ALU.mult, op1=ALU.mult)
                    last.then_inc(l_ready.sem, 1)
                    dve.wait_ge(*l_ready.nth(l, s + 1))
                    link(v.tensor_tensor(wm, lmat, mask(0), ALU.mult))
                    link(v.tensor_tensor(xi, ident4, wm, ALU.subtract))
                    dve.wait_ge(*lt_ready.nth(l, s + 1))
                    for d in range(2):
                        last = v.tensor_tensor(wm[:, d], lmat_t[:, d],
                                               masks[:, 0, 1 - d].unsqueeze(1).to_broadcast([P, 4, P]), ALU.mult)
                    link(last)
                    dve.wait_ge(*at_ps.nth(l, s + 1))
                    for r in range(2):
                        dt_ = decay_t.rearrange("p d (q r) j -> p d q r j", r=2)[:, :, :, r]
                        v.tensor_tensor(dt_, psA[:, 2 + r, :].rearrange("p (d q j) -> p d q j", d=2, q=2), dt_,
                                        ALU.mult)
                    v.tensor_tensor(xit, ident4, wm, ALU.subtract).then_inc(x_inv.sem, 1)
                    for k in range(1, 7):
                        dve.wait_ge(*w_ps.nth(l, s * 6 + k))
                        v.tensor_tensor(wm, psA[:, 0:2, :].rearrange("p d (h j) -> p d h j", h=H), mask(k), ALU.mult)\
                            .then_inc(w_ready.sem, 1)
                        dve.wait_ge(*xw_ps.nth(l, s * 6 + k))
                        if k < 6:
                            v.tensor_tensor(xi, xi, psA[:, 0:2, :].rearrange("p d (h j) -> p d h j", h=H),
                                            ALU.subtract)
                        v.tensor_tensor(xit, xit, psA[:, 2:4, :].rearrange("p d (h j) -> p d h j", h=H),
                                        ALU.subtract).then_inc(x_inv.sem, 1)
                    dve.wait_ge(*ks_ps.nth(l, s + 1))
                    for r in range(2):
                        out = rhs.rearrange("p d (q r) v -> p d q r v", r=2)[:, :, :, r]
                        nb = small["nbeg"][:, s].rearrange("p d (q r) -> p d q r", r=2)[:, :, :, r]
                        last = v.tensor_tensor(out, psA[:, r, 0:256].rearrange("p (d q v) -> p d q v", d=2, q=2),
                                               nb.unsqueeze(3).to_broadcast([P, 2, 2, 64]), ALU.mult)
                    link(last)
                    dve.wait_ge(*scan_in.nth(l, s + 1))
                    v.tensor_tensor(rhs, bv, rhs, ALU.subtract).then_inc(rhs_ready.sem, 1)
                    dve.wait_ge(*o_ps.nth(l, s + 1))
                    for d in range(2):
                        o = oT[:, :, tiles[d] * P:(tiles[d] + 1) * P]
                        ins_ = v.tensor_tensor(o, o, psA[:, 3, d * 256:(d + 1) * 256].rearrange(
                            "p (q j) -> p q j", q=2), ALU.add)
                        if s == 4 and d == 0:
                            link(ins_)
                    for r in range(2):
                        lanes = slice(64 * r, 64 * r + 64)
                        et = small["etot"][lanes, s].rearrange("p d (q r) -> p d q r", r=2)[:, :, :, r]
                        last = v.tensor_tensor(state[lanes, seq], state[lanes, seq],
                                               et.unsqueeze(3).to_broadcast([64, 2, 2, 64]), ALU.mult)
                    link(last)
                    v.tensor_tensor(state[:, seq].rearrange("p d q v -> p (d q v)"),
                                    state[:, seq].rearrange("p d q v -> p (d q v)"), psA[:, 0, 0:256], ALU.add)\
                        .then_inc(scan_done.sem, 1)
                dve.wait_ge(*block_done.nth(l, B_LATE + N_LATE))
                link(v.tensor_tensor(mod[:, 16:48], psD[:, 0, 0:64].rearrange("p (m s) -> p m s", s=2),
                                     p_("bada")[:, 16:48].unsqueeze(2).to_broadcast([P, 32, 2]), ALU.add))
                v.tensor_scalar(gt_half[:], mod[:, 16:24], 0.5, None, ALU.mult)
                norm_scale(1, "nmlp").then_inc(mod_ready.sem, 1)
                link(v.tensor_scalar(gz, gz, p_("gnw"), 0.5, ALU.mult, ALU.mult))
                dve.wait_ge(*o_rs.nth(l, 1))
                link(v.tensor_tensor(osq, osq, gz, ALU.mult))
                v.tensor_tensor(bout[:, 1], oT, osq, ALU.mult).then_inc(gdn_done.sem, 1)

            def attend(l, n0, n_maps, sc, small_, probs, otok):
                x0 = 0 if n_maps == 1 else U

                def row_max(u):
                    nk = T if u % NT < NT - 1 else CTX
                    dve.wait_ge(*s_ps.nth(l, n0 + u + 1))
                    for m in range(n_maps):
                        b2 = 2 * (u % 2) if n_maps == 1 else 2 * m
                        src = psA[:, b2:b2 + 2, :].rearrange("p b n -> p (b n)")[:, 0:nk]
                        link(v.tensor_reduce(small_[:, 2 * m, u:u + 1], src, AX.X, ALU.max, negate=True))
                    for m in range(n_maps):
                        v.tensor_scalar(small_[:, 2 * m, u:u + 1], small_[:, 2 * m, u:u + 1], sc, None, ALU.mult)\
                            .then_inc(negmax.sem, 1)

                def combine(u):
                    nk = T if u % NT < NT - 1 else CTX
                    dve.wait_ge(*exps.nth(l, x0 + 2 * u + 2))
                    s1, s2, cf = (small_[:, i, u:u + 1] for i in (1, 3, 5))
                    link(v.reciprocal(cf, s2))
                    link(v.tensor_scalar(cf, cf, s1, lam_s[:, 71:72], ALU.mult, ALU.mult))
                    v.scalar_tensor_tensor(out=probs[0][:, u % 2, 0:nk], in0=probs[1][:, u % 2, 0:nk], scalar=cf,
                                           in1=probs[0][:, u % 2, 0:nk], op0=ALU.mult, op1=ALU.add)\
                        .then_inc(comb.sem, 1)

                row_max(0)
                if n_maps == 2:
                    combine(0)
                for u in range(U):
                    hh, t = divmod(u, NT)
                    if u + 1 < U:
                        row_max(u + 1)
                        if n_maps == 2:
                            combine(u + 1)
                    dve.wait_ge(*pv_ps.nth(l, n0 + u + 1))
                    link(v.reciprocal(small_[:, 1, u:u + 1], small_[:, 1, u:u + 1]))
                    v.tensor_scalar(otok[:, t, hh], psD[:, u % 2, T:T + 64], small_[:, 1, u:u + 1], None, ALU.mult)\
                        .then_inc(pv_in.sem, 1)

            def rope(dst, src, ps, c, s, tmp):
                link(v.tensor_tensor(tmp, ps, s, ALU.mult))
                link(v.tensor_tensor(dst, src, c, ALU.mult))
                return v.tensor_tensor(dst, dst, tmp, ALU.add)

            def mla(l):
                dve.wait_ge(*mla_rs.nth(l, 1))
                for c in range(2):
                    last = v.scalar_tensor_tensor(out=m_cq[:, c], in0=m_cq[:, c], scalar=p_("qn")[:, c:c + 1],
                                                  in1=m_rs[:, 0], op0=ALU.mult, op1=ALU.mult)
                last.then_inc(mla_n.sem, 1)
                dve.wait_ge(*mla_rs.nth(l, 2))
                v.tensor_copy(m_ckv[:, LAT:T], p_("ckv_c"))
                v.tensor_copy(kpe[64:96, LAT:T], p_("kpe_c", slice(64, 96)))
                for (p, q), o in zip(SEGS, (0, 128)):
                    last = v.scalar_tensor_tensor(out=m_ckv[:, p + o:q + o], in0=m_ckv[:, p + o:q + o],
                                                  scalar=p_("kvn"), in1=m_rs[:, 1, p:q], op0=ALU.mult, op1=ALU.mult)
                last.then_inc(mla_n.sem, 1)
                dve.wait_ge(*mla_n.nth(l, 2))
                cos, sin = c_("cos", slice(64, 96)), c_("sin", slice(64, 96))
                for n in range(5):
                    dve.wait_ge(*rot_ps.nth(l, n + 1))
                    dst = m_q[64:96, n, 0:LAT] if n < H else kpe[64:96, 0:LAT]
                    rope(dst, dst, psD[64:96, n % 2, 0:LAT], cos, sin, rot_s[64:96, n % H]).then_inc(rot_in.sem, 1)
                dve.wait_ge(*rot_in.nth(l, 5))
                v.tensor_copy(m_k[64:96], kpe[64:96].unsqueeze(1).to_broadcast([32, H, KEYS]))\
                    .then_inc(mla_k_rope.sem, 1)
                attend(l, 0, 1, 96 ** -0.5, att_small, (prob,), o_tok)

            def diff(l):
                dve.wait_ge(*br_done.nth(l, 1))
                dve.wait_ge(*dense_out.nth(l, N_WIN))
                pr = p_("lam").rearrange("p (i n) -> p i n", i=4)
                for i in range(2):
                    last = v.tensor_tensor(lam_s[:, 32 * i:32 * i + 32], pr[:, 2 * i], pr[:, 2 * i + 1], ALU.mult)
                link(last)
                v.tensor_reduce(lam_s[:, 64:66], lam_s[:, 0:64].rearrange("p (i n) -> p i n", i=2), AX.X, ALU.add)\
                    .then_inc(lam_sum.sem, 1)
                cos, sin = c_("cos"), c_("sin")
                for n in range(4):
                    dve.wait_ge(*d_rot_ps.nth(l, n + 1))
                    dst = (d_q if n < 2 else d_k)[:, n % 2, 0:LAT]
                    rope(dst, dst, psD[:, n % 2, 0:LAT], cos, sin, d_rot[:, n]).then_inc(d_rot_in.sem, 1)
                dve.wait_ge(*lam_exp.nth(l, 1))
                link(v.tensor_tensor(lam_s[:, 70:71], lam_s[:, 69:70], lam_s[:, 68:69], ALU.subtract))
                link(v.tensor_tensor(lam_s[:, 71:72], lam_s[:, 70:71], p_("lamc")[:, 0:1], ALU.subtract))
                attend(l, U, 2, 32 ** -0.5, d_small, (d_prob, d_prob2), do_tok)
                dve.wait_ge(*pv_in.nth(l, 2 * U))
                link(v.tensor_tensor(do_sq, do_tok, do_tok, ALU.mult))
                v.tensor_reduce(d_small[:, 4], do_sq.rearrange("p t h v -> p (t h) v"), AX.X, ALU.add)\
                    .then_inc(do_sum.sem, 1)
                dve.wait_ge(*do_rs.nth(l, 1))
                link(v.tensor_scalar(d_small[:, 4], d_small[:, 4], p_("lamc")[:, 1:2], None, ALU.mult))
                o = do_tok.rearrange("p t h v -> p (t h) v")
                link(v.tensor_tensor(o, o, d_small[:, 4].unsqueeze(2).to_broadcast([P, U, 64]), ALU.mult))
                v.tensor_tensor(o, o, p_("danw").unsqueeze(1).to_broadcast([P, U, 64]), ALU.mult)\
                    .then_inc(do_normed.sem, 1)

            def add_residual(dst, b, gate):
                for half, s, p, q in ((0, 0, 0, HALF), (1, 0, HALF, LAT), (1, 1, LAT, T)):
                    ps = psum_halves(b)[:, half, p - half * HALF:q - half * HALF]
                    last = v.scalar_tensor_tensor(out=dst[:, p:q], in0=ps, scalar=gate[:, s:s + 1], in1=dst[:, p:q],
                                                  op0=ALU.mult, op1=ALU.add)
                return last

            def merge(l):
                dve.wait_ge(*br_done.nth(l, 2))
                for b in range(2):
                    v.memset(lam_s[:, b:b + 1], 0.0).then_inc(proj_used.sem, 1)
                with dve.Fori(0, KC) as d:
                    for n in range(4):
                        dve.wait_ge(gate_act.sem, l * N_GATE + d * 4 + (n + 1))
                        if n > 1:
                            dve.wait_ge(merged_add.sem, l * 24 + d * 3 + (n - 1))
                        ps = psA[:, 2 * (n % 2):2 * (n % 2) + 2, :].rearrange("p b n -> p (b n)")[:, 0:T]
                        v.scalar_tensor_tensor(out=md if n == 0 else mt, in0=tg[:, n % 2], scalar=1.0, in1=ps,
                                               op0=ALU.add, op1=ALU.mult).then_inc(proj_used.sem, 1)
                        if n:
                            dve.wait_ge(proj_used.sem, l * (N_GATE + 2) + d * 4 + (2 + n + 1))
                            v.tensor_tensor(md, md, mt, ALU.add).then_inc(merged_add.sem, 1)
                    dve.wait_ge(merged_add.sem, l * 24 + d * 3 + 3)
                    zh, zl = (z[:, bass.ds(d, 1), :].rearrange("p o t -> p (o t)") for z in (z_high, z_low))
                    v.tensor_copy(zh, md).then_inc(merged_high.sem, 1)
                    dve.wait_ge(merged_high.sem, l * KC + d + 1)
                    v.tensor_tensor(zl, md, zh.bitcast(F32), ALU.subtract).then_inc(merged_ready.sem, 1)
                    dve.wait_ge(merged_ready.sem, l * KC + d + 1)

            def out_proj(l):
                for m in range(KC):
                    dve.wait_ge(*block_done.nth(l, B_OUT + m + 1))
                    add_residual(x[:, m], m % 2, gt_half[:, m]).then_inc(residual.sem, 1)

            def mlp(l):
                first = RING + N_EARLY + B_MLP + RING + KC
                with dve.Fori(0, GROUPS) as g:
                    for j in range(KC):
                        dve.wait_ge(hid_square.sem, l * 32 + g * 8 + (j + 1))
                        v.tensor_copy(z_high[:, j], hid_sq[:, j % 2]).then_inc(hid_high.sem, 1)
                        dve.wait_ge(hid_high.sem, l * 32 + g * 8 + (j + 1))
                        v.tensor_tensor(z_low[:, j], hid_sq[:, j % 2], z_high[:, j].bitcast(F32), ALU.subtract)\
                            .then_inc(hid_ready.sem, 1)
                    for m in range(KC):
                        dve.wait_ge(block_done.sem, l * N_BLOCKS + g * N_GROUP + (first + m + 1))
                        dve.wait_ge(residual.sem, l * 40 + g * 8 + (1 + m + 1))
                        add_residual(x[:, m], m % 2, mod[:, 40 + m]).then_inc(residual.sem, 1)

            dve.wait_ge(const_in.sem, 16)
            dve.wait_ge(x_in.sem, 16)
            v.memset(stage[:], 0.0)
            dve.wait_ge(cond_tanh.sem, 1)
            v.scalar_tensor_tensor(out=cond_t[:], in0=cond_t[:], scalar=1.0, in1=cond[:], op0=ALU.add, op1=ALU.mult)\
                .then_inc(cond_sum.sem, 1)
            dve.wait_ge(cond_sum.sem, 1)
            v.tensor_scalar(cond[:], cond_t[:], 0.5, None, ALU.mult).then_inc(residual.sem, 1)
            with dve.Fori(0, DEPTH) as l:
                chain.l, chain.n = l, 0
                dve.wait_ge(*residual.nth(l, 0))
                dve.wait_ge(*params_in.nth(l, 1))
                dve.wait_ge(*block_done.nth(l, 0))
                link(v.tensor_tensor(mod[:, 0:16], psA[:, 0, 0:32].rearrange("p (m s) -> p m s", s=2),
                                     p_("bada")[:, 0:16].unsqueeze(2).to_broadcast([P, 16, 2]), ALU.add))
                norm_scale(0, "nmix").then_inc(mod_ready.sem, 1)
                norm(l, 0)
                hyena(l)
                gdn(l)
                mla(l)
                diff(l)
                merge(l)
                out_proj(l)
                norm(l, 1)
                split_h(l)
                mlp(l)
                n_links = chain.n
            assert n_links == links[0], ("DVE_LINKS", n_links)
            norm(DEPTH, 0)


SPEC = {"const": (P, CON_W), "x": (P, KC, T), "cond": (P, KC, 2), "w_early": (DEPTH, N_EARLY, P, KC * P), "w_late": (DEPTH, N_LATE, P, KC * P),
        "w_in": (DEPTH, N_WIN, P, KC * P), "w_gate": (DEPTH, N_GATE, P, 10 * P), "w_out": (DEPTH, N_OUT, P, KC * P),
        "w_mlp": (DEPTH, GROUPS * 2 * KC, P, KC * P), "par": (DEPTH, P, PAR_W), "dft": (P, DFT_W)}
OUTS = {"y": (P, KC, T), "state": (DEPTH, P, 256), "ckv": (DEPTH, P, CTX), "kpe": (DEPTH, 32, CTX),
        "dk": (DEPTH, P, 2, CTX), "dv": (DEPTH, P, 256)}


def constants():
    con = np.zeros((P, CON_W), np.float32)

    def put(dst, table, name, value, rows=slice(0, P)):
        a, w = table[name]
        value = np.asarray(value, np.float64)
        dst[rows, a:a + w] = value.reshape(value.shape[0], w) if value.ndim > 1 else value

    i, j = np.meshgrid(np.arange(P), np.arange(P), indexing="ij")
    put(con, CON, "ident", i == j)
    put(con, CON, "ones", np.ones((P, P)))
    put(con, CON, "blk", i // 64 == j // 64)
    put(con, CON, "tri", np.stack([i <= j, i >= j], 1))
    put(con, CON, "maskt", np.stack([np.where(j >= i, 0.0, -1e30), np.where(j <= i, 0.0, -1e30)], 1))
    put(con, CON, "maskn", np.stack([np.where(j < i, 0.0, 1e30), np.where(j > i, 0.0, 1e30)], 1))
    lv = []
    for k in range(7):
        m = (i >> (k + 1) == j >> (k + 1)) & ((i >> k) & 1 == 1) & ((j >> k) & 1 == 0)
        lv.append(np.stack([m, m.T], 1))
    put(con, CON, "lvl", np.stack(lv, 1))
    put(con, CON, "rot", i == np.where(j % 16 < 8, j + 8, j - 8))
    pos = np.arange(LAT)
    inv = 10000.0 ** (-(np.arange(P) % 8) / 8.0)
    ang = np.where((np.arange(P) % 32 < 16)[:, None], pos // GRID_W, pos % GRID_W) * inv[:, None]
    put(con, CON, "cos", np.cos(ang))
    put(con, CON, "sin", np.sin(ang) * np.where(np.arange(P) % 16 < 8, -1.0, 1.0)[:, None])
    wf = np.zeros((P, 5))
    wf[:, 0:4], wf[:, 4] = 1.0 / LAT, 1.0 / CTX
    wf[0, 0], wf[0, 4] = 0.5 / LAT, 0.5 / CTX
    put(con, CON, "wf", wf)
    put(con, CON, "alt", (1.0 - 2.0 * (np.arange(P) % 2))[:, None])
    put(con, CON, "altrow", (1.0 - 2.0 * (np.arange(LAT) % 2))[None], slice(0, 1))
    put(con, CON, "eps", np.full((P, 1), EPS))
    put(con, CON, "eps4", np.full((P, 1), 4 * EPS))

    dft = np.zeros((P, DFT_W), np.float32)
    n = np.arange(LAT)
    a = 2 * np.pi * ((n[:, None] * n[None]) % (2 * LAT)) / (2 * LAT)
    put(dft, DFT, "cs", np.stack([np.cos(a), np.sin(a)], 1).reshape(4, P, 2, LAT).transpose(1, 0, 2, 3))
    n = np.arange(CTX)
    a = 2 * np.pi * ((n[:, None] * n[None]) % (2 * CTX)) / (2 * CTX)
    put(dft, DFT, "csp", np.stack([np.cos(a), np.sin(a)], 1))
    deltas = np.abs(np.linspace(math.log(1e-2) / 1.5, math.log(1e-2) / 0.3, 256))
    wins, zs = [], []
    for seq in (LAT, CTX):
        pos = np.arange(seq)
        t = pos / max(seq - 1, 1)
        w = np.exp(-t[:, None] * deltas)
        wb = w.copy()
        wb[0] = 0.0
        wins.append(np.concatenate([w, wb], 1).reshape(seq // P, P, 512))
        ang = (2.0 * np.pi * pos / seq)[:, None] * np.linspace(1e-4, BANDS - 1, BANDS)
        zs.append(np.concatenate([t[:, None], np.cos(ang), -np.sin(ang)], 1))
    put(dft, DFT, "win", np.concatenate(wins, 0).transpose(1, 0, 2))
    put(dft, DFT, "z", np.concatenate(zs, 0).T, slice(0, 1 + 2 * BANDS))
    return con, dft


def blocks(w):
    d, k, m = w.shape
    return w.reshape(d, k // P, P, m // P, P).transpose(0, 3, 2, 1, 4)


def lay_out(inp):
    f = {k: np.asarray(v) for k, v in inp.items()}
    con, dft = constants()
    a, w = CON["fin"]
    con[:, a:a + w] = f["final_norm_w"].reshape(KC, P).T
    tok = np.concatenate([f["x_sample"][0], f["x_prompt"][0]], 0)
    xs = tok.T.reshape(KC, P, T).transpose(1, 0, 2)
    cond = np.stack([f["c"][0], f["c_ctx"]], 1).reshape(KC, P, 2).transpose(1, 0, 2)
    wi = f["w_in"]
    cols = lambda a, b: wi[:, :, a:b]
    kpe_cols = np.zeros((DEPTH, D, P), np.float32)
    kpe_cols[:, :, 64:96] = cols(384, 416)
    win_cols = np.concatenate([cols(1456, 2224), cols(416, 1440), cols(0, 384), kpe_cols, cols(2224, 2992)], 2)
    gates = wi[:, :, 2992:].reshape(DEPTH, D, 4, KC, P).transpose(0, 1, 3, 2, 4).reshape(DEPTH, D, N_GATE * P)
    wg = blocks(gates)
    wb = f["w_branch"].reshape(DEPTH, 4, 2, P, KC, P).transpose(0, 4, 1, 3, 2, 5).reshape(DEPTH, N_GATE, P, 2, P)
    w_gate = np.concatenate([wg, wb], 3)
    w1 = blocks(f["mlp_w1"]).reshape(DEPTH, 4, KC, P, KC, P)
    w2 = f["mlp_w2"].reshape(DEPTH, 4, KC, P, KC, P).transpose(0, 1, 4, 3, 2, 5)
    w_mlp = np.concatenate([w1, w2], 2)
    par = np.zeros((DEPTH, P, PAR_W), np.float32)

    def put(name, value, rows=slice(0, P)):
        a, w = PAR[name]
        value = np.asarray(value)
        par[:, rows, a:a + w] = value.reshape(DEPTH, value.shape[1], w)

    def feat(v, n):
        return v.reshape(DEPTH, n, P).transpose(0, 2, 1)

    def everywhere(v):
        return np.broadcast_to(v[:, None], (DEPTH, P, v.shape[-1]))

    ab = wi[:, :, 1440:1456].reshape(DEPTH, KC, P, 2, 2, 4).transpose(0, 2, 1, 4, 3, 5)
    put("wab", ab.reshape(DEPTH, P, KC * 16))
    put("uq", f["mla_w_uq"].reshape(DEPTH, 2, P, 384).transpose(0, 2, 1, 3))
    put("ukv", f["mla_w_ukv"])
    put("w1", f["hy_f_w1"], slice(0, 33))
    put("w2", f["hy_f_w2"], slice(0, 64))
    put("w3", f["hy_f_w3"], slice(0, 64))
    put("ckv_c", f["cache_mla_ckv"][0].transpose(0, 2, 1))
    put("kpe_c", f["cache_mla_kpe"][0].transpose(0, 2, 1), slice(64, 96))
    put("dk_c", f["cache_diff_k"][0].reshape(DEPTH, P, 256).transpose(0, 2, 1).reshape(DEPTH, 2, P, P)
        .transpose(0, 2, 1, 3))
    put("dv_c", f["cache_diff_v"][0].reshape(DEPTH, P, 256))
    put("s0", f["state_gdn"][0].reshape(DEPTH, 2, 2, 2, 64, 64).transpose(0, 3, 4, 1, 2, 5).reshape(DEPTH, P, 256))
    put("lam", everywhere(np.concatenate([f["da_lq1"], f["da_lk1"], f["da_lq2"], f["da_lk2"]], 1)))
    put("danw", everywhere(f["da_norm_w"]))
    put("alog", everywhere(f["gdn_a_log"].reshape(DEPTH, 8)))
    put("dtb", everywhere(f["gdn_dt_bias"].reshape(DEPTH, 8)))
    put("bada", feat(f["b_ada"], 48))
    put("nmix", feat(f["norm_mix_w"], 8))
    put("nmlp", feat(f["norm_mlp_w"], 8))
    put("qn", feat(f["mla_q_norm_w"], 2))
    put("kvn", feat(f["mla_kv_norm_w"], 1))
    put("gcw", f["gdn_conv_w"].reshape(DEPTH, 3, 6, P).transpose(0, 3, 2, 1))
    put("gnw", np.concatenate([f["gdn_norm_w"]] * 2, 1)[:, :, None])
    put("hcw", f["hy_conv_w"].reshape(DEPTH, 3, 6, P).transpose(0, 3, 2, 1))
    put("hcb", feat(f["hy_conv_b"], 6))
    put("hb1", f["hy_f_b1"][:, :, None], slice(0, 64))
    put("hb2", f["hy_f_b2"][:, :, None], slice(0, 64))
    put("hfr", f["hy_f_freq"][:, :, None], slice(0, 64))
    put("hyd", feat(f["hy_d"], 2))
    init = [0.8 - 0.6 * math.exp(-0.3 * l) for l in range(DEPTH)]
    put("lamc", np.broadcast_to(np.array([[[v, 1.0 - v]] for v in init], np.float32), (DEPTH, P, 2)))
    w_ada = blocks(f["w_ada"])
    early = np.roll(w_ada[:, :N_EARLY], -1, axis=0)
    arrays = {"const": con, "x": xs, "cond": cond, "w_early": early, "w_late": w_ada[:, N_EARLY:], "w_in": blocks(win_cols),
              "w_gate": w_gate, "w_out": blocks(f["w_out"]), "w_mlp": w_mlp, "par": par, "dft": dft}
    return {k: np.ascontiguousarray(v).reshape(SPEC[k]) for k, v in arrays.items()}


def build(nc):
    ins = {k: nc.dram_tensor(f"in_{k}", s, F32, kind="ExternalInput").ap() for k, s in SPEC.items()}
    outs = {k: nc.dram_tensor(f"out_{k}", s, F32, kind="ExternalOutput").ap() for k, s in OUTS.items()}
    trunk(nc, ins, outs, (DVE_LINKS, ACT_LINKS))


def kernel(**inputs):
    import concourse.bacc as bacc
    from concourse.bass_utils import run_bass_kernel_spmd

    nc = bacc.Bacc("TRN2", target_bir_lowering=False, num_devices=1)
    arrays = lay_out(inputs)
    build(nc)
    r = run_bass_kernel_spmd(nc, [{f"in_{k}": v for k, v in arrays.items()}], core_ids=[0]).results[0]
    y = r["out_y"].transpose(1, 0, 2).reshape(D, T).T
    dk = r["out_dk"].transpose(0, 2, 1, 3).reshape(DEPTH, 256, CTX).transpose(0, 2, 1)
    st = r["out_state"].reshape(DEPTH, 2, 64, 2, 2, 64).transpose(0, 3, 4, 1, 2, 5)
    c = np.ascontiguousarray
    return (c(y[LAT:])[None], c(y[:LAT])[None], c(r["out_ckv"].transpose(0, 2, 1))[None],
            c(r["out_kpe"].transpose(0, 2, 1))[None], c(dk.reshape(1, DEPTH, CTX, H, 2, 32)),
            c(r["out_dv"].reshape(1, DEPTH, CTX, H, 64)), c(st.reshape(1, DEPTH, 2, H, 64, 64)))
```

```python
import math
from contextlib import ExitStack

import numpy as np
import concourse.bass as bass
from concourse import mybir

F32 = mybir.dt.float32
F32R = mybir.dt.float32r
ALU = mybir.AluOpType
ACT = mybir.ActivationFunctionType
AX = mybir.AxisListType

P = 128
D = 1024
KC = D // P
DEPTH = 2
LAT, CTX = 512, 128
T = LAT + CTX
NT = T // P
SEGS = ((0, LAT), (LAT, T))
HALF = T // 2
KEYS = LAT + 128 + CTX
H = 4
GRID_W = 64
EPS = 1e-6
BANDS = 16
RING = 4

N_EARLY, N_LATE = 16, 32
N_ADA = N_EARLY + N_LATE
N_WIN, N_GATE, N_OUT = 24, 32, 8
GROUPS = 4
N_GROUP = 2 * KC + N_EARLY // GROUPS
B_GATE = N_WIN
B_OUT = B_GATE + N_GATE + N_LATE
B_MLP = B_OUT + N_OUT
N_BLOCKS = B_MLP + GROUPS * N_GROUP
PER_SLOT = N_BLOCKS // RING


def mlp_at(q):
    return B_MLP + q + (q + 2) // 4


def early_at(j):
    return B_MLP + 5 * j + 2


N_SPLIT = N_GATE + N_OUT + GROUPS * 2 * KC


CV = LAT + CTX + 2
PAD = CV + 2


def tok_cols(t):
    return t * P if t < NT - 1 else LAT + 2


def layout(fields):
    at, out = 0, {}
    for name, width in fields:
        out[name] = (at, width)
        at += width
    return out, at


PAR, PAR_W = layout([
    ("wab", KC * 16), ("uq", 2 * 384), ("ukv", 512), ("w1", 64), ("w2", 64), ("w3", 512),
    ("ckv_c", 128), ("kpe_c", 128), ("dk_c", 256), ("dv_c", 256), ("s0", 256),
    ("lam", 128), ("danw", 64), ("alog", 8), ("dtb", 8), ("bada", 48), ("nmix", 8), ("nmlp", 8),
    ("qn", 2), ("kvn", 1), ("gcw", 18), ("gnw", 1), ("hcw", 18), ("hcb", 6), ("hb1", 1), ("hb2", 1),
    ("hfr", 1), ("hyd", 2), ("lamc", 2)])

CON, CON_W = layout([
    ("ident", 128), ("ones", 128), ("blk", 128), ("tri", 256), ("maskt", 256), ("maskn", 256),
    ("lvl", 7 * 256), ("rot", 128), ("cos", LAT), ("sin", LAT), ("wf", 5), ("alt", 1), ("altrow", LAT),
    ("eps", 1), ("eps4", 1), ("fin", 8)])

DFT, DFT_W = layout([("cs", 4 * 2 * LAT), ("csp", 2 * CTX), ("win", NT * 512), ("z", T)])

TWO_PI_HI = 6.28125
TWO_PI_LO = 2 * math.pi - TWO_PI_HI
ROUND = 12582912.0

DVE_LINKS = 255
ACT_LINKS = 7


class Signal:

    def __init__(self, sem, per_layer, base=0, unit=1):
        self.sem, self.per_layer, self.base, self.unit = sem, per_layer, base, unit

    def nth(self, l, n):
        return self.sem, (l * self.per_layer + (self.base + n)) * self.unit


class Chain:

    def __init__(self, eng, sem, per_layer):
        self.eng, self.sem, self.per_layer, self.n, self.l = eng, sem, per_layer, 0, 0

    def link(self, ins):
        ins.then_inc(self.sem, 1)
        self.n += 1
        self.eng.wait_ge(self.sem, self.l * self.per_layer + self.n)


def trunk(nc, ins, outs, links):
    ctx = ExitStack()
    with ctx:
        def sb(name, shape):
            return ctx.enter_context(nc.sbuf_tensor(name, shape, F32))

        def signal(name, per_layer, base=0, unit=1):
            return Signal(ctx.enter_context(nc.semaphore(name)), per_layer, base, unit)

        x = sb("x_res", [P, KC, T])
        ring = sb("w_ring", [P, RING, 10, P])
        par = sb("par", [P, PAR_W])
        con = sb("con", [P, CON_W])
        bout = sb("bout", [P, 4, 2, T])
        stage = sb("stage", [P, 2, PAD])
        mod = sb("mod", [P, 48, 2])
        mod_a = sb("mod_a", [P, 2, KC, 2])
        weighed = sb("weighed", [P, 2, 2, P])
        gt_half = sb("gt_half", [P, KC, 2])
        cond = sb("cond_s", [P, KC, 2])
        cond_t = sb("cond_t", [P, KC, 2])
        rs = sb("rs", [P, T])
        lam_s = sb("lam_s", [P, 72])
        ARENA = 22016
        with ExitStack() as mixer:
            h = mixer.enter_context(nc.sbuf_tensor("h_norm", [P, KC, T], F32))
            arena = mixer.enter_context(nc.sbuf_tensor("arena", [P, ARENA], F32))

        def sbr(name, shape):
            return ctx.enter_context(nc.sbuf_tensor(name, shape, F32R))

        FLOW = ARENA - 3 * KC * T - 4 * KC * P
        h_low = sbr("h_low", [P, KC, T])
        z_high = sbr("z_high", [P, KC, T])
        z_low = sbr("z_low", [P, KC, T])
        flow = sb("flow", [P, FLOW])
        w_high = sbr("w_high", [P, 2, KC, P])
        w_low = sbr("w_low", [P, 2, KC, P])
        h_high = sbr("h_high", [P, KC, T])

        psD = ctx.enter_context(nc.psum_tensor("ps_dense", [P, 2, 1024], F32))
        psA = ctx.enter_context(nc.psum_tensor("ps_aux", [P, 4, 512], F32))

        def p_(name, rows=slice(0, P)):
            a, w = PAR[name]
            return par[rows, a:a + w]

        def c_(name, rows=slice(0, P)):
            a, w = CON[name]
            return con[rows, a:a + w]

        class Carve:
            def __init__(self, at=0):
                self.at = at

            def __call__(self, *dims, rows=P):
                n = math.prod(dims)
                a = arena[0:rows, self.at:self.at + n]
                self.at += n
                assert self.at <= ARENA, self.at
                if len(dims) == 1:
                    return a
                names = " ".join("abcd"[:len(dims)])
                return a.rearrange(f"p ({names}) -> p {names}", **dict(zip("abcd", dims)))

        cv = Carve()
        dft = cv(DFT_W)
        hx0, hx1, hv = cv(2, CV), cv(2, CV), cv(2, CV)
        hvt = cv(NT, 256)
        filt = cv(NT, 2, 256)
        hspec = cv(NT, 3, 256)
        yspec = filt
        hprod = cv(2, 512)
        hnyq = cv(2, 256)
        hmul = cv(512)
        sarg, sn, ssin = (hspec.rearrange("p a b c -> p (a b c)")[:, i * T:(i + 1) * T] for i in range(3))
        dcs = dft[:, 0:4096].rearrange("p (k c f) -> p k c f", k=4, c=2)
        dcsp = dft[:, 4096:4352].rearrange("p (c f) -> p c f", c=2)
        win = dft[:, 4352:4352 + 2560].rearrange("p (t c) -> p t c", t=NT)
        zf = dft[0:33, 4352 + 2560:4352 + 2560 + T]

        cv = Carve()
        qkv = cv(6, CV)
        gz = cv(2, T)
        th = cv(2, CV)
        ktok, vtok = cv(NT, 256), cv(NT, 256)
        small = {n: cv(5, 2, 4) for n in ("g", "beta", "gcol", "es", "eg", "etot", "nbeg", "u", "e", "w", "d", "z0",
                                          "ln", "tot")}
        ab = cv(5, 2, 8)
        expa = cv(8)
        oT = cv(2, T)
        state = cv(2, 2, 2, 64)
        at_norm = cv.at
        rn = cv(4, CV)
        osq = cv(2, T)
        cv = Carve(at_norm)
        decays_t = cv(2, 4, P), cv(2, 4, P)
        decay_n, lmat, lmat_t = cv(2, 4, P), cv(2, 4, P), cv(2, 4, P)
        xi, xit, wm = cv(2, 4, P), cv(2, 4, P), cv(2, 4, P)
        earg = th.rearrange("p c t -> p (c t)")[:, 0:1024].rearrange("p (d h j) -> p d h j", d=2, h=4)
        eq, qg = (qkv[:, 4:6, :].rearrange("p c t -> p (c t)")[:, i * 512:(i + 1) * 512]
                  .rearrange("p (d q j) -> p d q j", d=2, q=2) for i in range(2))
        bv, ks, rhs, vn = cv(2, 4, 64), cv(2, 4, 64), cv(2, 4, 64), cv(2, 4, 64)

        cv = Carve()
        m_cq, m_ckv = cv(2, T), cv(KEYS)
        m_q, m_k = cv(H, T), cv(H, KEYS)
        m_v = cv(6, 256)
        kpe = cv(KEYS)
        m_sq = cv(3, T)
        m_rs = cv(2, T)
        prob, prob_t = cv(2, T), cv(2, T)
        o_tok = cv(NT, H, 64)
        rot_s = cv(H, LAT)
        att_small = cv(4, 20)
        cv = Carve()
        d_q, d_k = cv(2, T), cv(2, KEYS)
        d_vf = cv(2, T)
        d_v = cv(6, 256)
        d_prob, d_prob2, d_prob_t = cv(2, T), cv(2, T), cv(2, T)
        do_tok = cv(NT, H, 64)
        do_sq = cv(NT, H, 64)
        d_rot = cv(4, LAT)
        d_small = cv(8, 20)
        tg = flow[:, 0:2 * T].rearrange("p (b t) -> p b t", b=2)
        hid_sq = tg
        md, mt = flow[:, 2 * T:3 * T], flow[:, 3 * T:4 * T]

        const_in = signal("const_in", 0, 1, 16)
        x_in = signal("x_in", 0, 1, 16)
        cond_in = signal("cond_in", 0, 1, 16)
        cond_tanh = signal("cond_tanh", 0, 1)
        ring_in = [signal(f"ring_in{j}", PER_SLOT, N_EARLY // RING, 16) for j in range(RING)]
        block_done = signal("block_done", N_BLOCKS, RING + N_EARLY)
        params_in = signal("params_in", 1, 0, 16)
        dft_in = signal("dft_in", 1, 0, 16)
        weighed_in = signal("weighed", N_ADA * 2 * KC, N_EARLY * 2 * KC)
        mod_ready = signal("mod_ready", 2)
        residual = signal("residual_added", 40, 1)
        x_squared = signal("x_squared", 16)
        sumsq_done = signal("sumsq_done", 2)
        rstd_ready = signal("rstd_ready", 2)
        x_scaled = signal("x_scaled", 16)
        h_ready = signal("h_ready", 16)
        dense_out = signal("dense_out", N_WIN)
        conv_out = signal("conv_out", 12)
        filt_ps = signal("filt_ps", 2 + NT)
        filt_arg = signal("filt_arg", 2)
        filt_sin = signal("filt_sin", 2)
        filt_out = signal("filt_out", NT)
        hv_ready = signal("hv_ready", 1)
        hvt_ps = signal("hvt_ps", 1)
        hvt_ready = signal("hvt_ready", 1)
        hspec_ps = signal("hspec_ps", NT)
        hspec_ready = signal("hspec_ready", NT)
        vspec_ps = signal("vspec_ps", NT)
        yspec_ready = signal("yspec_ready", NT)
        nyq_ps = signal("nyq_ps", 1)
        nyq_ready = signal("nyq_ready", 1)
        hy_ps = signal("hy_ps", 2)
        hy_done = signal("hyena_done", 1)
        g_tanh = signal("gdn_tanh", 8)
        g_silu = signal("gdn_silu", 8)
        ab_ps = signal("ab_ps", 1)
        ab_in = signal("ab_in", 1)
        ab_e = signal("ab_e", 1)
        ab_w = signal("ab_w", 1)
        ab_ln = signal("ab_ln", 1)
        g_ready = signal("g_ready", 1)
        cum_ps = signal("cum_ps", 1)
        cum_in = signal("cum_in", 1)
        cum_exp = signal("cum_exp", 1)
        steps_in = signal("step_scalars_ready", 1)
        qk_sq = signal("qk_squared", 4)
        qk_ps = signal("qk_ps", 4)
        qk_ln = signal("qk_ln", 4)
        qk_rs = signal("qk_rs", 1)
        qk_norm = signal("qk_normed", 1)
        kv_ps = signal("kv_ps", NT)
        kv_tok = signal("kv_tok", NT)
        cumrow_ps = signal("cumulative_rows_ps", 5)
        gram_ps = signal("gram_ps", 5)
        decay_arg = signal("decay_arg", 5)
        eq_ready = signal("eq_ready", 5)
        masked = signal("masked", 10)
        decay_ready = signal("decay_ready", 10)
        l_ready = signal("l_ready", 5)
        lt_ps = signal("lt_ps", 5)
        lt_ready = signal("lt_ready", 5)
        at_ps = signal("at_ps", 5)
        inv_in = signal("inverse_in", 5 * 26)
        inv_ps = signal("inverse_ps", 5 * 24)


        scan_in = signal("scan_inputs", 5)
        ks_ps = signal("ks_ps", 5)
        rhs_ready = signal("rhs_ready", 5)
        vn_ps = signal("vn_ps", 5)
        vn_ready = signal("vn_ready", 5)
        o_ps = signal("o_ps", 5)
        scan_done = signal("scan_done", 5)
        osq_ready = signal("osq_ready", 1)
        osum_ps = signal("osum_ps", 1)
        o_rs = signal("o_rs", 1)
        gdn_done = signal("gdn_done", 1)
        mla_sq = signal("mla_sq", 1)
        mla_sum = signal("mla_sum", 2)
        mla_rs = signal("mla_rs", 2)
        mla_n = signal("mla_normed", 2)
        mla_q_ps = signal("mla_q_ps", H)
        mla_q_in = signal("mla_q_in", H)
        mla_k_ps = signal("mla_k_ps", H)
        mla_k_in = signal("mla_k_in", H)
        mla_v_ps = signal("mla_v_ps", 3)
        mla_v_in = signal("mla_v_in", 3)
        rot_ps = signal("rot_ps", 5)
        rot_in = signal("rot_in", 5)
        mla_k_rope = signal("mla_k_rope", 1)
        d_rot_ps = signal("d_rot_ps", 4)
        d_rot_in = signal("d_rot_in", 4)
        dv_ps = signal("dv_ps", 3)
        dv_in = signal("dv_in", 3)
        U = NT * H
        s_ps = signal("scores_ps", 3 * U)
        negmax = signal("negmax", 3 * U)
        exps = signal("exps", 3 * U)
        comb = signal("combined", U)
        pt_ps = signal("pt_ps", 2 * U)
        pt_in = signal("pt_in", 2 * U)
        pv_ps = signal("pv_ps", 2 * U)
        pv_in = signal("pv_in", 2 * U)
        do_sum = signal("do_sum", 1)
        do_rs = signal("do_rs", 1)
        do_normed = signal("do_normed", 1)
        ot_ps = signal("ot_ps", 2)
        br_done = signal("attention_branch_done", 2)
        lam_sum = signal("lam_sum", 1)
        lam_exp = signal("lam_exp", 1)
        gate_act = signal("gate_act", N_GATE)
        proj_used = signal("proj_used", N_GATE + 2)
        merged_add = signal("merged_add", 24)
        merged_high = signal("merged_high", KC)
        merged_ready = signal("merged_ready", KC)
        w_high_in = signal("w_high_ready", N_SPLIT)
        w_low_in = signal("w_low_ready", N_SPLIT)
        h_high_in = signal("h_high_ready", 2 * KC)
        h_split = signal("h_split", 2)
        cond_sum = signal("cond_sum", 0)
        hid_relu = signal("hid_relu", 32)
        hid_square = signal("hid_square", 32)
        hid_high = signal("hid_high", 32)
        hid_ready = signal("hid_ready", 32)
        stored = signal("stored", 5, 0, 16)
        y_ready = signal("y_ready", 0)
        y_out = signal("y_out", 0)
        dve_chain = signal("dve_chain", 0)
        act_chain = signal("act_chain", 0)
        held_waits = signal("held_waits", 0)
        pool_chain = signal("pool_chain", 0)

        def halves(ap):
            return ap.rearrange("p (s n) -> p s n", s=2)

        def psum_halves(b):
            return psD[:, b, :].rearrange("p (s n) -> p s n", s=2)[:, :, 0:HALF]

        def held(eng, *event):
            eng.wait_ge(*event)
            eng.nop().then_inc(held_waits.sem, 1)

        block = ctx.enter_context(nc.Block())

        @block.sync
        def _(sp):
            sp.dma_start(con[:], ins["const"]).then_inc(const_in.sem, 16)
            sp.dma_start(x[:], ins["x"]).then_inc(x_in.sem, 16)
            sp.dma_start(cond[:], ins["cond"]).then_inc(cond_in.sem, 16)

            def load(l, place, dram, at, subs, more=0):
                sp.wait_ge(block_done.sem, l * N_BLOCKS + more + (N_EARLY + place + 1))
                src = dram[l, at].rearrange("o p (s m) -> p (o s) m", m=P)
                j = place % RING
                sp.dma_start(ring[:, j, 0:subs, :], src).then_inc(ring_in[j].sem, 16)

            def stream(l, place, first, n, dram, subs):
                with sp.Fori(0, n // RING) as i:
                    for j in range(RING):
                        load(l, place + j, dram, bass.ds(i * RING + (first + j), 1), subs, i * RING)

            with sp.Fori(0, N_EARLY // RING) as i:
                for j in range(RING):
                    sp.wait_ge(block_done.sem, i * RING + (j + 1))
                    src = ins["w_early"][DEPTH - 1, bass.ds(i * RING + j, 1)].rearrange("o p (s m) -> p (o s) m", m=P)
                    sp.dma_start(ring[:, j, 0:KC, :], src).then_inc(ring_in[j].sem, 16)
            with sp.Fori(0, DEPTH) as l:
                stream(l, 0, 0, N_WIN, ins["w_in"], KC)
                with sp.Fori(0, KC) as d:
                    for n in range(4):
                        load(l, B_GATE + 2 * n, ins["w_gate"], bass.ds(d * 4 + n, 1), 10, d * 8)
                        load(l, B_GATE + 2 * n + 1, ins["w_late"], bass.ds(d * 4 + n, 1), KC, d * 8)
                stream(l, B_OUT, 0, N_OUT, ins["w_out"], KC)
                with sp.Fori(0, GROUPS) as g:
                    for q in range(2 * KC):
                        load(l, mlp_at(q), ins["w_mlp"], bass.ds(g * (2 * KC) + q, 1), KC, g * N_GROUP)
                        if q % 4 == 1:
                            load(l, early_at(q // 4), ins["w_early"], bass.ds(g * RING + q // 4, 1), KC, g * N_GROUP)
            sp.wait_ge(y_ready.sem, KC)
            sp.dma_start(outs["y"], h[:]).then_inc(y_out.sem, 16)
            sp.wait_ge(y_out.sem, 16)

        @block.gpsimd
        def _(pool):
            g = nc.gpsimd
            with pool.Fori(0, DEPTH) as l:
                held(pool, *residual.nth(l, 0))
                pool.dma_start(par[:], ins["par"][bass.ds(l, 1)].rearrange("o p w -> p (o w)"))\
                    .then_inc(params_in.sem, 16)
                pool.dma_start(dft, ins["dft"]).then_inc(dft_in.sem, 16)
                for s in range(5):
                    tiles = (s, 3 - s) if s < 4 else (4, 4)
                    pool.wait_ge(*decay_arg.nth(l, s + 1))
                    for dst, mask in ((decays_t[s % 2], "maskt"), (decay_n, "maskn")):
                        mk = c_(mask).rearrange("p (d j) -> p d j", d=2).unsqueeze(2).to_broadcast([P, 2, 4, P])
                        g.tensor_tensor(dst, earg, mk, ALU.add).then_inc(masked.sem, 1)
                    if s == 0:
                        pool.wait_ge(*steps_in.nth(l, 1))
                        pool.wait_ge(*kv_tok.nth(l, NT))
                    else:
                        pool.wait_ge(*o_ps.nth(l, s))
                    pool.wait_ge(*eq_ready.nth(l, s + 1))
                    for d in range(2):
                        t = tiles[d]
                        vt = vtok[:, t].rearrange("p (h v) -> p h v", h=H)
                        kt = ktok[:, t].rearrange("p (h v) -> p h v", h=H)
                        g.tensor_tensor(bv[:, d], vt, small["beta"][:, s, d].unsqueeze(2).to_broadcast([P, H, 64]),
                                        ALU.mult)
                        g.tensor_tensor(ks[:, d], kt, small["es"][:, s, d].unsqueeze(2).to_broadcast([P, H, 64]),
                                        ALU.mult)
                        c0 = tok_cols(t)
                        last = g.tensor_tensor(qg[:, d], eq[:, d], qkv[:, 0:2, c0:c0 + P], ALU.mult)
                    last.then_inc(scan_in.sem, 1)
                for name, src, complete in (
                        ("state", state[:, 1].rearrange("p d q v -> p (d q v)"), scan_done.nth(l, 5)),
                        ("ckv", m_ckv[:, T:KEYS], mla_n.nth(l, 2)),
                        ("kpe", kpe[64:96, T:KEYS], mla_n.nth(l, 2)),
                        ("dk", d_k[:, :, T:KEYS], dense_out.nth(l, 22)),
                        ("dv", d_v[:, 5], dv_in.nth(l, 3))):
                    held(pool, *complete)
                    dst = outs[name][bass.ds(l, 1)]
                    dst = dst.rearrange("o p c w -> p (o c) w") if name == "dk" else dst.rearrange("o p w -> p (o w)")
                    pool.dma_start(dst, src).then_inc(stored.sem, 16)
                held(pool, *block_done.nth(l, N_WIN - 1 + 1))
                for c in range(KC):
                    g.tensor_copy(h_high[:, c], h[:, c]).then_inc(h_high_in.sem, 1)
                for c in range(KC):
                    held(pool, *h_high_in.nth(l, c + 1))
                    last = g.tensor_tensor(h_low[:, c], h[:, c], h_high[:, c].bitcast(F32), ALU.subtract)
                last.then_inc(h_split.sem, 1)
                held(pool, *stored.nth(l, 5))

                def low_part(l, n, slot, more=0):
                    pool.wait_ge(w_high_in.sem, l * N_SPLIT + more + (n + 1))
                    g.tensor_tensor(w_low[:, n % 2], ring[:, slot, 0:KC, :], w_high[:, n % 2].bitcast(F32),
                                    ALU.subtract).then_inc(w_low_in.sem, 1)

                with pool.Fori(0, KC) as d:
                    for n in range(4):
                        low_part(l, n, 2 * n % RING, d * 4)
                for m in range(N_OUT):
                    low_part(l, N_GATE + m, m % RING)
                with pool.Fori(0, GROUPS) as g_:
                    for j in range(2 * KC):
                        low_part(l, N_GATE + N_OUT + j, mlp_at(j) % RING, g_ * (2 * KC))

        @block.tensor
        def _(pe):
            mm = nc.tensor.matmul

            def dense(out, j, rhs):
                for k in range(KC):
                    for a, b in SEGS:
                        last = mm(out[:, a:b], ring[:, j, k, :], rhs[:, k, a:b], start=k == 0, stop=k == KC - 1)
                return last

            def dense_split(b, par_, x_high, x_low):
                for k in range(KC):
                    for w_, x_ in ((w_high, x_high), (w_high, x_low), (w_low, x_high)):
                        for s in range(2):
                            last = mm(psD[:, b, s * 512:s * 512 + HALF], w_[:, par_, k, :],
                                      x_[:, k, s * HALF:(s + 1) * HALF], start=k == 0 and x_ is x_high and w_ is w_high,
                                      stop=k == KC - 1 and w_ is w_low)
                last.then_inc(block_done.sem, 1)

            def landed(l, place, turns=0):
                j = place % RING
                pe.wait_ge(ring_in[j].sem, (l * PER_SLOT + turns + ((N_EARLY + place) // RING + 1)) * 16)

            def modulation(l, out, n, more=0):
                pe.wait_ge(weighed_in.sem, l * (N_ADA * 2 * KC) + more * (2 * KC) + (N_EARLY + n + 1) * 2 * KC)
                for c in range(2):
                    last = mm(out(c), weighed[:, n % 2, c, :], c_("ones")[:, 0:1], start=True, stop=True)
                last.then_inc(block_done.sem, 1)

            def norm_sum(l, which):
                for c in range(KC):
                    pe.wait_ge(*x_squared.nth(l, which * KC + c + 1))
                    for a, b in SEGS:
                        last = mm(psD[:, 0, a:b], c_("ones"), h[:, c, a:b], start=c == 0, stop=c == KC - 1)
                last.then_inc(sumsq_done.sem, 1)

            def win_block(l, n):
                j = n % RING
                landed(l, n)
                if n >= 2:
                    pe.wait_ge(*dense_out.nth(l, n - 1))
                dense(psD[:, n % 2], j, h).then_inc(block_done.sem, 1)

            for _ in range(RING):
                pe.nop().then_inc(block_done.sem, 1)
            pe.wait_ge(const_in.sem, 16)

            def hyena(l):
                pe.wait_ge(*params_in.nth(l, 1))
                pe.wait_ge(*dft_in.nth(l, 1))
                held(pe, *mod_ready.nth(l, 1))
                flat = psA[0:64, 2:4, :].rearrange("p b n -> p (b n)")
                for a, b in SEGS:
                    last = mm(flat[:, a:b], p_("w1", slice(0, 33)), zf[:, a:b], start=True, stop=True)
                last.then_inc(filt_ps.sem, 1)
                held(pe, *filt_sin.nth(l, 1))
                for a, b in SEGS:
                    last = mm(flat[:, a:b], p_("w2", slice(0, 64)), ssin[0:64, a:b], start=True, stop=True)
                last.then_inc(filt_ps.sem, 1)
                pe.wait_ge(*filt_sin.nth(l, 2))
                for t in range(NT):
                    if t >= 2:
                        pe.wait_ge(*filt_out.nth(l, t - 1))
                    mm(psA[:, t % 2, :], ssin[0:64, t * P:(t + 1) * P], p_("w3", slice(0, 64)), start=True, stop=True)\
                        .then_inc(filt_ps.sem, 1)
                pe.wait_ge(*filt_out.nth(l, NT))
                for f in range(NT):
                    if f >= 2:
                        pe.wait_ge(*hspec_ready.nth(l, f - 1))
                    for c in range(2):
                        out = psA[:, f % 2, c * 256:(c + 1) * 256]
                        if f < 4:
                            for k in range(4):
                                last = mm(out, dcs[:, k, c, f * P:(f + 1) * P], filt[:, k, c, :],
                                          start=k == 0, stop=k == 3)
                        else:
                            last = mm(out, dcsp[:, c, :], filt[:, 4, c, :], start=True, stop=True)
                    last.then_inc(hspec_ps.sem, 1)
                pe.wait_ge(*hv_ready.nth(l, 1))
                pe.wait_ge(*hspec_ready.nth(l, NT))
                for t in range(NT):
                    for c in range(2):
                        c0 = tok_cols(t)
                        last = nc.tensor.transpose(psA[:, t // 2, (t % 2) * 256 + c * P:(t % 2) * 256 + (c + 1) * P],
                                                   hv[:, c, c0:c0 + P], c_("ident"))
                last.then_inc(hvt_ps.sem, 1)
                pe.wait_ge(*hvt_ready.nth(l, 1))
                for s, tiles in enumerate((range(4), (4,))):
                    for i, src in enumerate((filt, hvt)):
                        for n, t in enumerate(tiles):
                            r = src[:, t, 0, :] if i == 0 else src[:, t, :]
                            last = mm(psA[0:1, 2 + s, i * 256:(i + 1) * 256], c_("alt"), r,
                                      start=n == 0, stop=n == len(tiles) - 1)
                last.then_inc(nyq_ps.sem, 1)
                pe.wait_ge(*nyq_ready.nth(l, 1))
                for f in range(NT):
                    if f >= 2:
                        pe.wait_ge(*yspec_ready.nth(l, f - 1))
                    for c in range(2):
                        out = psA[:, f % 2, c * 256:(c + 1) * 256]
                        if f < 4:
                            for k in range(4):
                                last = mm(out, dcs[:, k, c, f * P:(f + 1) * P], hvt[:, k, :],
                                          start=k == 0, stop=k == 3)
                        else:
                            last = mm(out, dcsp[:, c, :], hvt[:, 4, :], start=True, stop=True)
                    last.then_inc(vspec_ps.sem, 1)
                pe.wait_ge(*yspec_ready.nth(l, NT))
                for c in range(2):
                    cols = slice(c * P, (c + 1) * P)
                    for k in range(4):
                        for r in range(2):
                            mm(psD[:, c, 0:LAT], yspec[:, k, r, cols], dcs[:, k, r, :],
                               start=k == 0 and r == 0, stop=False)
                    mm(psD[:, c, 0:LAT], hnyq[0:1, 0, cols], c_("altrow", slice(0, 1)), start=False, stop=True)
                    for r in range(2):
                        mm(psD[:, c, LAT:T], yspec[:, 4, r, cols], dcsp[:, r, :], start=r == 0, stop=False)
                    mm(psD[:, c, LAT:T], hnyq[0:1, 1, cols], c_("altrow", slice(0, 1))[:, 0:CTX],
                       start=False, stop=True).then_inc(hy_ps.sem, 1)

            def gdn(l):
                for t in range(NT):
                    for k in range(KC):
                        last = mm(psA[:, 0, t * 16:(t + 1) * 16], h[:, k, t * P:(t + 1) * P],
                                  p_("wab")[:, k * 16:(k + 1) * 16], start=k == 0, stop=k == KC - 1)
                last.then_inc(ab_ps.sem, 1)
                pe.wait_ge(*g_ready.nth(l, 1))
                tri = c_("tri").rearrange("p (d j) -> p d j", d=2)
                for d in range(2):
                    mm(psA[:, 1, d * 20:(d + 1) * 20], tri[:, d], small["g"][:, :, d, :], start=True, stop=True)
                mm(psA[:, 1, 40:80], c_("ones"), small["g"].rearrange("p s d h -> p (s d h)"), start=True, stop=True)\
                    .then_inc(cum_ps.sem, 1)
                pe.wait_ge(*cum_in.nth(l, 1))
                for c in range(4):
                    pe.wait_ge(*qk_sq.nth(l, c + 1))
                    if c >= 2:
                        pe.wait_ge(*qk_ln.nth(l, c - 1))
                    out = psA[:, 2 * (c % 2):2 * (c % 2) + 2, :].rearrange("p b n -> p (b n)")
                    for a, b in ((0, 512), (512, CV)):
                        last = mm(out[:, a:b], c_("blk"), th[:, c % 2, a:b], start=True, stop=True)
                    last.then_inc(qk_ps.sem, 1)
                pe.wait_ge(*qk_norm.nth(l, 1))
                for t in range(NT):
                    if t >= 2:
                        pe.wait_ge(*kv_tok.nth(l, t - 1))
                    c0 = tok_cols(t)
                    for c in range(4):
                        last = nc.tensor.transpose(psA[:, t % 2, c * P:(c + 1) * P], qkv[:, 2 + c, c0:c0 + P],
                                                   c_("ident"))
                    last.then_inc(kv_ps.sem, 1)
                pe.wait_ge(*kv_tok.nth(l, NT))
                pe.wait_ge(*steps_in.nth(l, 1))
                units = [(d, hh) for d in range(2) for hh in range(H)]
                pe.wait_ge(*dense_out.nth(l, 14))

                out_bank = psD[:, 0, 512:1024]
                pair = psD[:, 1, :].rearrange("p (b n) -> p b n", b=2)

                def rows(hh):
                    return slice(64 * (hh % 2), 64 * (hh % 2) + 64)

                def part(s, hh, d, c):
                    c0 = tok_cols((s, 3 - s)[d] if s < 4 else 4)
                    return qkv[rows(hh), c + hh // 2, c0:c0 + P]

                def cumulative(s):
                    for d, hh in units:
                        last = mm(pair[:, d, hh * P:(hh + 1) * P],
                                  small["g"][:, s, d, hh:hh + 1].to_broadcast([P, P]), tri[:, d],
                                  start=True, stop=True)
                    last.then_inc(cumrow_ps.sem, 1)

                def k_times(s, c, done):
                    for d, hh in units:
                        q4 = d * 2 + hh // 2
                        last = mm(pair[:, hh % 2, q4 * P:(q4 + 1) * P], part(s, hh, d, 2), part(s, hh, d, c),
                                  start=True, stop=True)
                    last.then_inc(done.sem, 1)

                def keys_of_state(s):
                    for d, hh in units:
                        q4 = d * 2 + hh // 2
                        last = mm(pair[:, hh % 2, q4 * 64:(q4 + 1) * 64], part(s, hh, d, 2),
                                  state[rows(hh), s // 4, d, hh // 2, :], start=True, stop=True)
                    last.then_inc(ks_ps.sem, 1)

                def new_values(s):
                    for d, hh in units:
                        last = mm(out_bank[:, (d * 4 + hh) * 64:(d * 4 + hh + 1) * 64], xit[:, d, hh], rhs[:, d, hh],
                                  start=True, stop=True)
                    last.then_inc(vn_ps.sem, 1)

                def outputs(s):
                    for d, hh in units:
                        q4 = d * 2 + hh // 2
                        out = out_bank[rows(hh), q4 * P:(q4 + 1) * P]
                        mm(out, vn[:, d, hh], decays_t[s % 2][:, d, hh], start=True, stop=False)
                        mm(out, state[rows(hh), s // 4, d, hh // 2, :], qg[rows(hh), d, hh // 2],
                           start=False, stop=True)
                    for d, hh in units:
                        q4 = d * 2 + hh // 2
                        last = mm(pair[rows(hh), 0, q4 * 64:(q4 + 1) * 64], ks[:, d, hh], vn[:, d, hh],
                                  start=True, stop=True)
                    last.then_inc(o_ps.sem, 1)

                cumulative(0)
                pe.wait_ge(*decay_arg.nth(l, 1))
                pe.wait_ge(*eq_ready.nth(l, 1))
                k_times(0, 2, gram_ps)
                for s in range(5):
                    pe.wait_ge(*l_ready.nth(l, s + 1))
                    for d, hh in units:
                        last = nc.tensor.transpose(psA[:, d, hh * P:(hh + 1) * P], lmat[:, d, hh], c_("ident"))
                    last.then_inc(lt_ps.sem, 1)
                    k_times(s, 0, at_ps)
                    for k in range(1, 7):
                        for d in range(2):
                            pe.wait_ge(*inv_in.nth(l, s * 26 + 4 * k - 3 + d))
                            for hh in range(H):
                                last = mm(psA[:, d, hh * P:(hh + 1) * P], lmat_t[:, d, hh], xi[:, d, hh],
                                          start=True, stop=True)
                            last.then_inc(inv_ps.sem, 1)
                        if k == 1 and s:
                            pe.wait_ge(*vn_ready.nth(l, s))
                            outputs(s - 1)
                        if k == 2:
                            if s:
                                pe.wait_ge(*scan_done.nth(l, s))
                            keys_of_state(s)
                        if k == 4 and s < 4:
                            pe.wait_ge(*rhs_ready.nth(l, s + 1))
                            cumulative(s + 1)
                        if k == 5 and s < 4:
                            pe.wait_ge(*decay_arg.nth(l, s + 2))
                            pe.wait_ge(*eq_ready.nth(l, s + 2))
                            k_times(s + 1, 2, gram_ps)
                        for d in range(2):
                            pe.wait_ge(*inv_in.nth(l, s * 26 + 4 * k - 1 + d))
                            for hh in range(H):
                                last = mm(psA[:, 2 + d, hh * P:(hh + 1) * P], wm[:, d, hh], xit[:, d, hh],
                                          start=True, stop=True)
                            if k < 6:
                                for hh in range(H):
                                    last = mm(psA[:, d, hh * P:(hh + 1) * P], xit[:, d, hh], wm[:, d, hh],
                                              start=True, stop=True)
                            last.then_inc(inv_ps.sem, 1)
                    pe.wait_ge(*inv_in.nth(l, s * 26 + 26))
                    if s == 4:
                        pe.wait_ge(*rhs_ready.nth(l, 5))
                    new_values(s)
                pe.wait_ge(*vn_ready.nth(l, 5))
                outputs(4)
                pe.wait_ge(*osq_ready.nth(l, 1))
                for c in range(2):
                    out = psA[:, 2 * c:2 * c + 2, :].rearrange("p b n -> p (b n)")
                    for a, b in SEGS:
                        last = mm(out[:, a:b], c_("blk"), osq[:, c, a:b], start=True, stop=True)
                last.then_inc(osum_ps.sem, 1)

            def attend(l, n0, scores, ready, v, pt_src, n_maps):

                def score(u):
                    hh, t = divmod(u, NT)
                    for m in range(n_maps):
                        if n_maps == 1 and u >= 2:
                            pe.wait_ge(*exps.nth(l, u - 1))
                        if n_maps == 2 and u >= 1:
                            pe.wait_ge(*exps.nth(l, U + 2 * u - 1 + m))
                        b2 = 2 * (u % 2) if n_maps == 1 else 2 * m
                        out = psA[:, b2:b2 + 2, :].rearrange("p b n -> p (b n)")
                        q, k = scores(hh, m)
                        qt = q[:, t * P:(t + 1) * P]
                        if t < NT - 1:
                            for a, b in SEGS:
                                last = mm(out[:, a:b], qt, k[:, a:b], start=True, stop=True)
                        else:
                            last = mm(out[:, 0:CTX], qt, k[:, T:KEYS], start=True, stop=True)
                        last.then_inc(s_ps.sem, 1)

                def values(u):
                    hh, t = divmod(u, NT)
                    nk = 5 if t < NT - 1 else 1
                    pe.wait_ge(*pt_in.nth(l, n0 + u + 1))
                    pt = prob_t if n_maps == 1 else d_prob_t
                    for k in range(nk):
                        last = mm(psD[:, u % 2, T:T + 64], pt[:, u % 2, k * P:(k + 1) * P],
                                  v[:, k if nk > 1 else 5, hh * 64:(hh + 1) * 64], start=k == 0, stop=k == nk - 1)
                    last.then_inc(pv_ps.sem, 1)

                score(0)
                for u in range(U):
                    t = u % NT
                    if u + 1 < U:
                        score(u + 1)
                    nk = 5 if t < NT - 1 else 1
                    if u >= 2:
                        pe.wait_ge(*pv_in.nth(l, n0 + u - 1))
                    pe.wait_ge(*ready(u))
                    for k in range(nk):
                        last = nc.tensor.transpose(psD[:, u % 2, k * P:(k + 1) * P],
                                                   pt_src[:, u % 2, k * P:(k + 1) * P], c_("ident"))
                    last.then_inc(pt_ps.sem, 1)
                    if u:
                        values(u - 1)
                values(U - 1)

            def turn_outputs(o):
                for c in range(2):
                    out = psA[:, 2 * c:2 * c + 2, :].rearrange("p b n -> p (b n)")
                    for t in range(NT):
                        src = o[:, t].rearrange("p h v -> p (h v)")[:, c * P:(c + 1) * P]
                        last = nc.tensor.transpose(out[:, t * P:(t + 1) * P], src, c_("ident"))
                last.then_inc(ot_ps.sem, 1)

            def mla(l):
                pe.wait_ge(*gdn_done.nth(l, 1))
                pe.wait_ge(*mla_sq.nth(l, 1))
                for n, chunks in enumerate(((0, 1), (2,))):
                    out = psA[:, 2 * n:2 * n + 2, :].rearrange("p b n -> p (b n)")
                    for c in chunks:
                        for a, b in SEGS:
                            last = mm(out[:, a:b], c_("ones"), m_sq[:, c, a:b], start=c == chunks[0],
                                      stop=c == chunks[-1])
                    last.then_inc(mla_sum.sem, 1)
                pe.wait_ge(*mla_n.nth(l, 1))
                uq = p_("uq").rearrange("p (k c) -> p k c", k=2)
                for hh in range(H):
                    if hh >= 2:
                        pe.wait_ge(*mla_q_in.nth(l, hh - 1))
                    for k in range(2):
                        for a, b in SEGS:
                            last = mm(psD[0:96, hh % 2, a:b], uq[:, k, hh * 96:(hh + 1) * 96], m_cq[:, k, a:b],
                                      start=k == 0, stop=k == 1)
                    last.then_inc(mla_q_ps.sem, 1)
                pe.wait_ge(*mla_n.nth(l, 2))
                pe.wait_ge(*mla_q_in.nth(l, H))
                ukv = p_("ukv").rearrange("p (h c) -> p h c", h=H)
                for hh in range(H):
                    if hh >= 2:
                        pe.wait_ge(*mla_k_in.nth(l, hh - 1))
                    for a, b in ((0, 512), (512, KEYS)):
                        last = mm(psD[0:64, hh % 2, a:b], ukv[:, hh, 0:64], m_ckv[:, a:b], start=True, stop=True)
                    last.then_inc(mla_k_ps.sem, 1)
                for n in range(3):
                    for t in (2 * n, 2 * n + 1):
                        last = mm(psA[:, n, (t % 2) * 256:(t % 2 + 1) * 256], m_ckv[:, t * P:(t + 1) * P],
                                  ukv[:, :, 64:128], start=True, stop=True)
                    last.then_inc(mla_v_ps.sem, 1)
                for n in range(5):
                    if n == 0:
                        held(pe, *mla_k_in.nth(l, H))
                    else:
                        held(pe, *rot_in.nth(l, n))
                    src = m_q[64:96, n, 0:LAT] if n < H else kpe[64:96, 0:LAT]
                    mm(psD[64:96, n % 2, 0:LAT], c_("rot", slice(64, 96))[:, 64:96], src, start=True, stop=True)\
                        .then_inc(rot_ps.sem, 1)
                pe.wait_ge(*mla_k_rope.nth(l, 1))
                pe.wait_ge(*mla_v_in.nth(l, 3))
                attend(l, 0, lambda hh, m: (m_q[0:96, hh], m_k[0:96, hh]), lambda u: exps.nth(l, u + 1), m_v, prob, 1)
                pe.wait_ge(*pv_in.nth(l, U))
                turn_outputs(o_tok)

            def diff(l):
                pe.wait_ge(*br_done.nth(l, 1))
                for n in range(4):
                    if n == 0:
                        pe.wait_ge(*dense_out.nth(l, N_WIN))
                    else:
                        pe.wait_ge(*d_rot_in.nth(l, n))
                    src = (d_q if n < 2 else d_k)[:, n % 2, 0:LAT]
                    mm(psD[:, n % 2, 0:LAT], c_("rot"), src, start=True, stop=True).then_inc(d_rot_ps.sem, 1)
                for n in range(3):
                    for t in (2 * n, 2 * n + 1):
                        if t < NT:
                            for c in range(2):
                                last = nc.tensor.transpose(
                                    psA[:, n, (t % 2) * 256 + c * P:(t % 2) * 256 + (c + 1) * P],
                                    d_vf[:, c, t * P:(t + 1) * P], c_("ident"))
                    last.then_inc(dv_ps.sem, 1)
                pe.wait_ge(*d_rot_in.nth(l, 4))
                pe.wait_ge(*dv_in.nth(l, 3))

                def scores(hh, m):
                    g4 = hh * 2 + m
                    r = slice(32 * (g4 % 4), 32 * (g4 % 4) + 32)
                    return d_q[r, g4 // 4], d_k[r, g4 // 4]

                attend(l, U, scores, lambda u: comb.nth(l, u + 1), d_v, d_prob, 2)
                pe.wait_ge(*do_normed.nth(l, 1))
                turn_outputs(do_tok)

            def merge(l):
                held(pe, *br_done.nth(l, 2))
                held(pe, *h_split.nth(l, 1))
                with pe.Fori(0, KC) as d:
                    for n in range(4):
                        landed(l, B_GATE + 2 * n, d * 2)
                        b = n % 2
                        pe.wait_ge(proj_used.sem, l * (N_GATE + 2) + d * 4 + (n + 1))
                        out = psA[:, 2 * b:2 * b + 2, :].rearrange("p b n -> p (b n)")
                        for k in range(2):
                            for a, c in SEGS:
                                mm(out[:, a:c], ring[:, 2 * n % RING, KC + k, :], bout[:, n, k, a:c], start=k == 0, stop=k == 1)
                        pe.wait_ge(w_low_in.sem, l * N_SPLIT + d * 4 + (n + 1))
                        dense_split(b, b, h_high, h_low)
                        pe.wait_ge(proj_used.sem, l * (N_GATE + 2) + d * 4 + (n + 2))
                        modulation(l, lambda c: psD[:, 1 - b, bass.ds(d * 4 + (HALF + 2 * (n // 2) + c), 1)], n, d * 4)

            def out_proj(l):
                for m in range(KC):
                    pe.wait_ge(*w_low_in.nth(l, N_GATE + m + 1))
                    if m == 0:
                        pe.wait_ge(*merged_ready.nth(l, KC))
                        pe.wait_ge(*mod_ready.nth(l, 2))
                    elif m >= 2:
                        pe.wait_ge(*residual.nth(l, m - 1))
                    dense_split(m % 2, m % 2, z_high, z_low)

            def mlp(l):
                with pe.Fori(0, GROUPS) as g:
                    def early(j):
                        modulation(l, lambda c: psA[:, 0, bass.ds(g * (2 * RING) + (2 * j + c), 1)], N_LATE + j, g * 4)

                    for j in range(KC):
                        pe.wait_ge(w_low_in.sem, l * N_SPLIT + g * (2 * KC) + (N_GATE + N_OUT + j + 1))
                        if j == 0:
                            pe.wait_ge(*h_split.nth(l, 2))
                        if j < 2:
                            pe.wait_ge(residual.sem, l * 40 + g * 8 + (1 + 7 + j))
                        else:
                            pe.wait_ge(hid_relu.sem, l * 32 + g * 8 + (j - 1))
                        dense_split(j % 2, j % 2, h_high, h_low)
                        if j % 4 == 1:
                            early(j // 4)
                    for m in range(KC):
                        pe.wait_ge(w_low_in.sem, l * N_SPLIT + g * (2 * KC) + (N_GATE + N_OUT + KC + m + 1))
                        if m == 0:
                            pe.wait_ge(hid_ready.sem, l * 32 + g * 8 + 8)
                        if m < 2:
                            pe.wait_ge(hid_relu.sem, l * 32 + g * 8 + (7 + m))
                        else:
                            pe.wait_ge(residual.sem, l * 40 + g * 8 + (1 + 8 + m - 1))
                        dense_split(m % 2, m % 2, z_high, z_low)
                        if m % 4 == 1:
                            early(2 + m // 4)

            pe.wait_ge(residual.sem, 1)
            with pe.Fori(0, N_EARLY // RING) as i:
                for j in range(RING):
                    pe.wait_ge(weighed_in.sem, i * (RING * 2 * KC) + (j + 1) * 2 * KC)
                    for c in range(2):
                        last = mm(psA[:, 0, bass.ds(i * (2 * RING) + (2 * j + c), 1)], weighed[:, j % 2, c, :],
                                  c_("ones")[:, 0:1], start=True, stop=True)
                    last.then_inc(block_done.sem, 1)
            with pe.Fori(0, DEPTH) as l:
                norm_sum(l, 0)
                pe.wait_ge(*h_ready.nth(l, KC))
                for n in range(6):
                    win_block(l, n)
                hyena(l)
                pe.wait_ge(*hy_done.nth(l, 1))
                for n in range(6, 14):
                    win_block(l, n)
                gdn(l)
                pe.wait_ge(*gdn_done.nth(l, 1))
                for n in range(14, 18):
                    win_block(l, n)
                mla(l)
                pe.wait_ge(*br_done.nth(l, 1))
                for n in range(18, 24):
                    win_block(l, n)
                diff(l)
                merge(l)
                out_proj(l)
                pe.wait_ge(*residual.nth(l, 7))
                norm_sum(l, 1)
                mlp(l)
            norm_sum(DEPTH, 0)

        @block.scalar
        def _(act):
            a = nc.scalar.activation
            chain = Chain(act, act_chain.sem, links[1])

            def evac(l, n, dst):
                act.wait_ge(*block_done.nth(l, n + 1))
                a(dst, psD[:, n % 2, 0:T], ACT.Copy).then_inc(dense_out.sem, 1)

            def evac_conv(l, n):
                act.wait_ge(*block_done.nth(l, n + 1))
                if n >= 2:
                    act.wait_ge(*conv_out.nth(l, n - 1))
                a(stage[:, n % 2, 1:1 + LAT], psD[:, n % 2, 0:LAT], ACT.Copy)
                a(stage[:, n % 2, 3 + LAT:3 + T], psD[:, n % 2, LAT:T], ACT.Copy).then_inc(dense_out.sem, 1)

            def high_part(l, place, n, turns=0, back=2):
                j = place % RING
                act.wait_ge(ring_in[j].sem, (l * PER_SLOT + turns + ((N_EARLY + place) // RING + 1)) * 16)
                act.wait_ge(block_done.sem, l * N_BLOCKS + turns * RING + (RING + N_EARLY + place - back + 1))
                a(w_high[:, n % 2], ring[:, j, 0:KC, :], ACT.Copy).then_inc(w_high_in.sem, 1)

            def norm(l, which):
                for c in range(KC):
                    if which and c + 2 < N_OUT:
                        high_part(l, B_OUT + c + 2, c + 2)
                    act.wait_ge(*residual.nth(l, which * (c + 1)))
                    a(h[:, c], x[:, c], ACT.Square).then_inc(x_squared.sem, 1)
                act.wait_ge(*sumsq_done.nth(l, which + 1))
                chain.link(a(rs[:], psD[:, 0, 0:T], ACT.Ln, scale=1.0 / D, bias=c_("eps")))
                a(rs[:], rs[:], ACT.Exp, scale=-0.5).then_inc(rstd_ready.sem, 1)

            def modulate(l, which):
                act.wait_ge(*mod_ready.nth(l, 1 + which))
                for c in range(KC):
                    act.wait_ge(*x_scaled.nth(l, which * KC + c + 1))
                    for s, (p, q) in enumerate(SEGS):
                        last = a(h[:, c, p:q], h[:, c, p:q], ACT.Identity, scale=mod_a[:, which, c, s:s + 1],
                                 bias=mod[:, which * 24 + c, s:s + 1])
                    last.then_inc(h_ready.sem, 1)

            def hyena(l):
                for n in range(2):
                    act.wait_ge(*filt_arg.nth(l, n + 1))
                    a(ssin[0:64], sarg[0:64], ACT.Sin).then_inc(filt_sin.sem, 1)
                for f in range(NT):
                    act.wait_ge(*hspec_ps.nth(l, f + 1))
                    wf = c_("wf")[:, f:f + 1]
                    a(hspec[:, f, 0:2], psA[:, f % 2, :].rearrange("p (c n) -> p c n", c=2), ACT.Identity, scale=wf)
                    a(hspec[:, f, 2], psA[:, f % 2, 0:256], ACT.Identity, scale=wf).then_inc(hspec_ready.sem, 1)
                act.wait_ge(*hvt_ps.nth(l, 1))
                a(hvt[:, 0:4], psA[:, 0:2, :].rearrange("p b (t n) -> p (b t) n", t=2), ACT.Copy)
                a(hvt[:, 4], psA[:, 2, 0:256], ACT.Copy).then_inc(hvt_ready.sem, 1)

            def gdn(l):
                act.wait_ge(*hy_done.nth(l, 1))
                for n in range(6, 12):
                    evac_conv(l, n)
                    if n > 6:
                        silu_tanh(l, n - 7)
                silu_tanh(l, 5)
                for c in range(2):
                    act.wait_ge(*block_done.nth(l, 12 + c + 1))
                    ins_ = a(gz[:, c], psD[:, c, 0:T], ACT.Copy)
                    ins_.then_inc(dense_out.sem, 1)
                    act.wait_ge(*dense_out.nth(l, 13 + c))
                    act.wait_ge(*g_silu.nth(l, 5 + c))
                    a(th[:, c, 0:T], gz[:, c], ACT.Tanh, scale=0.5).then_inc(g_tanh.sem, 1)
                act.wait_ge(*ab_in.nth(l, 1))
                f8 = lambda n: small[n].rearrange("p s d h -> p (s d h)")
                a(expa, p_("alog"), ACT.Exp)
                a(small["z0"], ab[:, :, :, 4:8], ACT.Tanh, scale=0.5)
                chain.link(a(f8("e"), f8("u"), ACT.Abs))
                a(f8("e"), f8("e"), ACT.Exp, scale=-1.0).then_inc(ab_e.sem, 1)
                act.wait_ge(*ab_w.nth(l, 1))
                a(f8("ln"), f8("w"), ACT.Ln).then_inc(ab_ln.sem, 1)
                act.wait_ge(*cum_in.nth(l, 1))
                a(f8("eg"), f8("gcol"), ACT.Exp)
                a(f8("etot"), f8("tot"), ACT.Exp)
                a(f8("es"), f8("es"), ACT.Exp).then_inc(cum_exp.sem, 1)
                for c in range(4):
                    act.wait_ge(*(g_silu.nth(l, 8) if c < 2 else qk_ps.nth(l, c - 1)))
                    a(th[:, c % 2], qkv[:, c], ACT.Square).then_inc(qk_sq.sem, 1)
                    if c >= 1:
                        length_ln(l, c - 1)
                length_ln(l, 3)
                act.wait_ge(*qk_ln.nth(l, 4))
                a(rn, rn, ACT.Exp, scale=-0.5).then_inc(qk_rs.sem, 1)
                for t in range(NT):
                    act.wait_ge(*kv_ps.nth(l, t + 1))
                    a(ktok[:, t], psA[:, t % 2, 0:256], ACT.Copy)
                    a(vtok[:, t], psA[:, t % 2, 256:512], ACT.Copy, scale=0.5).then_inc(kv_tok.sem, 1)
                def exps_of_decays(s):
                    act.wait_ge(*decay_arg.nth(l, s + 1))
                    for r in range(2):
                        lanes = slice(64 * r, 64 * r + 64)
                        src = psD[lanes, 1, :].rearrange("p (d q r j) -> p d q r j", d=2, q=2, r=2)[:, :, :, r]
                        last = a(eq[lanes], src, ACT.Exp)
                    last.then_inc(eq_ready.sem, 1)
                    act.wait_ge(*masked.nth(l, 2 * s + 1))
                    a(decays_t[s % 2], decays_t[s % 2], ACT.Exp).then_inc(decay_ready.sem, 1)
                    act.wait_ge(*masked.nth(l, 2 * s + 2))
                    a(decay_n, decay_n, ACT.Exp, scale=-1.0).then_inc(decay_ready.sem, 1)

                exps_of_decays(0)
                for s in range(5):
                    act.wait_ge(*lt_ps.nth(l, s + 1))
                    a(lmat_t.rearrange("p d h j -> p d (h j)"), psA[:, 0:2, :], ACT.Copy).then_inc(lt_ready.sem, 1)
                    if s < 4:
                        exps_of_decays(s + 1)
                    act.wait_ge(*vn_ps.nth(l, s + 1))
                    a(vn.rearrange("p d h v -> p (d h v)"), psD[:, 0, 512:1024], ACT.Copy).then_inc(vn_ready.sem, 1)
                act.wait_ge(*scan_done.nth(l, 5))
                a(osq, oT, ACT.Square).then_inc(osq_ready.sem, 1)
                act.wait_ge(*osum_ps.nth(l, 1))
                src = psA[:, :, :].rearrange("p (c b) n -> p c (b n)", c=2)[:, :, 0:T]
                chain.link(a(osq, src, ACT.Ln, scale=1.0 / 64, bias=c_("eps")))
                a(osq, osq, ACT.Exp, scale=-0.5).then_inc(o_rs.sem, 1)

            def silu_tanh(l, c):
                act.wait_ge(*conv_out.nth(l, 6 + c + 1))
                if c >= 2:
                    act.wait_ge(*g_silu.nth(l, c - 1))
                a(th[:, c % 2], qkv[:, c], ACT.Tanh, scale=0.5).then_inc(g_tanh.sem, 1)

            def length_ln(l, c):
                act.wait_ge(*qk_ps.nth(l, c + 1))
                src = psA[:, 2 * (c % 2):2 * (c % 2) + 2, :].rearrange("p b n -> p (b n)")[:, 0:CV]
                a(rn[:, c], src, ACT.Ln, bias=c_("eps4")).then_inc(qk_ln.sem, 1)

            def attend(l, n0, n_maps, sc, small_, probs, pt):
                x0 = 0 if n_maps == 1 else U

                def exp(u):
                    nk = T if u % NT < NT - 1 else CTX
                    for m in range(n_maps):
                        n = x0 + n_maps * u + m + 1
                        act.wait_ge(*negmax.nth(l, n))
                        b2 = 2 * (u % 2) if n_maps == 1 else 2 * m
                        src = psA[:, b2:b2 + 2, :].rearrange("p b n -> p (b n)")[:, 0:nk]
                        a(probs[m][:, u % 2, 0:nk], src, ACT.Exp, scale=sc, bias=small_[:, 2 * m, u:u + 1],
                          accum_out=small_[:, 2 * m + 1, u:u + 1]).then_inc(exps.sem, 1)

                exp(0)
                for u in range(U):
                    if u + 1 < U:
                        exp(u + 1)
                    nk = T if u % NT < NT - 1 else CTX
                    act.wait_ge(*pt_ps.nth(l, n0 + u + 1))
                    if u >= 2:
                        act.wait_ge(*pv_ps.nth(l, n0 + u - 1))
                    a(pt[:, u % 2, 0:nk], psD[:, u % 2, 0:nk], ACT.Copy).then_inc(pt_in.sem, 1)

            def branch_out(l, n, branch):
                act.wait_ge(*ot_ps.nth(l, n))
                for c in range(2):
                    last = a(bout[:, branch, c], psA[:, 2 * c:2 * c + 2, :].rearrange("p b n -> p (b n)")[:, 0:T],
                             ACT.Copy)
                last.then_inc(br_done.sem, 1)

            def mla(l):
                act.wait_ge(*gdn_done.nth(l, 1))
                act.wait_ge(*stored.nth(l, 1))
                evac(l, 14, m_cq[:, 0])
                evac(l, 15, m_cq[:, 1])
                for n, dst in ((16, m_ckv), (17, kpe)):
                    act.wait_ge(*block_done.nth(l, n + 1))
                    a(dst[:, 0:LAT], psD[:, n % 2, 0:LAT], ACT.Copy)
                    a(dst[:, T:KEYS], psD[:, n % 2, LAT:T], ACT.Copy).then_inc(dense_out.sem, 1)
                act.wait_ge(*dense_out.nth(l, 18))
                a(m_sq[:, 0:2], m_cq, ACT.Square)
                a(m_sq[:, 2, 0:LAT], m_ckv[:, 0:LAT], ACT.Square)
                a(m_sq[:, 2, LAT:T], m_ckv[:, T:KEYS], ACT.Square).then_inc(mla_sq.sem, 1)
                for n, wd in enumerate((256, 128)):
                    act.wait_ge(*mla_sum.nth(l, n + 1))
                    src = psA[:, 2 * n:2 * n + 2, :].rearrange("p b n -> p (b n)")[:, 0:T]
                    chain.link(a(m_rs[:, n], src, ACT.Ln, scale=1.0 / wd, bias=c_("eps")))
                for n in range(2):
                    a(m_rs[:, n], m_rs[:, n], ACT.Exp, scale=-0.5).then_inc(mla_rs.sem, 1)
                for hh in range(H):
                    act.wait_ge(*mla_q_ps.nth(l, hh + 1))
                    a(m_q[0:96, hh], psD[0:96, hh % 2, 0:T], ACT.Copy).then_inc(mla_q_in.sem, 1)
                for hh in range(H):
                    act.wait_ge(*mla_k_ps.nth(l, hh + 1))
                    a(m_k[0:64, hh], psD[0:64, hh % 2, 0:KEYS], ACT.Copy).then_inc(mla_k_in.sem, 1)
                for n in range(3):
                    act.wait_ge(*mla_v_ps.nth(l, n + 1))
                    a(m_v[:, 2 * n:2 * n + 2], psA[:, n, :].rearrange("p (t c) -> p t c", t=2), ACT.Copy)\
                        .then_inc(mla_v_in.sem, 1)
                attend(l, 0, 1, 96 ** -0.5, att_small, (prob,), prob_t)
                branch_out(l, 1, 0)

            def diff(l):
                act.wait_ge(*stored.nth(l, 3))
                act.wait_ge(*br_done.nth(l, 1))
                for n in (18, 19):
                    evac(l, n, d_q[:, n - 18])
                for n in (20, 21):
                    act.wait_ge(*block_done.nth(l, n + 1))
                    a(d_k[:, n - 20, 0:LAT], psD[:, n % 2, 0:LAT], ACT.Copy)
                    a(d_k[:, n - 20, T:KEYS], psD[:, n % 2, LAT:T], ACT.Copy).then_inc(dense_out.sem, 1)
                for n in (22, 23):
                    evac(l, n, d_vf[:, n - 22])
                a(d_k[:, :, LAT:T], p_("dk_c").rearrange("p (c t) -> p c t", c=2), ACT.Copy)
                a(d_v[:, 4], p_("dv_c"), ACT.Copy)
                for n in range(3):
                    act.wait_ge(*dv_ps.nth(l, n + 1))
                    if n < 2:
                        last = a(d_v[:, 2 * n:2 * n + 2], psA[:, n, :].rearrange("p (t c) -> p t c", t=2), ACT.Copy)
                    else:
                        last = a(d_v[:, 5], psA[:, n, 0:256], ACT.Copy)
                    last.then_inc(dv_in.sem, 1)
                act.wait_ge(*lam_sum.nth(l, 1))
                a(lam_s[:, 68:70], lam_s[:, 64:66], ACT.Exp).then_inc(lam_exp.sem, 1)
                attend(l, U, 2, 32 ** -0.5, d_small, (d_prob, d_prob2), d_prob_t)
                act.wait_ge(*do_sum.nth(l, 1))
                chain.link(a(d_small[:, 4], d_small[:, 4], ACT.Ln, scale=1.0 / 64, bias=c_("eps")))
                a(d_small[:, 4], d_small[:, 4], ACT.Exp, scale=-0.5).then_inc(do_rs.sem, 1)
                branch_out(l, 2, 3)

            def merge(l):
                act.wait_ge(*stored.nth(l, 5))
                high_part(l, B_GATE, 0)
                with act.Fori(0, KC) as d:
                    for n in range(4):
                        high_part(l, B_GATE + 2 * (n + 1), n + 1, d * 2, 4)
                        act.wait_ge(block_done.sem, l * N_BLOCKS + d * 8 + (RING + N_EARLY + B_GATE + 2 * n + 1))
                        act.wait_ge(proj_used.sem, l * (N_GATE + 2) + d * 4 + (n + 1))
                        a(halves(tg[:, n % 2]), psum_halves(n % 2), ACT.Tanh, scale=0.5).then_inc(gate_act.sem, 1)

            def mlp(l):
                turns = N_GROUP // RING

                def high(q, g):
                    high_part(l, mlp_at(q), q, g * turns, 2 if q < 2 else mlp_at(q) - mlp_at(q - 2))

                with act.Fori(0, GROUPS) as g:
                    high(0, g)
                    for j in range(KC):
                        high(j + 1, g)
                        act.wait_ge(block_done.sem, l * N_BLOCKS + g * N_GROUP + (RING + N_EARLY + mlp_at(j) + 1))
                        if j >= 2:
                            act.wait_ge(hid_ready.sem, l * 32 + g * 8 + (j - 1))
                        a(halves(hid_sq[:, j % 2]), psum_halves(j % 2), ACT.Relu).then_inc(hid_relu.sem, 1)
                        act.wait_ge(hid_relu.sem, l * 32 + g * 8 + (j + 1))
                        a(hid_sq[:, j % 2], hid_sq[:, j % 2], ACT.Square).then_inc(hid_square.sem, 1)
                    for m in range(1, KC):
                        high(KC + m, g)

            act.wait_ge(const_in.sem, 16)
            act.wait_ge(cond_in.sem, 16)
            a(cond_t[:], cond[:], ACT.Tanh, scale=0.5).then_inc(cond_tanh.sem, 1)
            with act.Fori(0, DEPTH) as l:
                chain.l, chain.n = l, 0
                act.wait_ge(*params_in.nth(l, 1))
                norm(l, 0)
                modulate(l, 0)
                for n in range(6):
                    evac_conv(l, n)
                hyena(l)
                gdn(l)
                mla(l)
                diff(l)
                merge(l)
                high_part(l, B_OUT + 1, 1, 0, 3)
                norm(l, 1)
                modulate(l, 1)
                mlp(l)
                n_links = chain.n
            assert n_links == links[1], ("ACT_LINKS", n_links)
            chain.l, chain.n = DEPTH, 0
            norm(DEPTH, 0)
            for c in range(KC):
                act.wait_ge(*x_scaled.nth(DEPTH, c + 1))
                a(h[:, c], h[:, c], ACT.Identity, scale=c_("fin")[:, c:c + 1]).then_inc(y_ready.sem, 1)

        @block.vector
        def _(dve):
            v = nc.vector
            chain = Chain(dve, dve_chain.sem, links[0])
            link = chain.link

            def norm_scale(which, name):
                return v.scalar_tensor_tensor(out=mod_a[:, which], in0=mod[:, which * 24 + 8:which * 24 + 16],
                                              scalar=1.0, in1=p_(name).unsqueeze(2).to_broadcast([P, KC, 2]),
                                              op0=ALU.add, op1=ALU.mult)

            def norm(l, which):
                dve.wait_ge(*rstd_ready.nth(l, which + 1))
                for c in range(KC):
                    v.tensor_tensor(h[:, c], x[:, c], rs[:], ALU.mult).then_inc(x_scaled.sem, 1)

            def split_h(l):
                for c in range(KC):
                    dve.wait_ge(*h_ready.nth(l, KC + c + 1))
                    v.tensor_copy(h_high[:, c], h[:, c]).then_inc(h_high_in.sem, 1)
                    dve.wait_ge(*h_high_in.nth(l, KC + c + 1))
                    last = v.tensor_tensor(h_low[:, c], h[:, c], h_high[:, c].bitcast(F32), ALU.subtract)
                last.then_inc(h_split.sem, 1)

            def conv(l, n, dst, w, bias):
                dve.wait_ge(*dense_out.nth(l, n + 1))
                st = stage[:, n % 2]
                i = n % 6
                if bias is None:
                    link(v.tensor_scalar(dst, st[:, 1:1 + CV], w[:, 3 * i + 1:3 * i + 2], None, ALU.mult))
                else:
                    link(v.tensor_scalar(dst, st[:, 1:1 + CV], w[:, 3 * i + 1:3 * i + 2], bias[:, i:i + 1],
                                         ALU.mult, ALU.add))
                link(v.scalar_tensor_tensor(out=dst, in0=st[:, 0:CV], scalar=w[:, 3 * i:3 * i + 1], in1=dst,
                                            op0=ALU.mult, op1=ALU.add))
                v.scalar_tensor_tensor(out=dst, in0=st[:, 2:2 + CV], scalar=w[:, 3 * i + 2:3 * i + 3], in1=dst,
                                       op0=ALU.mult, op1=ALU.add).then_inc(conv_out.sem, 1)

            def sin_arg(l, n, src, bias, r):
                dve.wait_ge(*filt_ps.nth(l, n))
                link(v.tensor_scalar(sarg[r], src, bias, p_("hfr", r), ALU.add, ALU.mult))
                link(v.tensor_scalar(sn[r], sarg[r], 1 / (2 * math.pi), ROUND, ALU.mult, ALU.add))
                link(v.tensor_scalar(sn[r], sn[r], ROUND, None, ALU.subtract))
                link(v.scalar_tensor_tensor(out=sarg[r], in0=sn[r], scalar=-TWO_PI_HI, in1=sarg[r], op0=ALU.mult,
                                            op1=ALU.add))
                link(v.scalar_tensor_tensor(out=sarg[r], in0=sn[r], scalar=-TWO_PI_LO, in1=sarg[r], op0=ALU.mult,
                                            op1=ALU.add))
                pi = float(np.nextafter(np.float32(math.pi), np.float32(0)))
                v.tensor_scalar(sarg[r], sarg[r], pi, -pi, ALU.min, ALU.max).then_inc(filt_arg.sem, 1)

            def hyena(l):
                w, bias = p_("hcw"), p_("hcb")
                for n, dst in enumerate((hx0[:, 0], hx0[:, 1], hx1[:, 0], hx1[:, 1], hv[:, 0], hv[:, 1])):
                    conv(l, n, dst, w, bias)
                dve.wait_ge(*conv_out.nth(l, 6))
                v.tensor_tensor(hv, hv, hx1, ALU.mult).then_inc(hv_ready.sem, 1)
                r = slice(0, 64)
                flat = psA[0:64, 2:4, :].rearrange("p b n -> p (b n)")[:, 0:T]
                dve.wait_ge(*dft_in.nth(l, 1))
                sin_arg(l, 1, flat, p_("hb1", r), r)
                sin_arg(l, 2, flat, p_("hb2", r), r)
                for t in range(NT):
                    dve.wait_ge(*filt_ps.nth(l, 3 + t))
                    link(v.tensor_tensor(hprod[:, t % 2], psA[:, t % 2, :], win[:, t], ALU.mult))
                    f, b = hprod[:, t % 2, 0:256], hprod[:, t % 2, 256:512]
                    v.tensor_tensor(filt[:, t, 0], f, b, ALU.add)
                    v.tensor_tensor(filt[:, t, 1], b, f, ALU.subtract).then_inc(filt_out.sem, 1)
                dve.wait_ge(*nyq_ps.nth(l, 1))
                for s in range(2):
                    v_ = hmul[0:1, s * 256:(s + 1) * 256]
                    link(v.tensor_scalar(v_, psA[0:1, 2 + s, 0:256], 1.0 / (2 * (LAT, CTX)[s]), None, ALU.mult))
                    last = v.tensor_tensor(hnyq[0:1, s], psA[0:1, 2 + s, 256:512], v_, ALU.mult)
                last.then_inc(nyq_ready.sem, 1)
                for f in range(NT):
                    dve.wait_ge(*vspec_ps.nth(l, f + 1))
                    src = psA[:, f % 2, :].rearrange("p (c n) -> p c n", c=2)
                    pr = hprod.rearrange("p a (c n) -> p a c n", c=2)
                    v.tensor_tensor(pr[:, 0], src, hspec[:, f, 0:2], ALU.mult)
                    link(v.tensor_tensor(pr[:, 1], src, hspec[:, f, 1:3], ALU.mult))
                    v.tensor_tensor(yspec[:, f, 0], pr[:, 0, 0], pr[:, 0, 1], ALU.add)
                    ins_ = v.tensor_tensor(yspec[:, f, 1], pr[:, 1, 1], pr[:, 1, 0], ALU.subtract)
                    ins_.then_inc(yspec_ready.sem, 1)
                    dve.wait_ge(*yspec_ready.nth(l, f + 1))
                for c in range(2):
                    dve.wait_ge(*hy_ps.nth(l, c + 1))
                    for (p, q), o in zip(SEGS, (0, 2)):
                        link(v.scalar_tensor_tensor(out=bout[:, 2, c, p:q], in0=hv[:, c, p + o:q + o],
                                                    scalar=p_("hyd")[:, c:c + 1], in1=psD[:, c, p:q],
                                                    op0=ALU.mult, op1=ALU.add))
                        last = v.tensor_tensor(bout[:, 2, c, p:q], bout[:, 2, c, p:q], hx0[:, c, p + o:q + o], ALU.mult)
                last.then_inc(hy_done.sem, 1)

            def silu(l, c):
                dve.wait_ge(*g_tanh.nth(l, c + 1))
                v.scalar_tensor_tensor(out=qkv[:, c], in0=th[:, c % 2], scalar=1.0, in1=qkv[:, c], op0=ALU.add,
                                       op1=ALU.mult).then_inc(g_silu.sem, 1)

            def gdn(l):
                dve.wait_ge(*hy_done.nth(l, 1))
                for n in range(6, 12):
                    conv(l, n, qkv[:, n - 6], p_("gcw"), None)
                    if n > 6:
                        silu(l, n - 7)
                silu(l, 5)
                for c in range(2):
                    dve.wait_ge(*g_tanh.nth(l, 7 + c))
                    v.scalar_tensor_tensor(out=gz[:, c], in0=th[:, c, 0:T], scalar=1.0, in1=gz[:, c], op0=ALU.add,
                                           op1=ALU.mult).then_inc(g_silu.sem, 1)
                dve.wait_ge(*ab_ps.nth(l, 1))
                src = psA[:, 0, 0:NT * 16].rearrange("p (t d c) -> p t d c", t=NT, d=2)
                v.tensor_copy(ab[:, :, 0], src[:, :, 0])
                for s in range(5):
                    last = v.tensor_copy(ab[:, s, 1], src[:, 3 - s if s < 4 else 4, 1])
                link(last)
                f8 = lambda n: small[n].rearrange("p s d h -> p (s d h)")
                dtb = p_("dtb").rearrange("p (d h) -> p d h", d=2).unsqueeze(1).to_broadcast([P, 5, 2, 4])
                v.tensor_tensor(small["u"], ab[:, :, :, 0:4], dtb, ALU.add).then_inc(ab_in.sem, 1)
                dve.wait_ge(*ab_e.nth(l, 1))
                link(v.tensor_scalar(f8("w"), f8("e"), 1.0, None, ALU.add))
                v.tensor_scalar(f8("beta"), f8("z0"), 0.5, 0.5, ALU.mult, ALU.add).then_inc(ab_w.sem, 1)
                link(v.tensor_scalar(f8("d"), f8("w"), 1.0, None, ALU.subtract))
                dve.wait_ge(*ab_ln.nth(l, 1))
                link(v.tensor_scalar(f8("nbeg"), f8("d"), 0.0, None, ALU.is_equal))
                v.tensor_tensor(f8("ln"), f8("ln"), f8("nbeg"), ALU.add)
                link(v.tensor_tensor(f8("d"), f8("d"), f8("nbeg"), ALU.add))
                link(v.reciprocal(f8("d"), f8("d")))
                link(v.tensor_tensor(f8("ln"), f8("ln"), f8("d"), ALU.mult))
                link(v.tensor_tensor(f8("ln"), f8("ln"), f8("e"), ALU.mult))
                link(v.scalar_tensor_tensor(out=f8("g"), in0=f8("u"), scalar=0.0, in1=f8("ln"), op0=ALU.max,
                                            op1=ALU.add))
                link(v.tensor_scalar(f8("g"), f8("g"), -1.0, None, ALU.mult))
                ea = expa.rearrange("p (d h) -> p d h", d=2).unsqueeze(1).to_broadcast([P, 5, 2, 4])
                v.tensor_tensor(small["g"], small["g"], ea, ALU.mult).then_inc(g_ready.sem, 1)
                dve.wait_ge(*cum_ps.nth(l, 1))
                for d in range(2):
                    last = v.tensor_copy(small["gcol"][:, :, d, :],
                                         psA[:, 1, d * 20:(d + 1) * 20].rearrange("p (s h) -> p s h", s=5))
                link(last)
                v.tensor_copy(f8("tot"), psA[:, 1, 40:80])
                v.tensor_tensor(f8("es"), psA[:, 1, 40:80], f8("gcol"), ALU.subtract).then_inc(cum_in.sem, 1)
                v.memset(oT, 0.0)
                v.memset(state[:, 1], 0.0)
                v.tensor_copy(state[:, 0].rearrange("p d q v -> p (d q v)"), p_("s0"))
                dve.wait_ge(*cum_exp.nth(l, 1))
                v.tensor_tensor(f8("nbeg"), f8("beta"), f8("eg"), ALU.mult).then_inc(steps_in.sem, 1)
                dve.wait_ge(*qk_rs.nth(l, 1))
                v.scalar_tensor_tensor(out=qkv[:, 0:2], in0=qkv[:, 0:2], scalar=0.125, in1=rn[:, 0:2], op0=ALU.mult,
                                       op1=ALU.mult)
                v.tensor_tensor(qkv[:, 2:4], qkv[:, 2:4], rn[:, 2:4], ALU.mult).then_inc(qk_norm.sem, 1)
                masks = c_("lvl").rearrange("p (k d j) -> p k d j", k=7, d=2)
                ident4 = c_("ident").unsqueeze(1).unsqueeze(1).to_broadcast([P, 2, 4, P])

                def mask(k):
                    return masks[:, k].unsqueeze(2).to_broadcast([P, 2, 4, P])

                pair = psD[:, 1, :].rearrange("p (b n) -> p b n", b=2)

                def decay_args(s):
                    dve.wait_ge(*cumrow_ps.nth(l, s + 1))
                    if s:
                        dve.wait_ge(*masked.nth(l, 2 * s))
                    for d in range(2):
                        last = v.tensor_tensor(earg[:, d], pair[:, d].rearrange("p (h j) -> p h j", h=H),
                                               small["gcol"][:, s, d].unsqueeze(2).to_broadcast([P, H, P]),
                                               ALU.subtract)
                    last.then_inc(decay_arg.sem, 1)

                def lower(s):
                    dve.wait_ge(*gram_ps.nth(l, s + 1))
                    dve.wait_ge(*decay_ready.nth(l, 2 * s + 2))
                    for d in range(2):
                        for hh in range(H):
                            q4 = d * 2 + hh // 2
                            last = v.scalar_tensor_tensor(out=lmat[:, d, hh],
                                                          in0=pair[:, hh % 2, q4 * P:(q4 + 1) * P],
                                                          scalar=small["beta"][:, s, d, hh:hh + 1],
                                                          in1=decay_n[:, d, hh], op0=ALU.mult, op1=ALU.mult)
                    last.then_inc(l_ready.sem, 1)

                def right_side(s):
                    dve.wait_ge(*ks_ps.nth(l, s + 1))
                    for r in range(2):
                        out = rhs.rearrange("p d (q r) v -> p d q r v", r=2)[:, :, :, r]
                        nb = small["nbeg"][:, s].rearrange("p d (q r) -> p d q r", r=2)[:, :, :, r]
                        last = v.tensor_tensor(out, pair[:, r, 0:256].rearrange("p (d q v) -> p d q v", d=2, q=2),
                                               nb.unsqueeze(3).to_broadcast([P, 2, 2, 64]), ALU.mult)
                    link(last)
                    dve.wait_ge(*scan_in.nth(l, s + 1))
                    v.tensor_tensor(rhs, bv, rhs, ALU.subtract).then_inc(rhs_ready.sem, 1)

                def collect(s):
                    seq = s // 4
                    dve.wait_ge(*o_ps.nth(l, s + 1))
                    for d in range(2):
                        t = (s, 3 - s)[d] if s < 4 else 4
                        o = oT[:, :, t * P:(t + 1) * P]
                        ins_ = v.tensor_tensor(o, o, psD[:, 0, 512 + d * 256:512 + (d + 1) * 256].rearrange(
                            "p (q j) -> p q j", q=2), ALU.add)
                        if s == 4 and d == 0:
                            link(ins_)
                    for r in range(2):
                        lanes = slice(64 * r, 64 * r + 64)
                        et = small["etot"][lanes, s].rearrange("p d (q r) -> p d q r", r=2)[:, :, :, r]
                        last = v.tensor_tensor(state[lanes, seq], state[lanes, seq],
                                               et.unsqueeze(3).to_broadcast([64, 2, 2, 64]), ALU.mult)
                    link(last)
                    v.tensor_tensor(state[:, seq].rearrange("p d q v -> p (d q v)"),
                                    state[:, seq].rearrange("p d q v -> p (d q v)"), pair[:, 0, 0:256], ALU.add)\
                        .then_inc(scan_done.sem, 1)

                decay_args(0)
                lower(0)
                for s in range(5):
                    dve.wait_ge(*l_ready.nth(l, s + 1))
                    link(v.tensor_tensor(wm, lmat, mask(0), ALU.mult))
                    link(v.tensor_tensor(xi, ident4, wm, ALU.subtract))
                    dve.wait_ge(*lt_ready.nth(l, s + 1))
                    for d in range(2):
                        last = v.tensor_tensor(wm[:, d], lmat_t[:, d],
                                               masks[:, 0, 1 - d].unsqueeze(1).to_broadcast([P, 4, P]), ALU.mult)
                    link(last)
                    dve.wait_ge(*at_ps.nth(l, s + 1))
                    for r in range(2):
                        dt_ = decays_t[s % 2].rearrange("p d (q r) j -> p d q r j", r=2)[:, :, :, r]
                        v.tensor_tensor(dt_, pair[:, r].rearrange("p (d q j) -> p d q j", d=2, q=2), dt_, ALU.mult)
                    if s:
                        dve.wait_ge(*vn_ps.nth(l, s))
                    for d in range(2):
                        v.tensor_tensor(xit[:, d], ident4[:, d], wm[:, d], ALU.subtract).then_inc(inv_in.sem, 1)
                    for k in range(1, 7):
                        for d in range(2):
                            dve.wait_ge(*inv_ps.nth(l, s * 24 + 4 * k - 3 + d))
                            v.tensor_tensor(wm[:, d], psA[:, d, :].rearrange("p (h j) -> p h j", h=H),
                                            masks[:, k, d].unsqueeze(1).to_broadcast([P, 4, P]), ALU.mult)\
                                .then_inc(inv_in.sem, 1)
                        if k == 2 and s:
                            collect(s - 1)
                        if k == 3:
                            right_side(s)
                        if k == 5 and s < 4:
                            decay_args(s + 1)
                        for d in range(2):
                            dve.wait_ge(*inv_ps.nth(l, s * 24 + 4 * k - 1 + d))
                            if k < 6:
                                v.tensor_tensor(xi[:, d], xi[:, d], psA[:, d, :].rearrange("p (h j) -> p h j", h=H),
                                                ALU.subtract)
                            v.tensor_tensor(xit[:, d], xit[:, d],
                                            psA[:, 2 + d, :].rearrange("p (h j) -> p h j", h=H),
                                            ALU.subtract).then_inc(inv_in.sem, 1)
                    if s < 4:
                        lower(s + 1)
                collect(4)
                link(v.tensor_scalar(gz, gz, p_("gnw"), 0.5, ALU.mult, ALU.mult))
                dve.wait_ge(*o_rs.nth(l, 1))
                link(v.tensor_tensor(osq, osq, gz, ALU.mult))
                v.tensor_tensor(bout[:, 1], oT, osq, ALU.mult).then_inc(gdn_done.sem, 1)

            def attend(l, n0, n_maps, sc, small_, probs, otok):
                x0 = 0 if n_maps == 1 else U

                def row_max(u):
                    nk = T if u % NT < NT - 1 else CTX
                    for m in range(n_maps):
                        dve.wait_ge(*s_ps.nth(l, x0 + n_maps * u + m + 1))
                        b2 = 2 * (u % 2) if n_maps == 1 else 2 * m
                        src = psA[:, b2:b2 + 2, :].rearrange("p b n -> p (b n)")[:, 0:nk]
                        link(v.tensor_reduce(small_[:, 2 * m, u:u + 1], src, AX.X, ALU.max, negate=True))
                        v.tensor_scalar(small_[:, 2 * m, u:u + 1], small_[:, 2 * m, u:u + 1], sc, None, ALU.mult)\
                            .then_inc(negmax.sem, 1)

                def combine(u):
                    nk = T if u % NT < NT - 1 else CTX
                    dve.wait_ge(*exps.nth(l, x0 + 2 * u + 2))
                    s1, s2, cf = (small_[:, i, u:u + 1] for i in (1, 3, 5))
                    link(v.reciprocal(cf, s2))
                    link(v.tensor_scalar(cf, cf, s1, lam_s[:, 71:72], ALU.mult, ALU.mult))
                    v.scalar_tensor_tensor(out=probs[0][:, u % 2, 0:nk], in0=probs[1][:, u % 2, 0:nk], scalar=cf,
                                           in1=probs[0][:, u % 2, 0:nk], op0=ALU.mult, op1=ALU.add)\
                        .then_inc(comb.sem, 1)

                def scale_values(u):
                    hh, t = divmod(u, NT)
                    dve.wait_ge(*pv_ps.nth(l, n0 + u + 1))
                    link(v.reciprocal(small_[:, 1, u:u + 1], small_[:, 1, u:u + 1]))
                    v.tensor_scalar(otok[:, t, hh], psD[:, u % 2, T:T + 64], small_[:, 1, u:u + 1], None, ALU.mult)\
                        .then_inc(pv_in.sem, 1)

                row_max(0)
                for u in range(U):
                    if u + 1 < U:
                        row_max(u + 1)
                    if n_maps == 2:
                        combine(u)
                    if u:
                        scale_values(u - 1)
                scale_values(U - 1)

            def rope(dst, src, ps, c, s, tmp):
                link(v.tensor_tensor(tmp, ps, s, ALU.mult))
                link(v.tensor_tensor(dst, src, c, ALU.mult))
                return v.tensor_tensor(dst, dst, tmp, ALU.add)

            def mla(l):
                dve.wait_ge(*mla_rs.nth(l, 1))
                for c in range(2):
                    last = v.scalar_tensor_tensor(out=m_cq[:, c], in0=m_cq[:, c], scalar=p_("qn")[:, c:c + 1],
                                                  in1=m_rs[:, 0], op0=ALU.mult, op1=ALU.mult)
                last.then_inc(mla_n.sem, 1)
                dve.wait_ge(*mla_rs.nth(l, 2))
                v.tensor_copy(m_ckv[:, LAT:T], p_("ckv_c"))
                v.tensor_copy(kpe[64:96, LAT:T], p_("kpe_c", slice(64, 96)))
                for (p, q), o in zip(SEGS, (0, 128)):
                    last = v.scalar_tensor_tensor(out=m_ckv[:, p + o:q + o], in0=m_ckv[:, p + o:q + o],
                                                  scalar=p_("kvn"), in1=m_rs[:, 1, p:q], op0=ALU.mult, op1=ALU.mult)
                last.then_inc(mla_n.sem, 1)
                dve.wait_ge(*mla_n.nth(l, 2))
                cos, sin = c_("cos", slice(64, 96)), c_("sin", slice(64, 96))
                for n in range(5):
                    dve.wait_ge(*rot_ps.nth(l, n + 1))
                    dst = m_q[64:96, n, 0:LAT] if n < H else kpe[64:96, 0:LAT]
                    rope(dst, dst, psD[64:96, n % 2, 0:LAT], cos, sin, rot_s[64:96, n % H]).then_inc(rot_in.sem, 1)
                dve.wait_ge(*rot_in.nth(l, 5))
                v.tensor_copy(m_k[64:96], kpe[64:96].unsqueeze(1).to_broadcast([32, H, KEYS]))\
                    .then_inc(mla_k_rope.sem, 1)
                attend(l, 0, 1, 96 ** -0.5, att_small, (prob,), o_tok)

            def diff(l):
                dve.wait_ge(*br_done.nth(l, 1))
                dve.wait_ge(*dense_out.nth(l, N_WIN))
                pr = p_("lam").rearrange("p (i n) -> p i n", i=4)
                for i in range(2):
                    last = v.tensor_tensor(lam_s[:, 32 * i:32 * i + 32], pr[:, 2 * i], pr[:, 2 * i + 1], ALU.mult)
                link(last)
                v.tensor_reduce(lam_s[:, 64:66], lam_s[:, 0:64].rearrange("p (i n) -> p i n", i=2), AX.X, ALU.add)\
                    .then_inc(lam_sum.sem, 1)
                cos, sin = c_("cos"), c_("sin")
                for n in range(4):
                    dve.wait_ge(*d_rot_ps.nth(l, n + 1))
                    dst = (d_q if n < 2 else d_k)[:, n % 2, 0:LAT]
                    rope(dst, dst, psD[:, n % 2, 0:LAT], cos, sin, d_rot[:, n]).then_inc(d_rot_in.sem, 1)
                dve.wait_ge(*lam_exp.nth(l, 1))
                link(v.tensor_tensor(lam_s[:, 70:71], lam_s[:, 69:70], lam_s[:, 68:69], ALU.subtract))
                link(v.tensor_tensor(lam_s[:, 71:72], lam_s[:, 70:71], p_("lamc")[:, 0:1], ALU.subtract))
                attend(l, U, 2, 32 ** -0.5, d_small, (d_prob, d_prob2), do_tok)
                dve.wait_ge(*pv_in.nth(l, 2 * U))
                link(v.tensor_tensor(do_sq, do_tok, do_tok, ALU.mult))
                v.tensor_reduce(d_small[:, 4], do_sq.rearrange("p t h v -> p (t h) v"), AX.X, ALU.add)\
                    .then_inc(do_sum.sem, 1)
                dve.wait_ge(*do_rs.nth(l, 1))
                link(v.tensor_scalar(d_small[:, 4], d_small[:, 4], p_("lamc")[:, 1:2], None, ALU.mult))
                o = do_tok.rearrange("p t h v -> p (t h) v")
                link(v.tensor_tensor(o, o, d_small[:, 4].unsqueeze(2).to_broadcast([P, U, 64]), ALU.mult))
                v.tensor_tensor(o, o, p_("danw").unsqueeze(1).to_broadcast([P, U, 64]), ALU.mult)\
                    .then_inc(do_normed.sem, 1)

            def add_residual(dst, b, gate):
                for half, s, p, q in ((0, 0, 0, HALF), (1, 0, HALF, LAT), (1, 1, LAT, T)):
                    ps = psum_halves(b)[:, half, p - half * HALF:q - half * HALF]
                    last = v.scalar_tensor_tensor(out=dst[:, p:q], in0=ps, scalar=gate[:, s:s + 1], in1=dst[:, p:q],
                                                  op0=ALU.mult, op1=ALU.add)
                return last

            def weigh(slot, n, first):
                for i in range(2 * KC):
                    k, c = divmod(i, 2)
                    dst, w_, s_ = weighed[:, n % 2, c, :], ring[:, slot, k, :], cond[:, k, c:c + 1]
                    if k:
                        dve.wait_ge(weighed_in.sem, first + (i - 1))
                        last = v.scalar_tensor_tensor(out=dst, in0=w_, scalar=s_, in1=dst, op0=ALU.mult, op1=ALU.add)
                    else:
                        last = v.tensor_scalar(dst, w_, s_, None, ALU.mult)
                    last.then_inc(weighed_in.sem, 1)

            def weigh_block(l, place, n, back, turns=0, more=0):
                dve.wait_ge(ring_in[place % RING].sem,
                            (l * PER_SLOT + turns + ((N_EARLY + place) // RING + 1)) * 16)
                dve.wait_ge(block_done.sem, l * N_BLOCKS + turns * RING + (RING + N_EARLY + place - back + 1))
                weigh(place % RING, n, l * (N_ADA * 2 * KC) + more * (2 * KC) + (N_EARLY + n) * 2 * KC)

            def merge(l):
                dve.wait_ge(*br_done.nth(l, 2))
                for b in range(2):
                    v.memset(lam_s[:, b:b + 1], 0.0).then_inc(proj_used.sem, 1)
                with dve.Fori(0, KC) as d:
                    for n in range(4):
                        weigh_block(l, B_GATE + 2 * n + 1, n, 4, d * 2, d * 4)
                        dve.wait_ge(gate_act.sem, l * N_GATE + d * 4 + (n + 1))
                        if n > 1:
                            dve.wait_ge(merged_add.sem, l * 24 + d * 3 + (n - 1))
                        ps = psA[:, 2 * (n % 2):2 * (n % 2) + 2, :].rearrange("p b n -> p (b n)")[:, 0:T]
                        v.scalar_tensor_tensor(out=md if n == 0 else mt, in0=tg[:, n % 2], scalar=1.0, in1=ps,
                                               op0=ALU.add, op1=ALU.mult).then_inc(proj_used.sem, 1)
                        if n:
                            dve.wait_ge(proj_used.sem, l * (N_GATE + 2) + d * 4 + (2 + n + 1))
                            v.tensor_tensor(md, md, mt, ALU.add).then_inc(merged_add.sem, 1)
                    dve.wait_ge(merged_add.sem, l * 24 + d * 3 + 3)
                    zh, zl = (z[:, bass.ds(d, 1), :].rearrange("p o t -> p (o t)") for z in (z_high, z_low))
                    v.tensor_copy(zh, md).then_inc(merged_high.sem, 1)
                    dve.wait_ge(merged_high.sem, l * KC + d + 1)
                    v.tensor_tensor(zl, md, zh.bitcast(F32), ALU.subtract).then_inc(merged_ready.sem, 1)
                    dve.wait_ge(merged_ready.sem, l * KC + d + 1)

                dve.wait_ge(*block_done.nth(l, B_OUT))
                for b in range(2):
                    late = mod[:, 16:48].rearrange("p (j b) s -> p j b s", b=2)[:, :, b]
                    last = v.tensor_tensor(late, psD[:, 1 - b, HALF:HALF + N_LATE].rearrange("p (j s) -> p j s", s=2),
                                           p_("bada")[:, 16:48].rearrange("p (j b) -> p j b", b=2)[:, :, b].unsqueeze(2)
                                           .to_broadcast([P, 16, 2]), ALU.add)
                link(last)
                v.tensor_scalar(gt_half[:], mod[:, 16:24], 0.5, None, ALU.mult)
                norm_scale(1, "nmlp").then_inc(mod_ready.sem, 1)
                dve.wait_ge(*mod_ready.nth(l, 2))

            def out_proj(l):
                for m in range(KC):
                    dve.wait_ge(*block_done.nth(l, B_OUT + m + 1))
                    add_residual(x[:, m], m % 2, gt_half[:, m]).then_inc(residual.sem, 1)

            def mlp(l):
                turns = N_GROUP // RING
                with dve.Fori(0, GROUPS) as g:
                    for j in range(KC):
                        if j % 4 == 1:
                            weigh_block(l, early_at(j // 4), N_LATE + j // 4, 10, g * turns, g * 4)
                        dve.wait_ge(hid_square.sem, l * 32 + g * 8 + (j + 1))
                        v.tensor_copy(z_high[:, j], hid_sq[:, j % 2]).then_inc(hid_high.sem, 1)
                        dve.wait_ge(hid_high.sem, l * 32 + g * 8 + (j + 1))
                        v.tensor_tensor(z_low[:, j], hid_sq[:, j % 2], z_high[:, j].bitcast(F32), ALU.subtract)\
                            .then_inc(hid_ready.sem, 1)
                    for m in range(KC):
                        if m % 4 == 1:
                            weigh_block(l, early_at(2 + m // 4), N_LATE + 2 + m // 4, 10, g * turns, g * 4)
                        dve.wait_ge(block_done.sem, l * N_BLOCKS + g * N_GROUP + (RING + N_EARLY + mlp_at(KC + m) + 1))
                        dve.wait_ge(residual.sem, l * 40 + g * 8 + (1 + m + 1))
                        add_residual(x[:, m], m % 2, mod[:, 40 + m]).then_inc(residual.sem, 1)

            dve.wait_ge(const_in.sem, 16)
            dve.wait_ge(x_in.sem, 16)
            v.memset(stage[:], 0.0)
            dve.wait_ge(cond_tanh.sem, 1)
            v.scalar_tensor_tensor(out=cond_t[:], in0=cond_t[:], scalar=1.0, in1=cond[:], op0=ALU.add, op1=ALU.mult)\
                .then_inc(cond_sum.sem, 1)
            dve.wait_ge(cond_sum.sem, 1)
            v.tensor_scalar(cond[:], cond_t[:], 0.5, None, ALU.mult).then_inc(residual.sem, 1)
            dve.wait_ge(residual.sem, 1)
            with dve.Fori(0, N_EARLY // RING) as i:
                for j in range(RING):
                    dve.wait_ge(ring_in[j].sem, (i + 1) * 16)
                    dve.wait_ge(block_done.sem, i * RING + (RING + j - 1))
                    weigh(j, j, i * (RING * 2 * KC) + j * 2 * KC)
            with dve.Fori(0, DEPTH) as l:
                chain.l, chain.n = l, 0
                dve.wait_ge(*residual.nth(l, 0))
                dve.wait_ge(*params_in.nth(l, 1))
                dve.wait_ge(*block_done.nth(l, 0))
                link(v.tensor_tensor(mod[:, 0:16], psA[:, 0, 0:32].rearrange("p (m s) -> p m s", s=2),
                                     p_("bada")[:, 0:16].unsqueeze(2).to_broadcast([P, 16, 2]), ALU.add))
                norm_scale(0, "nmix").then_inc(mod_ready.sem, 1)
                norm(l, 0)
                hyena(l)
                gdn(l)
                mla(l)
                diff(l)
                merge(l)
                out_proj(l)
                norm(l, 1)
                split_h(l)
                mlp(l)
                n_links = chain.n
            assert n_links == links[0], ("DVE_LINKS", n_links)
            norm(DEPTH, 0)


SPEC = {"const": (P, CON_W), "x": (P, KC, T), "cond": (P, KC, 2), "w_early": (DEPTH, N_EARLY, P, KC * P), "w_late": (DEPTH, N_LATE, P, KC * P),
        "w_in": (DEPTH, N_WIN, P, KC * P), "w_gate": (DEPTH, N_GATE, P, 10 * P), "w_out": (DEPTH, N_OUT, P, KC * P),
        "w_mlp": (DEPTH, GROUPS * 2 * KC, P, KC * P), "par": (DEPTH, P, PAR_W), "dft": (P, DFT_W)}
OUTS = {"y": (P, KC, T), "state": (DEPTH, P, 256), "ckv": (DEPTH, P, CTX), "kpe": (DEPTH, 32, CTX),
        "dk": (DEPTH, P, 2, CTX), "dv": (DEPTH, P, 256)}


def constants():
    con = np.zeros((P, CON_W), np.float32)

    def put(dst, table, name, value, rows=slice(0, P)):
        a, w = table[name]
        value = np.asarray(value, np.float64)
        dst[rows, a:a + w] = value.reshape(value.shape[0], w) if value.ndim > 1 else value

    i, j = np.meshgrid(np.arange(P), np.arange(P), indexing="ij")
    put(con, CON, "ident", i == j)
    put(con, CON, "ones", np.ones((P, P)))
    put(con, CON, "blk", i // 64 == j // 64)
    put(con, CON, "tri", np.stack([i <= j, i >= j], 1))
    put(con, CON, "maskt", np.stack([np.where(j >= i, 0.0, -1e30), np.where(j <= i, 0.0, -1e30)], 1))
    put(con, CON, "maskn", np.stack([np.where(j < i, 0.0, 1e30), np.where(j > i, 0.0, 1e30)], 1))
    lv = []
    for k in range(7):
        m = (i >> (k + 1) == j >> (k + 1)) & ((i >> k) & 1 == 1) & ((j >> k) & 1 == 0)
        lv.append(np.stack([m, m.T], 1))
    put(con, CON, "lvl", np.stack(lv, 1))
    put(con, CON, "rot", i == np.where(j % 16 < 8, j + 8, j - 8))
    pos = np.arange(LAT)
    inv = 10000.0 ** (-(np.arange(P) % 8) / 8.0)
    ang = np.where((np.arange(P) % 32 < 16)[:, None], pos // GRID_W, pos % GRID_W) * inv[:, None]
    put(con, CON, "cos", np.cos(ang))
    put(con, CON, "sin", np.sin(ang) * np.where(np.arange(P) % 16 < 8, -1.0, 1.0)[:, None])
    wf = np.zeros((P, 5))
    wf[:, 0:4], wf[:, 4] = 1.0 / LAT, 1.0 / CTX
    wf[0, 0], wf[0, 4] = 0.5 / LAT, 0.5 / CTX
    put(con, CON, "wf", wf)
    put(con, CON, "alt", (1.0 - 2.0 * (np.arange(P) % 2))[:, None])
    put(con, CON, "altrow", (1.0 - 2.0 * (np.arange(LAT) % 2))[None], slice(0, 1))
    put(con, CON, "eps", np.full((P, 1), EPS))
    put(con, CON, "eps4", np.full((P, 1), 4 * EPS))

    dft = np.zeros((P, DFT_W), np.float32)
    n = np.arange(LAT)
    a = 2 * np.pi * ((n[:, None] * n[None]) % (2 * LAT)) / (2 * LAT)
    put(dft, DFT, "cs", np.stack([np.cos(a), np.sin(a)], 1).reshape(4, P, 2, LAT).transpose(1, 0, 2, 3))
    n = np.arange(CTX)
    a = 2 * np.pi * ((n[:, None] * n[None]) % (2 * CTX)) / (2 * CTX)
    put(dft, DFT, "csp", np.stack([np.cos(a), np.sin(a)], 1))
    deltas = np.abs(np.linspace(math.log(1e-2) / 1.5, math.log(1e-2) / 0.3, 256))
    wins, zs = [], []
    for seq in (LAT, CTX):
        pos = np.arange(seq)
        t = pos / max(seq - 1, 1)
        w = np.exp(-t[:, None] * deltas)
        wb = w.copy()
        wb[0] = 0.0
        wins.append(np.concatenate([w, wb], 1).reshape(seq // P, P, 512))
        ang = (2.0 * np.pi * pos / seq)[:, None] * np.linspace(1e-4, BANDS - 1, BANDS)
        zs.append(np.concatenate([t[:, None], np.cos(ang), -np.sin(ang)], 1))
    put(dft, DFT, "win", np.concatenate(wins, 0).transpose(1, 0, 2))
    put(dft, DFT, "z", np.concatenate(zs, 0).T, slice(0, 1 + 2 * BANDS))
    return con, dft


def blocks(w):
    d, k, m = w.shape
    return w.reshape(d, k // P, P, m // P, P).transpose(0, 3, 2, 1, 4)


def lay_out(inp):
    f = {k: np.asarray(v) for k, v in inp.items()}
    con, dft = constants()
    a, w = CON["fin"]
    con[:, a:a + w] = f["final_norm_w"].reshape(KC, P).T
    tok = np.concatenate([f["x_sample"][0], f["x_prompt"][0]], 0)
    xs = tok.T.reshape(KC, P, T).transpose(1, 0, 2)
    cond = np.stack([f["c"][0], f["c_ctx"]], 1).reshape(KC, P, 2).transpose(1, 0, 2)
    wi = f["w_in"]
    cols = lambda a, b: wi[:, :, a:b]
    kpe_cols = np.zeros((DEPTH, D, P), np.float32)
    kpe_cols[:, :, 64:96] = cols(384, 416)
    win_cols = np.concatenate([cols(1456, 2224), cols(416, 1440), cols(0, 384), kpe_cols, cols(2224, 2992)], 2)
    gates = wi[:, :, 2992:].reshape(DEPTH, D, 4, KC, P).transpose(0, 1, 3, 2, 4).reshape(DEPTH, D, N_GATE * P)
    wg = blocks(gates)
    wb = f["w_branch"].reshape(DEPTH, 4, 2, P, KC, P).transpose(0, 4, 1, 3, 2, 5).reshape(DEPTH, N_GATE, P, 2, P)
    w_gate = np.concatenate([wg, wb], 3)
    w1 = blocks(f["mlp_w1"]).reshape(DEPTH, 4, KC, P, KC, P)
    w2 = f["mlp_w2"].reshape(DEPTH, 4, KC, P, KC, P).transpose(0, 1, 4, 3, 2, 5)
    w_mlp = np.concatenate([w1, w2], 2)
    par = np.zeros((DEPTH, P, PAR_W), np.float32)

    def put(name, value, rows=slice(0, P)):
        a, w = PAR[name]
        value = np.asarray(value)
        par[:, rows, a:a + w] = value.reshape(DEPTH, value.shape[1], w)

    def feat(v, n):
        return v.reshape(DEPTH, n, P).transpose(0, 2, 1)

    def everywhere(v):
        return np.broadcast_to(v[:, None], (DEPTH, P, v.shape[-1]))

    ab = wi[:, :, 1440:1456].reshape(DEPTH, KC, P, 2, 2, 4).transpose(0, 2, 1, 4, 3, 5)
    put("wab", ab.reshape(DEPTH, P, KC * 16))
    put("uq", f["mla_w_uq"].reshape(DEPTH, 2, P, 384).transpose(0, 2, 1, 3))
    put("ukv", f["mla_w_ukv"])
    put("w1", f["hy_f_w1"], slice(0, 33))
    put("w2", f["hy_f_w2"], slice(0, 64))
    put("w3", f["hy_f_w3"], slice(0, 64))
    put("ckv_c", f["cache_mla_ckv"][0].transpose(0, 2, 1))
    put("kpe_c", f["cache_mla_kpe"][0].transpose(0, 2, 1), slice(64, 96))
    put("dk_c", f["cache_diff_k"][0].reshape(DEPTH, P, 256).transpose(0, 2, 1).reshape(DEPTH, 2, P, P)
        .transpose(0, 2, 1, 3))
    put("dv_c", f["cache_diff_v"][0].reshape(DEPTH, P, 256))
    put("s0", f["state_gdn"][0].reshape(DEPTH, 2, 2, 2, 64, 64).transpose(0, 3, 4, 1, 2, 5).reshape(DEPTH, P, 256))
    put("lam", everywhere(np.concatenate([f["da_lq1"], f["da_lk1"], f["da_lq2"], f["da_lk2"]], 1)))
    put("danw", everywhere(f["da_norm_w"]))
    put("alog", everywhere(f["gdn_a_log"].reshape(DEPTH, 8)))
    put("dtb", everywhere(f["gdn_dt_bias"].reshape(DEPTH, 8)))
    put("bada", feat(f["b_ada"], 48))
    put("nmix", feat(f["norm_mix_w"], 8))
    put("nmlp", feat(f["norm_mlp_w"], 8))
    put("qn", feat(f["mla_q_norm_w"], 2))
    put("kvn", feat(f["mla_kv_norm_w"], 1))
    put("gcw", f["gdn_conv_w"].reshape(DEPTH, 3, 6, P).transpose(0, 3, 2, 1))
    put("gnw", np.concatenate([f["gdn_norm_w"]] * 2, 1)[:, :, None])
    put("hcw", f["hy_conv_w"].reshape(DEPTH, 3, 6, P).transpose(0, 3, 2, 1))
    put("hcb", feat(f["hy_conv_b"], 6))
    put("hb1", f["hy_f_b1"][:, :, None], slice(0, 64))
    put("hb2", f["hy_f_b2"][:, :, None], slice(0, 64))
    put("hfr", f["hy_f_freq"][:, :, None], slice(0, 64))
    put("hyd", feat(f["hy_d"], 2))
    init = [0.8 - 0.6 * math.exp(-0.3 * l) for l in range(DEPTH)]
    put("lamc", np.broadcast_to(np.array([[[v, 1.0 - v]] for v in init], np.float32), (DEPTH, P, 2)))
    w_ada = blocks(f["w_ada"])
    early = np.roll(w_ada[:, :N_EARLY], -1, axis=0)
    arrays = {"const": con, "x": xs, "cond": cond, "w_early": early, "w_late": w_ada[:, N_EARLY:], "w_in": blocks(win_cols),
              "w_gate": w_gate, "w_out": blocks(f["w_out"]), "w_mlp": w_mlp, "par": par, "dft": dft}
    return {k: np.ascontiguousarray(v).reshape(SPEC[k]) for k, v in arrays.items()}


def build(nc):
    ins = {k: nc.dram_tensor(f"in_{k}", s, F32, kind="ExternalInput").ap() for k, s in SPEC.items()}
    outs = {k: nc.dram_tensor(f"out_{k}", s, F32, kind="ExternalOutput").ap() for k, s in OUTS.items()}
    trunk(nc, ins, outs, (DVE_LINKS, ACT_LINKS))


def kernel(**inputs):
    import concourse.bacc as bacc
    from concourse.bass_utils import run_bass_kernel_spmd

    nc = bacc.Bacc("TRN2", target_bir_lowering=False, num_devices=1)
    arrays = lay_out(inputs)
    build(nc)
    r = run_bass_kernel_spmd(nc, [{f"in_{k}": v for k, v in arrays.items()}], core_ids=[0]).results[0]
    y = r["out_y"].transpose(1, 0, 2).reshape(D, T).T
    dk = r["out_dk"].transpose(0, 2, 1, 3).reshape(DEPTH, 256, CTX).transpose(0, 2, 1)
    st = r["out_state"].reshape(DEPTH, 2, 64, 2, 2, 64).transpose(0, 3, 4, 1, 2, 5)
    c = np.ascontiguousarray
    return (c(y[LAT:])[None], c(y[:LAT])[None], c(r["out_ckv"].transpose(0, 2, 1))[None],
            c(r["out_kpe"].transpose(0, 2, 1))[None], c(dk.reshape(1, DEPTH, CTX, H, 2, 32)),
            c(r["out_dv"].reshape(1, DEPTH, CTX, H, 64)), c(st.reshape(1, DEPTH, 2, H, 64, 64)))
```
